# Optimizing a Trainium2 kernel written in Bass

```python
import math
import jax, jax.numpy as jnp
from jax import lax
import numpy as np

D_MODEL = 1024
BATCH = 1
SEQ = 256
DEPTH = 2

ATTN_WIDTH = D_MODEL // 2
HEAD_DIM = 64
N_ATTN_HEADS = ATTN_WIDTH // HEAD_DIM
DILATED_PATTERNS = ((128, 1), (512, 4), (2048, 16))
REL_BUCKETS = 32
REL_MAX_DISTANCE = 1024
SSM_WIDTH = D_MODEL - ATTN_WIDTH
SSM_GROUP = 16
SSM_GROUPS = SSM_WIDTH // SSM_GROUP
SSM_STATE = 64
STEP_MIN = 1e-3
STEP_MAX = 1e-1
PEER_HEADS = 8
PEER_KEYS = 128
PEER_EXPERTS = PEER_KEYS * PEER_KEYS
PEER_QUERY_DIM = 128
PEER_TOPK = 16
PEER_CHUNK = 128
EPS = 1e-6
NEG_INF = -1e30

kernel_name = "hybrid_dilated_attn_s5_peer_encoder"

def _rmsnorm(x, g):
    x32 = x.astype(jnp.float32)
    y = x32 * lax.rsqrt(jnp.mean(x32 * x32, axis=-1, keepdims=True) + EPS) * g.astype(jnp.float32)
    return y.astype(x.dtype)

def _t5_buckets(rel):
    half = REL_BUCKETS // 2
    max_exact = half // 2
    n = np.abs(rel)
    large = max_exact + (np.log(np.maximum(n, 1) / max_exact)
                         / np.log(REL_MAX_DISTANCE / max_exact) * (half - max_exact)).astype(np.int32)
    large = np.minimum(large, half - 1)
    return (np.where(rel > 0, half, 0) + np.where(n < max_exact, n, large)).astype(np.int32)

def _band_structure(length, dilation, half):
    blk = half
    nb = -(-length // blk)
    ql = np.arange(blk)[:, None]
    t = np.arange(3 * blk)[None, :]
    delta = t - blk - ql
    key_pos = (np.arange(nb)[:, None, None] - 1) * blk + t[None]
    valid = (np.abs(delta)[None] <= half) & (key_pos >= 0) & (key_pos < length)
    buckets = _t5_buckets(delta * dilation)
    return nb, valid, buckets

def _dilated_band_attention(q, k, v, rel_bias, window, dilation):
    bsz, seq, heads, hd = q.shape
    half = window // (2 * dilation)
    blk = half
    length = seq // dilation
    nb, valid, buckets = _band_structure(length, dilation, half)
    pad = nb * blk - length

    def to_sub(t):
        return t.reshape(bsz, length, dilation, heads, hd).transpose(0, 2, 3, 1, 4)

    qs = jnp.pad(to_sub(q), ((0, 0), (0, 0), (0, 0), (0, pad), (0, 0)))
    qs = qs.reshape(bsz, dilation, heads, nb, blk, hd)

    def windows(t):
        tp = jnp.pad(to_sub(t), ((0, 0), (0, 0), (0, 0), (blk, pad + blk), (0, 0)))
        tp = tp.reshape(bsz, dilation, heads, nb + 2, blk, hd)
        return jnp.concatenate([tp[:, :, :, :-2], tp[:, :, :, 1:-1], tp[:, :, :, 2:]], axis=4)

    kw, vw = windows(k), windows(v)
    bias = jnp.transpose(rel_bias[buckets], (2, 0, 1)).astype(jnp.float32)
    logits = jnp.einsum('brhnqd,brhnkd->brhnqk', qs, kw,
                        preferred_element_type=jnp.float32) * (hd ** -0.5)
    logits = jnp.where(valid[None, None, None], logits + bias[None, None, :, None], NEG_INF)
    m = jnp.max(logits, axis=-1, keepdims=True)
    p = jnp.exp(logits - m)
    s = jnp.sum(p, axis=-1, keepdims=True)
    o = jnp.einsum('brhnqk,brhnkd->brhnqd', p, vw.astype(jnp.float32)) / s
    lse = (m + jnp.log(s))[..., 0]

    o = o.reshape(bsz, dilation, heads, nb * blk, hd)[:, :, :, :length]
    o = o.transpose(0, 3, 1, 2, 4).reshape(bsz, seq, heads, hd)
    lse = lse.reshape(bsz, dilation, heads, nb * blk)[:, :, :, :length]
    lse = lse.transpose(0, 3, 1, 2).reshape(bsz, seq, heads)
    return o, lse

def _dilated_attention_mixture(q, k, v, rel_bias):
    outs, lses = zip(*[_dilated_band_attention(q, k, v, rel_bias, w, d) for w, d in DILATED_PATTERNS])
    weights = jax.nn.softmax(jnp.stack(lses), axis=0)
    return jnp.sum(weights[..., None] * jnp.stack(outs), axis=0)

def _ssm_combine(e_i, e_j):
    a_i, b_i = e_i
    a_j, b_j = e_j
    return a_j * a_i, a_j * b_i + b_j

def _s5_bidirectional(u, lam_re, lam_im, log_step, b_re, b_im, c_re, c_im, d_skip):
    bsz, seq, _ = u.shape
    f32 = jnp.float32
    u_g = u.astype(f32).reshape(bsz, seq, SSM_GROUPS, SSM_GROUP)
    lam = lax.complex(lam_re.astype(f32), lam_im.astype(f32))
    step = jnp.exp(log_step.astype(f32))[..., None]
    lam_bar = jnp.exp(lam * step)
    b = lax.complex(b_re.astype(f32), b_im.astype(f32))
    b_bar = ((lam_bar - 1.0) / lam)[..., None] * b
    c = lax.complex(c_re.astype(f32), c_im.astype(f32))
    u_c = u_g.astype(jnp.complex64)
    y = d_skip.astype(f32).reshape(SSM_GROUPS, SSM_GROUP) * u_g
    for direction, rev in ((0, False), (1, True)):
        bu = jnp.einsum('bsgc,gpc->bsgp', u_c, b_bar[direction])
        a = jnp.broadcast_to(lam_bar[direction], (1, seq, SSM_GROUPS, SSM_STATE))
        _, states = lax.associative_scan(_ssm_combine, (a, bu), axis=1, reverse=rev)
        y = y + jnp.einsum('bsgp,gcp->bsgc', states, c[direction]).real
    return y.reshape(bsz, seq, SSM_WIDTH)

def _peer(h, w_query, sub_keys, expert_u, expert_v):
    bsz, seq, dm = h.shape
    f32 = jnp.float32
    q = (h @ w_query).reshape(bsz, seq, PEER_HEADS, PEER_QUERY_DIM)
    half = PEER_QUERY_DIM // 2
    s1 = jnp.einsum('bshk,hnk->bshn', q[..., :half], sub_keys[0], preferred_element_type=f32)
    s2 = jnp.einsum('bshk,hnk->bshn', q[..., half:], sub_keys[1], preferred_element_type=f32)
    t1, i1 = lax.top_k(s1, PEER_TOPK)
    t2, i2 = lax.top_k(s2, PEER_TOPK)
    cand = (t1[..., :, None] + t2[..., None, :]).reshape(bsz, seq, PEER_HEADS, PEER_TOPK * PEER_TOPK)
    top_s, top_c = lax.top_k(cand, PEER_TOPK)
    e1 = jnp.take_along_axis(i1, top_c // PEER_TOPK, axis=-1)
    e2 = jnp.take_along_axis(i2, top_c % PEER_TOPK, axis=-1)
    experts = e1 * PEER_KEYS + e2
    gates = jax.nn.softmax(top_s, axis=-1)
    n_chunk = (bsz * seq) // PEER_CHUNK
    sel = PEER_HEADS * PEER_TOPK
    hc = h.reshape(n_chunk, PEER_CHUNK, dm)
    ec = experts.reshape(n_chunk, PEER_CHUNK, sel)
    gc = gates.reshape(n_chunk, PEER_CHUNK, sel)

    def chunk(args):
        h_c, e_c, g_c = args
        act = jax.nn.gelu(jnp.einsum('td,ted->te', h_c, expert_u[e_c], preferred_element_type=f32),
                          approximate=False)
        out = jnp.einsum('te,ted->td', g_c * act, expert_v[e_c].astype(f32))
        return out.astype(h.dtype)

    return lax.map(chunk, (hc, ec, gc)).reshape(bsz, seq, dm)

def setup_inputs(seed: int = 0) -> dict:
    key = jax.random.key(seed)
    ks = jax.random.split(key, 24)
    f32 = jnp.float32

    def nrm(k, shape, scale):
        return jax.random.normal(k, shape, f32) * scale

    mix_in = 3 * ATTN_WIDTH + SSM_WIDTH
    ssm_shape = (DEPTH, 2, SSM_GROUPS, SSM_STATE)
    return {
        "x": nrm(ks[0], (BATCH, SEQ, D_MODEL), 1.0),
        "w_in": nrm(ks[1], (DEPTH, D_MODEL, mix_in), D_MODEL ** -0.5),
        "w_out": nrm(ks[2], (DEPTH, D_MODEL, D_MODEL), D_MODEL ** -0.5),
        "rel_bias": nrm(ks[3], (REL_BUCKETS, N_ATTN_HEADS), 0.5),
        "g_attn": 1.0 + nrm(ks[4], (DEPTH, ATTN_WIDTH), 0.05),
        "g_ssm": 1.0 + nrm(ks[5], (DEPTH, SSM_WIDTH), 0.05),
        "norm_mix": 1.0 + nrm(ks[6], (DEPTH, D_MODEL), 0.05),
        "norm_ffn": 1.0 + nrm(ks[7], (DEPTH, D_MODEL), 0.05),
        "lam_re": -0.5 + nrm(ks[8], ssm_shape, 0.01),
        "lam_im": math.pi * jnp.arange(SSM_STATE, dtype=f32) + nrm(ks[9], ssm_shape, 0.01),
        "log_step": jax.random.uniform(ks[10], (DEPTH, 2, SSM_GROUPS), f32,
                                       minval=math.log(STEP_MIN), maxval=math.log(STEP_MAX)),
        "b_re": nrm(ks[11], (DEPTH, 2, SSM_GROUPS, SSM_STATE, SSM_GROUP), (2 * SSM_GROUP) ** -0.5),
        "b_im": nrm(ks[12], (DEPTH, 2, SSM_GROUPS, SSM_STATE, SSM_GROUP), (2 * SSM_GROUP) ** -0.5),
        "c_re": nrm(ks[13], (DEPTH, 2, SSM_GROUPS, SSM_GROUP, SSM_STATE), (2 * SSM_STATE) ** -0.5),
        "c_im": nrm(ks[14], (DEPTH, 2, SSM_GROUPS, SSM_GROUP, SSM_STATE), (2 * SSM_STATE) ** -0.5),
        "d_skip": nrm(ks[15], (DEPTH, SSM_WIDTH), 1.0),
        "w_glu": nrm(ks[16], (DEPTH, SSM_WIDTH, 2 * SSM_WIDTH), SSM_WIDTH ** -0.5),
        "w_query": nrm(ks[17], (DEPTH, D_MODEL, PEER_HEADS * PEER_QUERY_DIM), D_MODEL ** -0.5),
        "sub_keys": nrm(ks[18], (DEPTH, 2, PEER_HEADS, PEER_KEYS, PEER_QUERY_DIM // 2),
                         (PEER_QUERY_DIM // 2) ** -0.5),
        "expert_u": nrm(ks[19], (DEPTH, PEER_EXPERTS, D_MODEL), D_MODEL ** -0.5),
        "expert_v": nrm(ks[20], (DEPTH, PEER_EXPERTS, D_MODEL), PEER_HEADS ** -0.5),
        "norm_final": 1.0 + nrm(ks[21], (D_MODEL,), 0.05),
    }

def reference(x, w_in, w_out, rel_bias, g_attn, g_ssm, norm_mix, norm_ffn, lam_re, lam_im,
              log_step, b_re, b_im, c_re, c_im, d_skip, w_glu, w_query, sub_keys,
              expert_u, expert_v, norm_final):
    bsz, seq, _ = x.shape
    for l in range(DEPTH):
        h = _rmsnorm(x, norm_mix[l])
        proj = h @ w_in[l]
        q = proj[..., :ATTN_WIDTH].reshape(bsz, seq, N_ATTN_HEADS, HEAD_DIM)
        k = proj[..., ATTN_WIDTH:2 * ATTN_WIDTH].reshape(bsz, seq, N_ATTN_HEADS, HEAD_DIM)
        v = proj[..., 2 * ATTN_WIDTH:3 * ATTN_WIDTH].reshape(bsz, seq, N_ATTN_HEADS, HEAD_DIM)
        u = proj[..., 3 * ATTN_WIDTH:]

        attn = _dilated_attention_mixture(q, k, v, rel_bias)
        attn = attn.reshape(bsz, seq, ATTN_WIDTH).astype(x.dtype)

        y = jax.nn.gelu(_s5_bidirectional(u, lam_re[l], lam_im[l], log_step[l], b_re[l], b_im[l],
                                          c_re[l], c_im[l], d_skip[l]).astype(x.dtype),
                        approximate=False)
        ab = y @ w_glu[l]
        ssm = ab[..., :SSM_WIDTH] * jax.nn.sigmoid(ab[..., SSM_WIDTH:])

        mix = jnp.concatenate([_rmsnorm(attn, g_attn[l]), _rmsnorm(ssm, g_ssm[l])], axis=-1)
        x = x + mix @ w_out[l]

        x = x + _peer(_rmsnorm(x, norm_ffn[l]), w_query[l], sub_keys[l], expert_u[l], expert_v[l])
    return _rmsnorm(x, norm_final)


_drawn_inputs = setup_inputs


def setup_inputs(seed=0):
    import zlib

    import numpy as np

    out = dict(_drawn_inputs(seed))
    spreads = {}
    factors = {}
    for name, (base, spread) in spreads.items():
        noise = np.random.default_rng([zlib.crc32(name.encode()), seed]).standard_normal(out[name].shape)
        drawn = base * np.exp(spread * noise) if base else spread * noise
        out[name] = __import__('jax').numpy.asarray(drawn.astype(out[name].dtype))
    for name, factor in factors.items():
        out[name] = (out[name] * factor).astype(out[name].dtype)
    return out
```

```python
import concourse.bass as bass
from concourse import mybir
from contextlib import ExitStack

F32 = mybir.dt.float32
F32R = mybir.dt.float32r
U32 = mybir.dt.uint32
ALU = mybir.AluOpType
ACT = mybir.ActivationFunctionType
AX = mybir.AxisListType

P = 128
D = 1024
S = 256
DEPTH = 2
AW = 512
HD = 64
NH = 8
NQ = 4
DC = D // P
TT = S // P
NT = 8
PH = 8
PK = 128
TOPK = 16
EPS = 1e-6
ROUND = 12582912.0
GRID14 = 768.0
TWO_PI_A = 6.28125
TWO_PI_B = 0.0019353071795864769
INV_TWO_PI = 0.15915494309189535
TWO_PI_BELOW = 6.28318501
HALF_PI = 1.5707963267948966
LOWEST = -3.0e38
NCONST = 3 * P + 32
TOEP = 2 * S


def encoder(nc, x, w_in, w_out, w_glu, w_query, keys, expert_u, expert_v, rel_bias, gains,
            norm_final, ssm_par, ssm_b, ssm_c, consts, bucket_rows, out):
    ctx = ExitStack()
    with ctx:
        def sb(name, shape, dt=F32):
            return ctx.enter_context(nc.sbuf_tensor(name, shape, dt))

        def sem(name):
            return ctx.enter_context(nc.semaphore(name))

        cst = sb("cst", [P, NCONST])
        ident, antiident, iota = cst[:, 0:P], cst[:, P:2 * P], cst[:, 2 * P:3 * P]
        steps_ab = cst[:, 3 * P:3 * P + 32]
        iota16 = cst[:, 2 * P:2 * P + TOPK]
        gain = sb("gain", [P, 28])
        g_mix, g_ffn, g_cat, d_skip = gain[:, 0:8], gain[:, 8:16], gain[:, 16:24], gain[:, 24:28]
        tiny = sb("tiny", [P, 4])
        eps_c, half_pi_c = tiny[:, 0:1], tiny[:, 1:2]
        fence = sb("fence", [P, 2])
        sel_T = sb("sel_T", [P, 3, S])
        hot = sb("hot", [P, 4, 2, P])
        h_hl = sb("h_hl", [P, 2, DC, S], F32R)
        u_hl = [sb(f"u_hl{i}", [P, 2, DC, P], F32R) for i in range(2)]
        v_hl = [sb(f"v_hl{i}", [P, 2, D], F32R) for i in range(2)]
        w_hl = [sb(f"w_hl{i}", [P, 2, S], F32R) for i in range(2)]
        u_raw = [sb(f"u_raw{i}", [P, DC, P]) for i in range(2)]
        v_raw = [sb(f"v_raw{i}", [P, D]) for i in range(2)]
        act_w = sb("act_w", [P, 2, S])

        arena = sb("arena", [P, PK * S])
        gates = arena[:, :].rearrange("p (c t) -> p c t", t=S)
        at = [0]

        def take(words):
            at[0] += words
            assert at[0] <= PK * S
            return arena[:, at[0] - words:at[0]]

        xs_f = take(TT * D)
        xs = xs_f.rearrange("p (a n) -> p a n", a=TT)
        w_slot_f = take(DC * 512)
        w_slot = w_slot_f.rearrange("p (k m n) -> p k m n", k=DC, m=4)
        w_glu_sb = w_slot_f.rearrange("p (k n) -> p k n", k=4)
        hT_f = take(DC * S)
        hT = hT_f.rearrange("p (k t) -> p k t", k=DC)
        mixn = hT_f.rearrange("p (a n) -> p a n", a=TT)
        slots = take(4 * S)
        uT, uTr, qT, kT = (slots[:, i * S:(i + 1) * S] for i in range(4))
        ssm = slots.rearrange("p (a n) -> p a n", a=TT)
        v_sb = take(TT * P).rearrange("p (a n) -> p a n", a=TT)
        bias_f = take(NH * 3 * P)
        bias = bias_f.rearrange("p (h n) -> p h n", h=NH)
        big = at[0]
        tab = take(2 * NT * S).rearrange("p (s n t) -> p s n t", s=2, n=NT)
        turn_f = take(2 * 2 * S)
        turn = turn_f.rearrange("p (s r t) -> p s r t", s=2, r=2)
        turn2 = take(2 * 2 * S).rearrange("p (s r t) -> p s r t", s=2, r=2)
        drive = take(2 * 2 * S).rearrange("p (s r t) -> p s r t", s=2, r=2)
        state = take(2 * 2 * S).rearrange("p (s r t) -> p s r t", s=2, r=2)
        outc = take(2 * 2 * S).rearrange("p (s r t) -> p s r t", s=2, r=2)
        outs = take(2 * 2 * S).rearrange("p (s r t) -> p s r t", s=2, r=2)
        w_out_sb = arena[:, big:big + DC * D].rearrange("p (k n) -> p k n", k=DC)
        xn = arena[:, big:big + TT * D].rearrange("p (a n) -> p a n", a=TT)
        b_f = take(NT * 2 * P)
        b_sb = b_f.rearrange("p (n r m) -> p n r m", n=NT, r=2)
        mixT = b_f.rearrange("p (k t) -> p k t", k=DC)
        c_raw = take(NT * 2 * 32).rearrange("p (n r m) -> p n r m", n=NT, r=2)
        c_sb = take(3 * NT * 32).rearrange("p (j n m) -> p j n m", j=3, n=NT)
        probs_f = take(4 * S)
        probs = probs_f.rearrange("p (s t) -> p s t", s=4)
        c_tmp = probs_f.rearrange("p (j n m) -> p j n m", j=4, n=NT)
        angle_t = probs_f.rearrange("p (n j) -> p n j", j=32)
        pT = take(2 * S).rearrange("p (s a t) -> p s a t", s=2, a=TT)
        attn = take(TT * AW).rearrange("p (a n) -> p a n", a=TT)
        yT = take(4 * S).rearrange("p (k t) -> p k t", k=4)
        ysum = take(2 * S).rearrange("p (s t) -> p s t", s=2)
        angle = take(NQ * NT * 32).rearrange("p (n j) -> p n j", j=32)
        par = take(3 * 32).rearrange("p (k n) -> p k n", k=3)
        sm = take(24 * 32).rearrange("p (k n) -> p k n", k=24)
        stat = take(32)
        sel0 = at[0]
        wq_slot = bias_f[:, 0:2048].rearrange("p (s k n) -> p s k n", s=2, k=DC)
        key_slot = bias_f[:, 2048:2048 + 2 * P].rearrange("p (s n) -> p s n", s=2)
        at[0] = big

        def again(words):
            return take(words)

        qh = again(S)
        sc = again(2 * TT * PK).rearrange("p (b a n) -> p b a n", b=2, a=TT)
        sc2 = again(2 * TT * PK).rearrange("p (b a n) -> p b a n", b=2, a=TT)
        t16 = again(4 * TOPK).rearrange("p (b a n) -> p b a n", b=2, a=TT)
        i16u = again(4 * TOPK).bitcast(U32).rearrange("p (b a n) -> p b a n", b=2, a=TT)
        i16 = again(4 * TOPK).rearrange("p (b a n) -> p b a n", b=2, a=TT)
        cand = again(TT * S).rearrange("p (a i j) -> p a i j", a=TT, i=TOPK)
        cand2 = again(TT * S).rearrange("p (a n) -> p a n", a=TT)
        top = again(TT * TOPK).rearrange("p (a n) -> p a n", a=TT)
        cu = again(TT * TOPK).bitcast(U32).rearrange("p (a n) -> p a n", a=TT)
        rank_u = again(2 * TT * TOPK).bitcast(U32).rearrange("p (b a n) -> p b a n", b=2, a=TT)
        rank = again(2 * TT * TOPK).rearrange("p (b a n) -> p b a n", b=2, a=TT)
        pick = again(2 * TT * S).rearrange("p (b a i j) -> p b a i j", b=2, a=TT, i=TOPK)
        sel = again(3 * TT * PH * TOPK).rearrange("p (k a h j) -> p k a h j", k=3, a=TT, h=PH)
        gsum = again(TT * PH).rearrange("p (a h) -> p a h", a=TT)
        assert at[0] <= big + DC * D
        xb = xs
        gfin = arena[:, TT * D:TT * D + D]
        rel_sb = arena[0:33, 8192:8192 + NH]
        rows_sb = arena[0:33, 8704:8704 + TOEP]
        toep_sb = arena[0:NH, 9216:9216 + TOEP]

        ps = ctx.enter_context(nc.psum_tensor("ps", [P, 8, 512], F32))

        toep_d = nc.dram_tensor("toep_scratch", [NH, TOEP], F32, kind="Internal")
        x_d = nc.dram_tensor("x_scratch", [P, TT * D], F32, kind="Internal")

        s_const = sem("s_const")
        s_memset = sem("s_memset")
        s_xin = sem("s_xin")
        s_rel = sem("s_rel")
        s_relones = sem("s_relones")
        s_toep_mm = sem("s_toep_mm")
        s_toep_sb = sem("s_toep_sb")
        s_toep_d = sem("s_toep_d")
        s_gain = sem("s_gain")
        s_par = sem("s_par")
        s_bias = sem("s_bias")
        s_layer = sem("s_layer")
        s_rms = sem("s_rms")
        s_rstd = sem("s_rstd")
        s_xn = sem("s_xn")
        s_tr = sem("s_tr")
        s_hT = sem("s_hT")
        s_p1 = sem("s_p1")
        s_p2 = sem("s_p2")
        s_p3 = sem("s_p3")
        s_coef = sem("s_coef")
        s_w = sem("s_w")
        s_bc = sem("s_bc")
        s_proj = sem("s_proj")
        s_u_sb = sem("s_u_sb")
        s_qkv_sb = sem("s_qkv_sb")
        s_turns = sem("s_turns")
        s_tab = sem("s_tab")
        s_c = sem("s_c")
        s_bu = sem("s_bu")
        s_pp = sem("s_pp")
        s_drive = sem("s_drive")
        s_state = sem("s_state")
        s_outs = sem("s_outs")
        s_outc = sem("s_outc")
        s_y = sem("s_y")
        s_ysum = sem("s_ysum")
        s_yT = sem("s_yT")
        s_score = sem("s_score")
        s_max = sem("s_max")
        s_exp = sem("s_exp")
        s_ptr = sem("s_ptr")
        s_pT = sem("s_pT")
        s_pv = sem("s_pv")
        s_attn = sem("s_attn")
        s_wglu = sem("s_wglu")
        s_wout = sem("s_wout")
        s_glu = sem("s_glu")
        s_sig = sem("s_sig")
        s_ssm = sem("s_ssm")
        s_mixn = sem("s_mixn")
        s_mixtr = sem("s_mixtr")
        s_mixT = sem("s_mixT")
        s_wo = sem("s_wo")
        s_x1 = sem("s_x1")
        s_spill = sem("s_spill")
        s_wq = [sem(f"s_wq{i}") for i in range(2)]
        s_q = sem("s_q")
        s_qh = sem("s_qh")
        s_sc = sem("s_sc")
        s_sc_sb = sem("s_sc_sb")
        s_sc_used = sem("s_sc_used")
        s_topd = sem("s_topd")
        s_gexp = sem("s_gexp")
        s_sel = sem("s_sel")
        s_seltr = sem("s_seltr")
        s_selT = sem("s_selT")
        s_hhi = sem("s_hhi")
        s_hlo = sem("s_hlo")
        s_hot = sem("s_hot")
        s_hot_free = sem("s_hot_free")
        s_gmm = sem("s_gmm")
        s_gates = sem("s_gates")
        s_u_ld = [sem(f"s_u_ld{i}") for i in range(2)]
        s_v_ld = [sem(f"s_v_ld{i}") for i in range(2)]
        s_u_hi = sem("s_u_hi")
        s_v_hi = sem("s_v_hi")
        s_u_lo = sem("s_u_lo")
        s_v_lo = sem("s_v_lo")
        s_u_mm = sem("s_u_mm")
        s_v_mm = sem("s_v_mm")
        s_gelu = sem("s_gelu")
        s_wt = sem("s_wt")
        s_xback = sem("s_xback")
        s_gfin = sem("s_gfin")
        s_fin = sem("s_fin")
        s_out = sem("s_out")

        block = ctx.enter_context(nc.Block())

        def col(ap, i, n=1):
            return ap[:, bass.ds(i, n)]

        def over(ap, n):
            return ap.unsqueeze(1).broadcast_to([ap.shape[0], n, ap.shape[1]])

        @block.sync
        def _(sp):
            sp.dma_start(cst[:, :], consts).then_inc(s_const, 16)
            sp.dma_start(xs, x.rearrange("(a p) n -> p a n", p=P)).then_inc(s_xin, 16)
            sp.wait_ge(s_relones, 1)
            sp.dma_start(rel_sb[0:32, :], rel_bias).then_inc(s_rel, 16)
            sp.dma_start(rows_sb, bucket_rows).then_inc(s_rel, 16)
            sp.wait_ge(s_toep_sb, 1)
            sp.dma_start(toep_d.ap(), toep_sb).then_inc(s_toep_d, 16)
            sp.wait_ge(s_toep_d, 16)
            overlap = bass.AP(toep_d, 0, [[1, P], [TOEP, NH], [1, 3 * P]])

            def load_u(l, c, s):
                sp.dma_start(u_raw[s][:, :, :], expert_u[bass.ds(l * PK + c, 1), :, :]
                             .rearrange("o p n -> (o p) n").rearrange("p (k n) -> p k n", k=DC)).then_inc(s_u_ld[s], 16)

            def load_v(l, c, s):
                sp.dma_start(v_raw[s][:, :], expert_v[bass.ds(l * PK + c, 1), :, :]
                             .rearrange("o p n -> (o p) n")).then_inc(s_v_ld[s], 16)

            with sp.Fori(0, DEPTH) as l:
                sp.wait_ge(s_layer, 1 + l)
                sp.dma_start(gain[:, :], gains[bass.ds(l, 1), :, :].rearrange("o p n -> (o p) n"))\
                    .then_inc(s_gain, 16)
                sp.dma_start(par, ssm_par[bass.ds(l, 1), :, :, :].rearrange("o p k n -> (o p) k n"))\
                    .then_inc(s_par, 16)
                sp.dma_start(bias, overlap).then_inc(s_bias, 16)
                for s in range(2):
                    load_u(l, s, s)
                    load_v(l, s, s)
                with sp.Fori(0, NQ) as q:
                    it = l * NQ + q
                    sp.wait_ge(s_proj, 1 + it * 3)
                    sp.dma_start(w_slot_f, w_in[bass.ds(it, 1), :, :].rearrange("o p n -> (o p) n"))\
                        .then_inc(s_w, 16)
                    sp.wait_ge(s_bu, 1 + it * NT)
                    sp.dma_start(b_f, ssm_b[bass.ds(it, 1), :, :].rearrange("o p n -> (o p) n"))\
                        .then_inc(s_bc, 16)
                    sp.wait_ge(s_c, 1 + it)
                    sp.dma_start(c_raw, ssm_c[bass.ds(it, 1), :, :].rearrange("o p n -> (o p) n")
                                 .rearrange("p (n r m) -> p n r m", n=NT, r=2)).then_inc(s_bc, 16)
                sp.wait_ge(s_proj, 1 + (l + 1) * 3 * NQ)
                sp.dma_start(w_glu_sb, w_glu[bass.ds(l, 1), :, :].rearrange("o p n -> (o p) n")
                             .rearrange("p (k n) -> p k n", k=4)).then_inc(s_wglu, 16)
                sp.wait_ge(s_y, 1 + (l + 1) * NT * NQ)
                sp.dma_start(w_out_sb, w_out[bass.ds(l, 1), :, :].rearrange("o p n -> (o p) n")
                             .rearrange("p (k n) -> p k n", k=DC)).then_inc(s_wout, 16)
                sp.wait_ge(s_x1, l + 1)
                sp.dma_start(x_d.ap(), xs_f).then_inc(s_spill, 16)
                with sp.Fori(0, PH // 2) as hp:
                    for s in range(2):
                        ih = l * PH + hp * 2 + s
                        if s == 0:
                            sp.wait_ge(s_sc, 1 + ih)
                        sp.dma_start(wq_slot[:, s, :, :], w_query[bass.ds(ih, 1), :, :]
                                     .rearrange("o p n -> (o p) n").rearrange("p (k n) -> p k n", k=DC))\
                            .then_inc(s_wq[s], 16)
                        sp.dma_start(key_slot[:, s, :], keys[bass.ds(ih, 1), :, :]
                                     .rearrange("o p n -> (o p) n")).then_inc(s_wq[s], 16)
                with sp.Fori(0, PK // 2 - 1) as i:
                    for s in range(2):
                        n = l * PK + i * 2 + s + 1
                        sp.wait_ge(s_u_lo, n)
                        load_u(l, i * 2 + s + 2, s)
                        sp.wait_ge(s_v_lo, n)
                        load_v(l, i * 2 + s + 2, s)
                sp.wait_ge(s_wt, (l + 1) * PK)
                sp.dma_start(xs_f, x_d.ap()).then_inc(s_xback, 16)
            sp.wait_ge(s_layer, 1 + DEPTH)
            sp.dma_start(gfin, norm_final.partition_broadcast(P)).then_inc(s_gfin, 16)
            sp.wait_ge(s_fin, 1)
            sp.dma_start(out.rearrange("(a p) n -> p a n", p=P), xn).then_inc(s_out, 16)
            sp.wait_ge(s_out, 16)

        @block.tensor
        def _(pe):
            pe.wait_ge(s_const, 16)
            pe.wait_ge(s_rel, 32)
            pe.matmul(ps[0:NH, 0, :], rel_sb, rows_sb, start=True, stop=True).then_inc(s_toep_mm, 1)

            def transposes(src, sem_done):
                for c in range(DC):
                    for a in range(TT):
                        m = pe.transpose(ps[:, c // 2, (c % 2) * S + a * P:(c % 2) * S + (a + 1) * P],
                                         src[:, a, c * P:(c + 1) * P], ident)
                    if c % 2:
                        m.then_inc(sem_done, 1)

            with pe.Fori(0, DEPTH) as l:
                pe.wait_ge(s_toep_sb, 1)
                pe.wait_ge(s_xn, 2 * l + 1)
                transposes(xn, s_tr)
                with pe.Fori(0, NQ) as q:
                    it = l * NQ + q
                    pe.wait_ge(s_hT, (2 * l + 1) * DC)
                    pe.wait_ge(s_bias, 16 * (l + 1))
                    pe.wait_ge(s_w, 16 * (it + 1))
                    pe.wait_ge(s_attn, 1 + it)
                    pe.wait_ge(s_pT, 1 + it * 2)
                    for kind, bank, o in ((3, 4, 0), (0, 0, 0), (1, 0, S)):
                        for k in range(DC):
                            m = pe.matmul(ps[:, bank, o:o + S], w_slot[:, k, kind, :], hT[:, k, :],
                                          start=(k == 0), stop=(k == DC - 1))
                        if kind != 0:
                            m.then_inc(s_proj, 1)
                    for a in range(TT):
                        for k in range(DC):
                            m = pe.matmul(ps[:, 1, a * P:(a + 1) * P], hT[:, k, a * P:(a + 1) * P],
                                          w_slot[:, k, 2, :], start=(k == 0), stop=(k == DC - 1))
                    m.then_inc(s_proj, 1)

                    def b_product(n):
                        if n < 2:
                            pe.wait_ge(s_pp, 1 + it * NT)
                        else:
                            pe.wait_ge(s_pp, 1 + it * NT + n - 1)
                        for r in range(2):
                            m = pe.matmul(ps[:, 5 + n % 2, r * S:(r + 1) * S], b_sb[:, n, r, :],
                                          uT if n % 2 == 0 else uTr, start=True, stop=True)
                        m.then_inc(s_bu, 1)

                    def c_product(n):
                        pe.wait_ge(s_outc, 1 + it * NT + n + 1)
                        pe.wait_ge(s_outs, it * NT + n + 1)
                        k, o = n // 2, (n % 2) * S
                        terms = ((0, outc[:, n % 2, 0, :]), (1, outs[:, n % 2, 1, :]),
                                 (2, outs[:, n % 2, 0, :]), (2, outc[:, n % 2, 1, :]))
                        for j, (kind, rhs) in enumerate(terms):
                            m = pe.matmul(ps[32 * k:32 * k + 32, 7, o:o + S], c_sb[:, kind, n, :], rhs,
                                          start=(j == 0), stop=(j == 3))
                        m.then_inc(s_y, 1)

                    def scores(head):
                        for a in range(TT):
                            dst = ps[:, 2 + head, a * S:(a + 1) * S]
                            pe.matmul(dst, antiident, bias[:, bass.ds(q * 2 + head, 1), P - a * P:P - a * P + S]
                                      .rearrange("p o n -> p (o n)"), start=True, stop=False)
                            m = pe.matmul(dst, qT[head * HD:(head + 1) * HD, a * P:(a + 1) * P],
                                          kT[head * HD:(head + 1) * HD, :], start=False, stop=True)
                        m.then_inc(s_score, 1)

                    def prob_transposes(head):
                        pe.wait_ge(s_exp, it * 2 + head + 1)
                        for a in range(TT):
                            for b in range(TT):
                                o = a * S + b * P
                                m = pe.transpose(ps[:, 4, o:o + P], probs[:, 2 * head + a, b * P:(b + 1) * P],
                                                 ident)
                        m.then_inc(s_ptr, 1)

                    def values(head):
                        pe.wait_ge(s_pT, 1 + it * 2 + head + 1)
                        for a in range(TT):
                            s = 2 * head + a
                            for b in range(TT):
                                m = pe.matmul(ps[:, 0, s * HD:(s + 1) * HD], pT[:, a, b, :],
                                              v_sb[:, b, head * HD:(head + 1) * HD],
                                              start=(b == 0), stop=(b == TT - 1))
                        if head:
                            m.then_inc(s_pv, 1)

                    pe.wait_ge(s_bc, 32 * (it + 1))
                    pe.wait_ge(s_u_sb, 2 * (it + 1))
                    b_product(0)
                    b_product(1)
                    pe.wait_ge(s_qkv_sb, 3 * (it + 1))
                    pe.wait_ge(s_ysum, 1 + it)
                    pe.wait_ge(s_c, 1 + it + 1)
                    for n in range(NT):
                        if n < 2:
                            scores(n)
                        c_product(n)
                        if n + 2 < NT:
                            b_product(n + 2)
                        if n in (2, 4):
                            prob_transposes(n // 2 - 1)
                        if n in (3, 5):
                            values(n // 2 - 1)

                pe.wait_ge(s_wglu, 16 * (l + 1))
                pe.wait_ge(s_yT, 1 + NQ * (l + 1))
                pe.wait_ge(s_attn, 1 + NQ * (l + 1))
                for a in range(TT):
                    for half in range(2):
                        for k in range(4):
                            m = pe.matmul(ps[:, 2 * a + half, :], yT[:, k, a * P:(a + 1) * P],
                                          w_glu_sb[:, k, half * AW:(half + 1) * AW],
                                          start=(k == 0), stop=(k == 3))
                    m.then_inc(s_glu, 1)
                pe.wait_ge(s_mixn, l + 1)
                transposes(mixn, s_mixtr)
                pe.wait_ge(s_mixT, (l + 1) * DC)
                pe.wait_ge(s_wout, 16 * (l + 1))
                for a in range(TT):
                    for half in range(2):
                        for k in range(DC):
                            m = pe.matmul(ps[:, 4 + 2 * a + half, :], mixT[:, k, a * P:(a + 1) * P],
                                          w_out_sb[:, k, half * 512:(half + 1) * 512],
                                          start=(k == 0), stop=(k == DC - 1))
                        m.then_inc(s_wo, 1)
                pe.wait_ge(s_xn, 2 * l + 2)
                transposes(xn, s_tr)

                with pe.Fori(0, PH // 2) as hp:
                    for s in range(2):
                        ih = l * PH + hp * 2 + s
                        if s == 0:
                            pe.wait_ge(s_hT, (2 * l + 2) * DC)
                        pe.wait_ge(s_wq[s], 32 * (l * (PH // 2) + hp + 1))
                        for k in range(DC):
                            m = pe.matmul(ps[:, 4 + s, 0:S], wq_slot[:, s, k, :], hT[:, k, :],
                                          start=(k == 0), stop=(k == DC - 1))
                        m.then_inc(s_q, 1)
                        pe.wait_ge(s_qh, ih + 1)
                        pe.wait_ge(s_sc_sb, 1 + ih)
                        for half in range(2):
                            for a in range(TT):
                                m = pe.matmul(ps[:, half, a * PK:(a + 1) * PK],
                                              qh[half * 64:half * 64 + 64, a * P:(a + 1) * P],
                                              key_slot[half * 64:half * 64 + 64, s, :], start=True, stop=True)
                        m.then_inc(s_sc, 1)
                pe.wait_ge(s_sel, l + 1)
                for k in range(3):
                    for a in range(TT):
                        m = pe.transpose(ps[:, 2 + k // 2, (k % 2) * S + a * P:(k % 2) * S + (a + 1) * P],
                                         sel[:, k, a, :, :].rearrange("p h j -> p (h j)"), ident)
                m.then_inc(s_seltr, 1)
                with pe.Fori(0, S // 8) as i:
                    for j in range(8):
                        tok = l * S + i * 8 + j
                        if j % 4 == 0:
                            pe.wait_ge(s_gates, (l * (S // 8) + i) * 2 + j // 4 + 1)
                        pe.wait_ge(s_hot, tok + 1)
                        m = pe.matmul(ps[:, 6 + j // 4, (j % 4) * P:(j % 4 + 1) * P], hot[:, j % 4, 1, :],
                                      hot[:, j % 4, 0, :], start=True, stop=True)
                        m.then_inc(s_hot_free, 1)

                def up(c, s):
                    n = l * PK + c
                    pe.wait_ge(s_u_lo, n + 1)
                    pe.wait_ge(s_gelu, 1 + (l * PK if isinstance(c, int) else n - 1))
                    terms = ((0, 0), (0, 1), (1, 0))
                    for k in range(DC):
                        for j, (wp, hp_) in enumerate(terms):
                            m = pe.matmul(ps[:, 4 + s, 0:S], u_hl[s][:, wp, k, :], h_hl[:, hp_, k, :],
                                          start=(k == 0 and j == 0), stop=(k == DC - 1 and j == 2))
                    m.then_inc(s_u_mm, 1)

                def down(c, s, first=False, last=False):
                    n = l * PK + c
                    pe.wait_ge(s_v_lo, n + 1)
                    pe.wait_ge(s_wt, n + 1)
                    terms = ((0, 0), (0, 1), (1, 0))
                    for a in range(TT):
                        for j, (wp, vp) in enumerate(terms):
                            for half in range(2):
                                m = pe.matmul(ps[:, 2 * a + half, :], w_hl[s][:, wp, a * P:(a + 1) * P],
                                              v_hl[s][:, vp, half * 512:(half + 1) * 512],
                                              start=(first and j == 0), stop=(last and j == 2))
                    m.then_inc(s_v_mm, 1)

                pe.wait_ge(s_hlo, l + 1)
                pe.wait_ge(s_selT, l + 1)
                up(0, 0)
                up(1, 1)
                down(0, 0, first=True)
                with pe.Fori(0, PK // 2 - 1) as i:
                    up(i * 2 + 2, 0)
                    down(i * 2 + 1, 1)
                    up(i * 2 + 3, 1)
                    down(i * 2 + 2, 0)
                down(PK - 1, 1, last=True)

        @block.scalar
        def _(act):
            def fenced():
                act.activation(fence[0:1, 0:1], fence[0:1, 1:2], ACT.Copy)

            act.wait_ge(s_toep_mm, 1)
            act.activation(toep_sb, ps[0:NH, 0, :], ACT.Copy).then_inc(s_toep_sb, 1)
            act.wait_ge(s_memset, 1)

            def squares(src, n, j, scratch):
                return act.activation(scratch[:, 0:n], src, ACT.Square, accum_out=stat[:, j:j + 1])

            with act.Fori(0, DEPTH) as l:
                act.wait_ge(s_xin, 16)
                act.wait_ge(s_layer, 1 + l)
                for a in range(TT):
                    if a:
                        act.drain()
                    squares(xs[:, a, :], D, a, turn_f)
                act.drain()
                act.activation(stat[:, 2:4], stat[:, 0:2], ACT.Sqrt, bias=eps_c, scale=1.0 / D).then_inc(s_rms, 1)
                act.wait_ge(s_par, 16 * (l + 1))
                act.activation(sm[:, 0, :], par[:, 2, :], ACT.Exp).then_inc(s_p1, 1)
                act.wait_ge(s_p2, l + 1)
                act.activation(sm[:, 3, :], sm[:, 2, :], ACT.Exp)
                act.activation(sm[:, 9, :], sm[:, 7, :], ACT.Sin, scale=TWO_PI_BELOW)
                act.activation(sm[:, 8, :], sm[:, 7, :], ACT.Abs)
                act.drain()
                act.activation(sm[:, 10, :], sm[:, 8, :], ACT.Sin, scale=-TWO_PI_BELOW, bias=half_pi_c)\
                    .then_inc(s_p3, 1)
                act.wait_ge(s_gain, 16 * (l + 1))
                for c in range(DC):
                    act.wait_ge(s_tr, l * DC + c // 2 + 1)
                    act.activation(hT[:, c, :], ps[:, c // 2, (c % 2) * S:(c % 2 + 1) * S], ACT.Copy,
                                   scale=g_mix[:, c:c + 1]).then_inc(s_hT, 1)
                with act.Fori(0, NQ) as q:
                    it = l * NQ + q
                    act.wait_ge(s_turns, it + 1)
                    act.activation(tab[:, 1, :, :], tab[:, 0, :, :], ACT.Abs)
                    act.drain()
                    act.activation(tab[:, 0, :, :], tab[:, 0, :, :], ACT.Sin, scale=TWO_PI_BELOW)
                    act.activation(tab[:, 1, :, :], tab[:, 1, :, :], ACT.Sin, scale=-TWO_PI_BELOW,
                                   bias=half_pi_c).then_inc(s_tab, 1)
                    act.wait_ge(s_proj, 1 + it * 3 + 1)
                    act.wait_ge(s_ysum, 1 + it)
                    act.activation(uT, ps[:, 4, 0:S], ACT.Copy).then_inc(s_u_sb, 1)
                    act.activation(uTr, ps[:, 4, 0:S][:, ::-1], ACT.Copy).then_inc(s_u_sb, 1)
                    act.wait_ge(s_proj, 1 + it * 3 + 2)
                    act.activation(qT, ps[:, 0, 0:S], ACT.Copy, scale=HD ** -0.5).then_inc(s_qkv_sb, 1)
                    act.activation(kT, ps[:, 0, S:2 * S], ACT.Copy).then_inc(s_qkv_sb, 1)
                    act.wait_ge(s_proj, 1 + it * 3 + 3)
                    act.activation(v_sb, ps[:, 1, 0:S].rearrange("p (a n) -> p a n", a=TT), ACT.Copy)\
                        .then_inc(s_qkv_sb, 1)
                    for head in range(2):
                        act.wait_ge(s_max, it * 2 + head + 1)
                        for a in range(TT):
                            s = 2 * head + a
                            m = act.activation(probs[:, s, :], ps[:, 2 + head, a * S:(a + 1) * S], ACT.Exp,
                                               bias=stat[:, 8 + s:9 + s], accum_out=stat[:, 12 + s:13 + s])
                        m.then_inc(s_exp, 1)
                    for head in range(2):
                        act.wait_ge(s_ptr, 1 + it * 2 + head + 1)
                        act.activation(pT, ps[:, 4, :].rearrange("p (s a n) -> p s a n", s=2, a=TT), ACT.Copy)\
                            .then_inc(s_pT, 1)
                    act.drain()
                    act.wait_ge(s_ysum, 1 + it + 1)
                    fenced()
                    act.activation(yT[:, bass.ds(q, 1), :].rearrange("p o n -> p (o n)"), ysum[:, 1, :],
                                   ACT.Gelu).then_inc(s_yT, 1)

                for a in range(TT):
                    act.wait_ge(s_glu, l * TT + a + 1)
                    act.activation(ssm[:, a, :], ps[:, 2 * a + 1, :], ACT.Sigmoid).then_inc(s_sig, 1)
                act.wait_ge(s_attn, 1 + NQ * (l + 1))
                for a in range(TT):
                    squares(attn[:, a, :], AW, 16 + a, probs_f[:, a * AW:(a + 1) * AW])
                act.drain()
                for a in range(TT):
                    act.wait_ge(s_ssm, l * TT + a + 1)
                    squares(ssm[:, a, :], AW, 18 + a, probs_f[:, a * AW:(a + 1) * AW])
                act.drain()
                act.activation(stat[:, 20:24], stat[:, 16:20], ACT.Sqrt, bias=eps_c, scale=1.0 / AW)\
                    .then_inc(s_rms, 1)
                for c in range(DC):
                    act.wait_ge(s_mixtr, l * (DC // 2) + c // 2 + 1)
                    act.activation(mixT[:, c, :], ps[:, c // 2, (c % 2) * S:(c % 2 + 1) * S], ACT.Copy,
                                   scale=g_cat[:, c:c + 1]).then_inc(s_mixT, 1)
                act.wait_ge(s_x1, l + 1)
                for a in range(TT):
                    if a:
                        act.drain()
                    squares(xs[:, a, :], D, a, probs_f)
                act.drain()
                act.activation(stat[:, 2:4], stat[:, 0:2], ACT.Sqrt, bias=eps_c, scale=1.0 / D).then_inc(s_rms, 1)
                for c in range(DC):
                    act.wait_ge(s_tr, l * DC + DC // 2 + c // 2 + 1)
                    act.activation(hT[:, c, :], ps[:, c // 2, (c % 2) * S:(c % 2 + 1) * S], ACT.Copy,
                                   scale=g_ffn[:, c:c + 1]).then_inc(s_hT, 1)
                act.drain()
                act.activation(h_hl[:, 0, :, :], hT, ACT.Copy).then_inc(s_hhi, 1)
                with act.Fori(0, PH // 2) as hp:
                    for s in range(2):
                        ih = l * PH + hp * 2 + s
                        act.wait_ge(s_q, ih + 1)
                        act.activation(qh, ps[:, 4 + s, 0:S], ACT.Copy).then_inc(s_qh, 1)
                        act.wait_ge(s_sc, 1 + ih + 1)
                        act.wait_ge(s_sc_used, 1 + ih)
                        act.activation(sc, ps[:, 0:2, 0:S].rearrange("p b (a n) -> p b a n", a=TT), ACT.Copy)\
                            .then_inc(s_sc_sb, 1)
                act.wait_ge(s_topd, l + 1)
                act.activation(sel[:, 2, :, :, :], sel[:, 2, :, :, :], ACT.Exp).then_inc(s_gexp, 1)
                act.wait_ge(s_seltr, l + 1)
                act.activation(sel_T[:, 0:2, :], ps[:, 2, :].rearrange("p (k t) -> p k t", k=2), ACT.Copy)
                act.activation(sel_T[:, 2, :], ps[:, 3, 0:S], ACT.Copy).then_inc(s_selT, 1)
                act.wait_ge(s_spill, 16 * (l + 1))
                with act.Fori(0, S // 8) as i:
                    for j in range(2):
                        act.drain()
                        act.wait_ge(s_hot_free, 4 + l * S + i * 8 + 4 * j + 4)
                        fenced()
                        act.activation(gates[:, :, bass.ds(i * 8 + j * 4, 4)],
                                       ps[:, 6 + j, :].rearrange("p (t c) -> p c t", c=PK), ACT.Copy)\
                            .then_inc(s_gates, 1)

                def split_high(c, pair, s):
                    n = l * PK + c
                    act.wait_ge(s_u_ld[s], 16 * (l * (PK // 2) + pair + 1))
                    if not (isinstance(c, int) and c < 2):
                        act.wait_ge(s_u_mm, n - 1)
                    act.activation(u_hl[s][:, 0, :, :], u_raw[s][:, :, :], ACT.Copy).then_inc(s_u_hi, 1)
                    act.wait_ge(s_v_ld[s], 16 * (l * (PK // 2) + pair + 1))
                    if not (isinstance(c, int) and c < 2):
                        act.wait_ge(s_v_mm, 1 + n - 1)
                    act.activation(v_hl[s][:, 0, :], v_raw[s][:, :], ACT.Copy).then_inc(s_v_hi, 1)

                def gelu(c, s):
                    n = l * PK + c
                    act.wait_ge(s_u_mm, n + 1)
                    if not (isinstance(c, int) and c < 2):
                        act.wait_ge(s_wt, n - 1)
                    act.activation(act_w[:, s, :], ps[:, 4 + s, 0:S], ACT.Gelu).then_inc(s_gelu, 1)

                act.wait_ge(s_v_mm, 1 + l * PK)
                split_high(0, 0, 0)
                split_high(1, 0, 1)
                for s in range(2):
                    gelu(s, s)
                    split_high(s + 2, 1, s)
                with act.Fori(0, PK // 2 - 2) as i:
                    for s in range(2):
                        gelu(i * 2 + s + 2, s)
                        split_high(i * 2 + s + 4, i + 2, s)
                gelu(PK - 2, 0)
                gelu(PK - 1, 1)

            act.wait_ge(s_layer, 1 + DEPTH)
            for a in range(TT):
                if a:
                    act.drain()
                squares(xs[:, a, :], D, a, turn_f)
            act.drain()
            act.activation(stat[:, 2:4], stat[:, 0:2], ACT.Sqrt, bias=eps_c, scale=1.0 / D).then_inc(s_rms, 1)

        @block.vector
        def _(dve):
            dve.memset(rel_sb, 1.0).then_inc(s_relones, 1)
            dve.memset(fence[:, :], 0.0)
            dve.memset(eps_c, EPS)
            dve.memset(half_pi_c, HALF_PI).then_inc(s_memset, 1)
            dve.sem_inc(s_hot_free, 4)
            dve.sem_inc(s_gates, 2)
            for counter in (s_layer, s_proj, s_bu, s_c, s_attn, s_pT, s_pp, s_drive, s_y, s_state, s_outc, s_ysum, s_yT, s_ptr, s_sc, s_sc_sb, s_sc_used, s_v_mm, s_gelu):
                dve.sem_inc(counter, 1)

            def tt(o, a, b, op):
                return dve.tensor_tensor(o, a, b, op)

            with dve.Fori(0, DEPTH) as l:
                dve.wait_ge(s_rms, 3 * l + 1)
                dve.reciprocal(stat[:, 4:6], stat[:, 2:4])
                dve.drain()
                for a in range(TT):
                    m = dve.tensor_scalar(xn[:, a, :], xs[:, a, :], stat[:, 4 + a:5 + a], None, ALU.mult)
                m.then_inc(s_xn, 1)

                lr, li, step = par[:, 0, :], par[:, 1, :], sm[:, 0, :]
                theta, sig, mag, turns, whole, phi = (sm[:, i, :] for i in (1, 2, 3, 4, 5, 7))
                dve.wait_ge(s_p1, l + 1)
                tt(theta, li, step, ALU.mult)
                tt(sig, lr, step, ALU.mult)
                dve.drain()
                dve.tensor_scalar(turns, theta, INV_TWO_PI, None, ALU.mult)
                dve.drain()
                dve.tensor_scalar(whole, turns, ROUND, ROUND, ALU.add, ALU.subtract)
                dve.drain()
                dve.scalar_tensor_tensor(theta, whole, -TWO_PI_A, theta, ALU.mult, ALU.add)
                dve.drain()
                dve.scalar_tensor_tensor(theta, whole, -TWO_PI_B, theta, ALU.mult, ALU.add)
                dve.drain()
                dve.tensor_scalar(sm[:, 6, :], theta, INV_TWO_PI, None, ALU.mult)
                dve.drain()
                dve.tensor_scalar(sm[:, 6, :], sm[:, 6, :], 0.5, -0.5, ALU.min, ALU.max)
                dve.drain()
                dve.tensor_copy(phi, sm[:, 6, :]).then_inc(s_p2, 1)
                dve.tensor_scalar(sm[:, 11, :], sm[:, 6, :], GRID14, GRID14, ALU.add, ALU.subtract)
                dve.drain()
                dve.tensor_tensor(sm[:, 12, :], sm[:, 6, :], sm[:, 11, :], ALU.subtract)
                dve.drain()
                n_all = NQ * NT

                def wide(i):
                    return sm[:, i, :].unsqueeze(2).broadcast_to([P, n_all, 32])

                ab = over(steps_ab, n_all)
                tt(angle, wide(11), ab, ALU.mult)
                dve.drain()
                dve.tensor_scalar(angle_t, angle, ROUND, ROUND, ALU.add, ALU.subtract)
                dve.drain()
                tt(angle, angle, angle_t, ALU.subtract)
                dve.drain()
                tt(angle_t, wide(12), ab, ALU.mult)
                dve.drain()
                tt(angle, angle, angle_t, ALU.add)
                dve.wait_ge(s_p3, l + 1)
                sin, cos = sm[:, 9, :], sm[:, 10, :]
                re, im, den, tmp = (sm[:, i, :] for i in (13, 14, 15, 16))
                f_re, f_im, nf_re, nf_im = (sm[:, i, :] for i in (17, 18, 19, 20))
                tt(re, mag, cos, ALU.mult)
                tt(im, mag, sin, ALU.mult)
                tt(den, lr, lr, ALU.mult)
                tt(tmp, li, li, ALU.mult)
                dve.drain()
                dve.tensor_scalar(re, re, -1.0, None, ALU.add)
                tt(den, den, tmp, ALU.add)
                dve.drain()
                dve.reciprocal(den, den)
                tt(f_re, re, lr, ALU.mult)
                tt(tmp, im, li, ALU.mult)
                dve.drain()
                tt(f_re, f_re, tmp, ALU.add)
                tt(f_im, im, lr, ALU.mult)
                dve.drain()
                tt(tmp, re, li, ALU.mult)
                dve.drain()
                tt(f_im, f_im, tmp, ALU.subtract)
                tt(f_re, f_re, den, ALU.mult)
                dve.drain()
                tt(f_im, f_im, den, ALU.mult)
                dve.tensor_scalar(nf_re, f_re, -1.0, None, ALU.mult)
                dve.drain()
                dve.tensor_scalar(nf_im, f_im, -1.0, None, ALU.mult).then_inc(s_coef, 1)

                with dve.Fori(0, NQ) as q:
                    it = l * NQ + q
                    a_part = angle[:, bass.ds(q * NT, NT), 0:16].unsqueeze(3).broadcast_to([P, NT, 16, 16])
                    b_part = angle[:, bass.ds(q * NT, NT), 16:32].unsqueeze(2).broadcast_to([P, NT, 16, 16])
                    t0 = tab[:, 0, :, :].rearrange("p n (a b) -> p n a b", a=16)
                    dve.wait_ge(s_outc, 1 + it * NT)
                    dve.wait_ge(s_tr, l * DC + DC // 2)
                    tt(t0, a_part, b_part, ALU.add)
                    dve.drain()
                    dve.tensor_scalar(tab[:, 1, :, :], tab[:, 0, :, :], ROUND, ROUND, ALU.add, ALU.subtract)
                    dve.drain()
                    tt(tab[:, 0, :, :], tab[:, 0, :, :], tab[:, 1, :, :], ALU.subtract).then_inc(s_turns, 1)
                    dve.wait_ge(s_tab, it + 1)

                    def two(j, n):
                        return over(tab[:, j, n, :], 2)

                    def turn_in(n):
                        s = n % 2
                        dve.wait_ge(s_bu, 1 + it * NT + n + 1)
                        if n < 2:
                            dve.wait_ge(s_drive, 1 + it * NT)
                        else:
                            dve.wait_ge(s_drive, 1 + it * NT + n - 1)
                        src = ps[:, 5 + s, :].rearrange("p (r t) -> p r t", r=2)
                        tt(turn[:, s, :, :], src, two(1, n), ALU.mult)
                        tt(turn2[:, s, :, :], src, two(0, n), ALU.mult).then_inc(s_pp, 1)

                    def scan(n):
                        s = n % 2
                        dve.wait_ge(s_drive, 1 + it * NT + n + 1)
                        if n < 2:
                            dve.wait_ge(s_y, 1 + it * NT)
                        else:
                            dve.wait_ge(s_y, 1 + it * NT + n - 1)
                        r_all = col(mag, q * NT + n).broadcast_to([P, S])
                        for r in range(2):
                            dve.tensor_tensor_scan(state[:, s, r, :], r_all, drive[:, s, r, :], 0.0,
                                                   ALU.mult, ALU.add).then_inc(s_state, 1)
                        dve.wait_ge(s_state, 1 + 2 * (it * NT + n + 1))
                        tt(outs[:, s, :, :], state[:, s, :, :], two(0, n), ALU.mult).then_inc(s_outs, 1)

                    def row_max(head):
                        dve.wait_ge(s_score, it * 2 + head + 1)
                        dve.tensor_reduce(stat[:, 8 + 2 * head:10 + 2 * head],
                                          ps[:, 2 + head, :].rearrange("p (a n) -> p a n", a=TT), AX.X, ALU.max,
                                          negate=True).then_inc(s_max, 1)

                    def attn_out():
                        dve.wait_ge(s_pv, it + 1)
                        dve.reciprocal(stat[:, 24:28], stat[:, 12:16])
                        dve.drain()
                        for s in range(4):
                            m = dve.tensor_scalar(attn[:, s % 2, bass.ds((q * 2 + s // 2) * HD, HD)],
                                                  ps[:, 0, s * HD:(s + 1) * HD], stat[:, 24 + s:25 + s], None,
                                                  ALU.mult)
                        m.then_inc(s_attn, 1)

                    turn_in(0)
                    for n in range(NT):
                        if n + 1 < NT:
                            turn_in(n + 1)
                        if n in (1, 2):
                            row_max(n - 1)
                        scan(n)
                        if n == 6:
                            attn_out()
                    dve.wait_ge(s_y, 1 + (it + 1) * NT)
                    dve.scalar_tensor_tensor(ysum[:, 0, :], uT, col(d_skip, q), ps[:, 7, 0:S], ALU.mult, ALU.add)
                    dve.drain()
                    dve.wait_ge(s_yT, 1 + it)
                    tt(ysum[:, 1, :], ysum[:, 0, :], ps[:, 7, S:2 * S][:, ::-1], ALU.add).then_inc(s_ysum, 1)

                for a in range(TT):
                    dve.wait_ge(s_sig, l * TT + a + 1)
                    tt(ssm[:, a, :], ps[:, 2 * a, :], ssm[:, a, :], ALU.mult).then_inc(s_ssm, 1)
                dve.wait_ge(s_rms, 3 * l + 2)
                dve.reciprocal(stat[:, 20:24], stat[:, 20:24])
                dve.drain()
                for a in range(TT):
                    dve.tensor_scalar(mixn[:, a, 0:AW], attn[:, a, :], stat[:, 20 + a:21 + a], None, ALU.mult)
                    m = dve.tensor_scalar(mixn[:, a, AW:D], ssm[:, a, :], stat[:, 22 + a:23 + a], None, ALU.mult)
                m.then_inc(s_mixn, 1)
                for a in range(TT):
                    for half in range(2):
                        dve.wait_ge(s_wo, 4 * l + 2 * a + half + 1)
                        o = xs[:, a, half * 512:(half + 1) * 512]
                        m = tt(o, o, ps[:, 4 + 2 * a + half, :], ALU.add)
                m.then_inc(s_x1, 1)
                dve.wait_ge(s_rms, 3 * l + 3)
                dve.reciprocal(stat[:, 4:6], stat[:, 2:4])
                dve.drain()
                for a in range(TT):
                    m = dve.tensor_scalar(xn[:, a, :], xs[:, a, :], stat[:, 4 + a:5 + a], None, ALU.mult)
                m.then_inc(s_xn, 1)
                dve.wait_ge(s_hhi, l + 1)
                tt(h_hl[:, 1, :, :], hT, h_hl[:, 0, :, :].bitcast(F32), ALU.subtract).then_inc(s_hlo, 1)

                def top16(src, spare, vals, idx):
                    for a, b, v, i in zip(src, spare, vals, idx):
                        dve.max(v[:, 0:8], a)
                    dve.drain()
                    for a, b, v, i in zip(src, spare, vals, idx):
                        dve.match_replace(b, v[:, 0:8], a, LOWEST)
                        dve.max_index(i[:, 0:8], v[:, 0:8], a)
                    dve.drain()
                    for a, b, v, i in zip(src, spare, vals, idx):
                        dve.max(v[:, 8:16], b)
                    dve.drain()
                    for a, b, v, i in zip(src, spare, vals, idx):
                        m = dve.max_index(i[:, 8:16], v[:, 8:16], b)
                    return m

                with dve.Fori(0, PH) as h:
                    ih = l * PH + h
                    dve.wait_ge(s_sc_sb, 1 + ih + 1)
                    dve.memset(fence[:, 0:1], 0.0)
                    pairs = [(b, a) for b in range(2) for a in range(TT)]
                    top16([sc[:, b, a, :] for b, a in pairs], [sc2[:, b, a, :] for b, a in pairs],
                          [t16[:, b, a, :] for b, a in pairs], [i16u[:, b, a, :] for b, a in pairs])\
                        .then_inc(s_sc_used, 1)
                    dve.drain()
                    dve.tensor_copy(i16, i16u)
                    tt(cand, t16[:, 0, :, :].unsqueeze(3).broadcast_to([P, TT, 16, 16]),
                       t16[:, 1, :, :].unsqueeze(2).broadcast_to([P, TT, 16, 16]), ALU.add)
                    dve.drain()
                    cf = [cand[:, a, :, :].rearrange("p i j -> p (i j)") for a in range(TT)]
                    top16(cf, [cand2[:, a, :] for a in range(TT)], [top[:, a, :] for a in range(TT)],
                          [cu[:, a, :] for a in range(TT)])
                    dve.drain()
                    dve.tensor_scalar(rank_u[:, 0, :, :], cu, 4, None, ALU.logical_shift_right)
                    dve.tensor_scalar(rank_u[:, 1, :, :], cu, 15, None, ALU.bitwise_and)
                    tt(sel[:, 2, :, bass.ds(h, 1), :].rearrange("p a o j -> p a (o j)"), top,
                       top[:, :, 0:1].broadcast_to([P, TT, TOPK]), ALU.subtract)
                    dve.drain()
                    dve.tensor_copy(rank, rank_u)
                    dve.drain()
                    for b in range(2):
                        for a in range(TT):
                            tt(pick[:, b, a, :, :], rank[:, b, a, :].unsqueeze(2).broadcast_to([P, 16, 16]),
                               over(iota16, 16), ALU.is_equal)
                    dve.drain()
                    for b in range(2):
                        for a in range(TT):
                            tt(pick[:, b, a, :, :], pick[:, b, a, :, :], over(i16[:, b, a, :], 16), ALU.mult)
                    dve.drain()
                    for b in range(2):
                        dve.tensor_reduce(sel[:, b, :, bass.ds(h, 1), :].rearrange("p a o j -> p a (o j)"),
                                          pick[:, b, :, :, :], AX.X, ALU.add)
                    dve.drain()
                dve.memset(fence[:, 0:1], 0.0).then_inc(s_topd, 1)
                dve.wait_ge(s_gexp, l + 1)
                dve.tensor_reduce(gsum, sel[:, 2, :, :, :], AX.X, ALU.add)
                dve.drain()
                dve.reciprocal(gsum, gsum)
                dve.drain()
                tt(sel[:, 2, :, :, :], sel[:, 2, :, :, :], gsum.unsqueeze(3).broadcast_to([P, TT, PH, TOPK]),
                   ALU.mult).then_inc(s_sel, 1)

                with dve.Fori(0, S // 8) as i:
                    dve.wait_ge(s_selT, l + 1)
                    for j in range(8):
                        tok = l * S + i * 8 + j
                        dve.wait_ge(s_hot_free, tok + 1)
                        t = i * 8 + j
                        dve.tensor_scalar(hot[:, j % 4, 0, :], iota, col(sel_T[:, 0, :], t),
                                          col(sel_T[:, 2, :], t), ALU.is_equal, ALU.mult)
                        dve.tensor_scalar(hot[:, j % 4, 1, :], iota, col(sel_T[:, 1, :], t), None,
                                          ALU.is_equal).then_inc(s_hot, 1)

                def split_low(c, s):
                    n = l * PK + c
                    dve.wait_ge(s_u_hi, n + 1)
                    tt(u_hl[s][:, 1, :, :], u_raw[s][:, :, :], u_hl[s][:, 0, :, :].bitcast(F32), ALU.subtract)\
                        .then_inc(s_u_lo, 1)
                    dve.wait_ge(s_v_hi, n + 1)
                    tt(v_hl[s][:, 1, :], v_raw[s][:, :], v_hl[s][:, 0, :].bitcast(F32), ALU.subtract)\
                        .then_inc(s_v_lo, 1)

                def weights(c, s):
                    n = l * PK + c
                    dve.wait_ge(s_gelu, 1 + n + 1)
                    if not (isinstance(c, int) and c < 2):
                        dve.wait_ge(s_v_mm, 1 + n - 1)
                    g = gates[:, bass.ds(c, 1), :].rearrange("p o t -> p (o t)")
                    tt(w_hl[s][:, 0, :], act_w[:, s, :], g, ALU.mult)
                    tt(act_w[:, s, :], act_w[:, s, :], g, ALU.mult)
                    dve.drain()
                    tt(w_hl[s][:, 1, :], act_w[:, s, :], w_hl[s][:, 0, :].bitcast(F32), ALU.subtract)\
                        .then_inc(s_wt, 1)

                dve.wait_ge(s_gates, 2 + (l + 1) * (S // 4))
                split_low(0, 0)
                split_low(1, 1)
                for s in range(2):
                    weights(s, s)
                    split_low(s + 2, s)
                with dve.Fori(0, PK // 2 - 2) as i:
                    for s in range(2):
                        weights(i * 2 + s + 2, s)
                        split_low(i * 2 + s + 4, s)
                weights(PK - 2, 0)
                weights(PK - 1, 1)
                dve.wait_ge(s_v_mm, 1 + (l + 1) * PK)
                dve.wait_ge(s_xback, 16 * (l + 1))
                for a in range(TT):
                    for half in range(2):
                        o = xs[:, a, half * 512:(half + 1) * 512]
                        m = tt(o, o, ps[:, 2 * a + half, :], ALU.add)
                m.then_inc(s_layer, 1)

            dve.wait_ge(s_rms, 3 * DEPTH + 1)
            dve.reciprocal(stat[:, 4:6], stat[:, 2:4])
            dve.wait_ge(s_gfin, 16)
            dve.drain()
            for a in range(TT):
                m = dve.scalar_tensor_tensor(xn[:, a, :], xs[:, a, :], stat[:, 4 + a:5 + a], gfin,
                                             ALU.mult, ALU.mult)
            m.then_inc(s_fin, 1)

        @block.gpsimd
        def _(pool):
            def tt(o, a, b, op):
                return pool.tensor_tensor(o, a, b, op)

            with pool.Fori(0, DEPTH) as l:
                with pool.Fori(0, NQ) as q:
                    it = l * NQ + q

                    def f(i):
                        return sm[:, i, bass.ds(q * NT, NT)].unsqueeze(2).broadcast_to([P, NT, 32])

                    pool.wait_ge(s_coef, l + 1)
                    pool.wait_ge(s_bc, 32 * (it + 1))
                    cre, cim = c_raw[:, :, 0, :], c_raw[:, :, 1, :]
                    pool.wait_ge(s_ptr, 1 + it * 2)
                    tt(c_tmp[:, 0, :, :], cre, f(17), ALU.mult)
                    tt(c_tmp[:, 1, :, :], cim, f(18), ALU.mult)
                    tt(c_tmp[:, 2, :, :], cre, f(20), ALU.mult)
                    tt(c_tmp[:, 3, :, :], cim, f(19), ALU.mult)
                    pool.drain()
                    pool.wait_ge(s_y, 1 + it * NT)
                    tt(c_sb[:, 0, :, :], c_tmp[:, 0, :, :], c_tmp[:, 1, :, :], ALU.subtract)
                    tt(c_sb[:, 1, :, :], c_tmp[:, 1, :, :], c_tmp[:, 0, :, :], ALU.subtract)
                    tt(c_sb[:, 2, :, :], c_tmp[:, 2, :, :], c_tmp[:, 3, :, :], ALU.add).then_inc(s_c, 1)

                    def drives(n):
                        s = n % 2
                        pool.wait_ge(s_pp, 1 + it * NT + n + 1)
                        if n < 2:
                            pool.wait_ge(s_state, 1 + 2 * it * NT)
                        else:
                            pool.wait_ge(s_state, 1 + 2 * (it * NT + n - 1))
                        tt(drive[:, s, 0, :], turn[:, s, 0, :], turn2[:, s, 1, :], ALU.add)
                        tt(drive[:, s, 1, :], turn[:, s, 1, :], turn2[:, s, 0, :], ALU.subtract)\
                            .then_inc(s_drive, 1)

                    drives(0)
                    for n in range(NT):
                        if n + 1 < NT:
                            drives(n + 1)
                        pool.wait_ge(s_state, 1 + 2 * (it * NT + n + 1))
                        if n < 2:
                            pool.wait_ge(s_y, 1 + it * NT)
                        else:
                            pool.wait_ge(s_y, 1 + it * NT + n - 1)
                        tt(outc[:, n % 2, :, :], state[:, n % 2, :, :], over(tab[:, 1, n, :], 2), ALU.mult)\
                            .then_inc(s_outc, 1)


def kernel(x, w_in, w_out, rel_bias, g_attn, g_ssm, norm_mix, norm_ffn, lam_re, lam_im, log_step,
           b_re, b_im, c_re, c_im, d_skip, w_glu, w_query, sub_keys, expert_u, expert_v, norm_final):
    import numpy as np
    import concourse.bacc as bacc
    from concourse.bass_utils import run_bass_kernel_spmd

    f32 = np.float32
    L = DEPTH

    def lay(a, shape, perm, to):
        return np.ascontiguousarray(np.asarray(a).reshape(shape).transpose(perm).reshape(to))

    def columns(a, n):
        return np.asarray(a).reshape(L, n, P).transpose(0, 2, 1)

    a_w_in = lay(w_in, (L, DC, P, 4, NQ, P), (0, 4, 2, 1, 3, 5), (L * NQ, P, DC * 512))
    a_w_out = lay(w_out, (L, DC, P, D), (0, 2, 1, 3), (L, P, DC * D))
    a_w_glu = lay(w_glu, (L, 4, P, D), (0, 2, 1, 3), (L, P, 4 * D))
    a_w_query = lay(w_query, (L, DC, P, PH, P), (0, 3, 2, 1, 4), (L * PH, P, DC * P))
    a_keys = lay(sub_keys, (L, 2, PH, PK, 64), (0, 2, 1, 4, 3), (L * PH, P, PK))
    a_u = lay(expert_u, (L, PK, PK, DC, P), (0, 1, 4, 3, 2), (L * PK, P, DC * P))
    a_v = lay(expert_v, (L, PK, PK, D), (0, 1, 2, 3), (L * PK, PK, D))
    a_gain = np.ascontiguousarray(np.concatenate(
        [columns(norm_mix, 8), columns(norm_ffn, 8), columns(g_attn, 4), columns(g_ssm, 4),
         columns(d_skip, 4)], axis=2))
    def per_state(a):
        return np.asarray(a).reshape(L, 2, NQ, 4, 2, 64).transpose(0, 4, 5, 2, 3, 1).reshape(L, P, 32)
    steps = np.broadcast_to(np.asarray(log_step)[..., None], (L, 2, 32, 64))
    a_par = np.ascontiguousarray(np.stack([per_state(lam_re), per_state(lam_im), per_state(steps)], axis=2))
    a_b = np.zeros((L, NQ, 4, 2, 16, 4, 2, 2, 2, 64), f32)
    a_c = np.zeros((L, NQ, 2, 64, 4, 2, 2, 2, 16), f32)
    for r, (b, c) in enumerate(((b_re, c_re), (b_im, c_im))):
        b = np.asarray(b).reshape(L, 2, NQ, 4, 2, 64, 16)
        c = np.asarray(c).reshape(L, 2, NQ, 4, 2, 16, 64)
        for k in range(4):
            for g in range(2):
                a_b[:, :, k, g, :, k, :, r, g, :] = b[:, :, :, k, g].transpose(0, 2, 4, 1, 3)
                a_c[:, :, g, :, k, :, r, g, :] = c[:, :, :, k, g].transpose(0, 2, 4, 1, 3)
    a_b = a_b.reshape(L * NQ, P, NT * 2 * P)
    a_c = a_c.reshape(L * NQ, P, NT * 2 * 32)

    a_const = np.zeros((P, NCONST), f32)
    a_const[:, 0:P] = np.eye(P)
    a_const[:, P:2 * P] = np.eye(P)[::-1]
    a_const[:, 2 * P:3 * P] = np.arange(P)
    a_const[:, 3 * P:3 * P + 16] = 16 * np.arange(16)
    a_const[:, 3 * P + 16:] = np.arange(16)
    delta = np.arange(TOEP) - (S - 1)
    n = np.abs(delta)
    large = 8 + (np.log(np.maximum(n, 1) / 8) / np.log(1024 / 8) * 8).astype(np.int32)
    bucket = np.where(delta > 0, 16, 0) + np.where(n < 8, n, np.minimum(large, 15))
    count = sum(((n % dil == 0) & (n <= win // 2)).astype(np.int64)
                for win, dil in ((128, 1), (512, 4), (2048, 16)))
    a_rows = np.zeros((33, TOEP), f32)
    a_rows[bucket, np.arange(TOEP)] = 1.0
    a_rows[32] = np.where(count > 0, np.log(np.maximum(count, 1)), -1e30)

    ins = {
        "x_in": np.ascontiguousarray(np.asarray(x).reshape(S, D)), "w_in": a_w_in, "w_out": a_w_out,
        "w_glu": a_w_glu, "w_query": a_w_query, "keys": a_keys, "expert_u": a_u, "expert_v": a_v,
        "rel_bias": np.ascontiguousarray(rel_bias), "gains": a_gain,
        "norm_final": np.ascontiguousarray(norm_final), "ssm_par": a_par, "ssm_b": a_b, "ssm_c": a_c,
        "consts": a_const, "bucket_rows": a_rows,
    }
    nc = bacc.Bacc("TRN2", target_bir_lowering=False, num_devices=1)
    args = [nc.dram_tensor(f"in_{k}", a.shape, mybir.dt.from_np(a.dtype), kind="ExternalInput").ap()
            for k, a in ins.items()]
    args.append(nc.dram_tensor("out_x", (S, D), F32, kind="ExternalOutput").ap())
    encoder(nc, *args)
    r = run_bass_kernel_spmd(nc, [{f"in_{k}": a for k, a in ins.items()}], core_ids=[0])
    return r.results[0]["out_x"].reshape(1, S, D)
```

```python
import concourse.bass as bass
from concourse import mybir
from contextlib import ExitStack

F32 = mybir.dt.float32
F32R = mybir.dt.float32r
U32 = mybir.dt.uint32
ALU = mybir.AluOpType
ACT = mybir.ActivationFunctionType
AX = mybir.AxisListType

P = 128
D = 1024
S = 256
DEPTH = 2
AW = 512
HD = 64
NH = 8
NQ = 4
DC = D // P
TT = S // P
NT = 8
PH = 8
PK = 128
TOPK = 16
EPS = 1e-6
ROUND = 12582912.0
GRID14 = 768.0
TWO_PI_A = 6.28125
TWO_PI_B = 0.0019353071795864769
INV_TWO_PI = 0.15915494309189535
TWO_PI_BELOW = 6.28318501
HALF_PI = 1.5707963267948966
LOWEST = -3.0e38
NCONST = 3 * P + 32
TOEP = 2 * S
EARLY = 32
HOT = 8
assert HOT * PK == D


def encoder(nc, x, w_in, w_out, w_glu, w_query, keys, expert_u, expert_v, rel_bias, gains,
            norm_final, ssm_par, ssm_b, ssm_c, consts, bucket_rows, out):
    ctx = ExitStack()
    with ctx:
        def sb(name, shape, dt=F32):
            return ctx.enter_context(nc.sbuf_tensor(name, shape, dt))

        def sem(name):
            return ctx.enter_context(nc.semaphore(name))

        cst = sb("cst", [P, NCONST])
        ident, antiident, iota = cst[:, 0:P], cst[:, P:2 * P], cst[:, 2 * P:3 * P]
        steps_ab = cst[:, 3 * P:3 * P + 32]
        iota16 = cst[:, 2 * P:2 * P + TOPK]
        gain = sb("gain", [P, 28])
        g_mix, g_ffn, g_cat, d_skip = gain[:, 0:8], gain[:, 8:16], gain[:, 16:24], gain[:, 24:28]
        tiny = sb("tiny", [P, 4])
        eps_c, half_pi_c = tiny[:, 0:1], tiny[:, 1:2]
        fence = sb("fence", [P, 5])
        sel_T = sb("sel_T", [P, 3, S])
        h_hl = sb("h_hl", [P, 2, DC, S], F32R)
        u_hl = [sb(f"u_hl{i}", [P, 2, DC, P], F32R) for i in range(2)]
        v_hl = [sb(f"v_hl{i}", [P, 2, D], F32R) for i in range(2)]
        w_hl = [sb(f"w_hl{i}", [P, 2, S], F32R) for i in range(2)]
        u_raw = [sb(f"u_raw{i}", [P, DC, P]) for i in range(2)]
        v_raw = [sb(f"v_raw{i}", [P, D]) for i in range(2)]
        act_w = sb("act_w", [P, 2, S])
        hot1 = [v_raw[b][:, :].rearrange("p (j n) -> p j n", j=HOT) for b in range(2)]
        hot2 = [u_raw[b][:, :, :] for b in range(2)]

        arena = sb("arena", [P, PK * S])
        gates = arena[:, :].rearrange("p (c t) -> p c t", t=S)
        at = [0]

        def take(words):
            at[0] += words
            assert at[0] <= PK * S
            return arena[:, at[0] - words:at[0]]

        xs_f = take(TT * D)
        xs = xs_f.rearrange("p (a n) -> p a n", a=TT)
        w_slot_f = take(DC * 512)
        w_slot = w_slot_f.rearrange("p (k m n) -> p k m n", k=DC, m=4)
        w_glu_sb = w_slot_f.rearrange("p (k n) -> p k n", k=4)
        slots = take(4 * S)
        uT, uTr, qT, kT = (slots[:, i * S:(i + 1) * S] for i in range(4))
        ssm = slots.rearrange("p (a n) -> p a n", a=TT)
        v_sb = take(TT * P).rearrange("p (a n) -> p a n", a=TT)
        attn = take(TT * AW).rearrange("p (a n) -> p a n", a=TT)
        assert at[0] >= EARLY * S
        hT_f = take(DC * S)
        hT = hT_f.rearrange("p (k t) -> p k t", k=DC)
        mixn = hT_f.rearrange("p (a n) -> p a n", a=TT)
        bias_f = take(NH * 3 * P)
        bias = bias_f.rearrange("p (h n) -> p h n", h=NH)
        big = at[0]
        tab = take(2 * NT * S).rearrange("p (s n t) -> p s n t", s=2, n=NT)
        turn_f = take(2 * 2 * S)
        turn = turn_f.rearrange("p (s r t) -> p s r t", s=2, r=2)
        turn2 = take(2 * 2 * S).rearrange("p (s r t) -> p s r t", s=2, r=2)
        drive = take(2 * 2 * S).rearrange("p (s r t) -> p s r t", s=2, r=2)
        state = take(2 * 2 * S).rearrange("p (s r t) -> p s r t", s=2, r=2)
        outc = take(2 * 2 * S).rearrange("p (s r t) -> p s r t", s=2, r=2)
        outs = take(2 * 2 * S).rearrange("p (s r t) -> p s r t", s=2, r=2)
        w_out_sb = arena[:, big:big + DC * D].rearrange("p (k n) -> p k n", k=DC)
        xn = arena[:, big:big + TT * D].rearrange("p (a n) -> p a n", a=TT)
        b_f = take(NT * 2 * P)
        b_sb = b_f.rearrange("p (n r m) -> p n r m", n=NT, r=2)
        mixT = b_f.rearrange("p (k t) -> p k t", k=DC)
        c_raw = take(NT * 2 * 32).rearrange("p (n r m) -> p n r m", n=NT, r=2)
        c_sb = take(3 * NT * 32).rearrange("p (j n m) -> p j n m", j=3, n=NT)
        probs_f = take(4 * S)
        probs = probs_f.rearrange("p (s t) -> p s t", s=4)
        c_tmp = probs_f.rearrange("p (j n m) -> p j n m", j=4, n=NT)
        angle_t = probs_f.rearrange("p (n j) -> p n j", j=32)
        pT = take(2 * S).rearrange("p (s a t) -> p s a t", s=2, a=TT)
        yT = take(4 * S).rearrange("p (k t) -> p k t", k=4)
        ysum = take(2 * S).rearrange("p (s t) -> p s t", s=2)
        angle = take(NQ * NT * 32).rearrange("p (n j) -> p n j", j=32)
        par = take(3 * 32).rearrange("p (k n) -> p k n", k=3)
        sm = take(24 * 32).rearrange("p (k n) -> p k n", k=24)
        stat = take(32)
        sel0 = at[0]
        wq_slot = bias_f[:, 0:2048].rearrange("p (s k n) -> p s k n", s=2, k=DC)
        key_slot = bias_f[:, 2048:2048 + 2 * P].rearrange("p (s n) -> p s n", s=2)
        at[0] = big

        def again(words):
            return take(words)

        qh = again(S)
        sc = again(2 * TT * PK).rearrange("p (b a n) -> p b a n", b=2, a=TT)
        sc2 = again(2 * TT * PK).rearrange("p (b a n) -> p b a n", b=2, a=TT)
        t16 = again(4 * TOPK).rearrange("p (b a n) -> p b a n", b=2, a=TT)
        i16u = again(4 * TOPK).bitcast(U32).rearrange("p (b a n) -> p b a n", b=2, a=TT)
        i16 = again(4 * TOPK).rearrange("p (b a n) -> p b a n", b=2, a=TT)
        cand = again(TT * S).rearrange("p (a i j) -> p a i j", a=TT, i=TOPK)
        cand2 = again(TT * S).rearrange("p (a n) -> p a n", a=TT)
        top = again(TT * TOPK).rearrange("p (a n) -> p a n", a=TT)
        cu = again(TT * TOPK).bitcast(U32).rearrange("p (a n) -> p a n", a=TT)
        rank_u = again(2 * TT * TOPK).bitcast(U32).rearrange("p (b a n) -> p b a n", b=2, a=TT)
        rank = again(2 * TT * TOPK).rearrange("p (b a n) -> p b a n", b=2, a=TT)
        pick = again(2 * TT * S).rearrange("p (b a i j) -> p b a i j", b=2, a=TT, i=TOPK)
        sel = again(3 * TT * PH * TOPK).rearrange("p (k a h j) -> p k a h j", k=3, a=TT, h=PH)
        gsum = again(TT * PH).rearrange("p (a h) -> p a h", a=TT)
        assert at[0] <= big + DC * D
        xb = xs
        gfin = arena[:, TT * D:TT * D + D]
        rel_sb = arena[0:33, 8192:8192 + NH]
        rows_sb = arena[0:33, 8704:8704 + TOEP]
        toep_sb = arena[0:NH, 9216:9216 + TOEP]

        ps = ctx.enter_context(nc.psum_tensor("ps", [P, 8, 512], F32))

        toep_d = nc.dram_tensor("toep_scratch", [NH, TOEP], F32, kind="Internal")
        x_d = nc.dram_tensor("x_scratch", [P, TT * D], F32, kind="Internal")

        s_const = sem("s_const")
        s_memset = sem("s_memset")
        s_xin = sem("s_xin")
        s_rel = sem("s_rel")
        s_relones = sem("s_relones")
        s_toep_mm = sem("s_toep_mm")
        s_toep_sb = sem("s_toep_sb")
        s_toep_d = sem("s_toep_d")
        s_gain = sem("s_gain")
        s_par = sem("s_par")
        s_bias = sem("s_bias")
        s_layer = sem("s_layer")
        s_rms = sem("s_rms")
        s_rstd = sem("s_rstd")
        s_xn = sem("s_xn")
        s_tr = sem("s_tr")
        s_hT = sem("s_hT")
        s_p1 = sem("s_p1")
        s_p2 = sem("s_p2")
        s_p3 = sem("s_p3")
        s_coef = sem("s_coef")
        s_w = sem("s_w")
        s_bc = sem("s_bc")
        s_proj = sem("s_proj")
        s_u_sb = sem("s_u_sb")
        s_qkv_sb = sem("s_qkv_sb")
        s_turns = sem("s_turns")
        s_tab = sem("s_tab")
        s_c = sem("s_c")
        s_bu = sem("s_bu")
        s_pp = sem("s_pp")
        s_drive = sem("s_drive")
        s_state = sem("s_state")
        s_outs = sem("s_outs")
        s_outc = sem("s_outc")
        s_y = sem("s_y")
        s_ysum = sem("s_ysum")
        s_yT = sem("s_yT")
        s_score = sem("s_score")
        s_max = sem("s_max")
        s_exp = sem("s_exp")
        s_ptr = sem("s_ptr")
        s_pT = sem("s_pT")
        s_pv = sem("s_pv")
        s_attn = sem("s_attn")
        s_wglu = sem("s_wglu")
        s_wout = sem("s_wout")
        s_glu = sem("s_glu")
        s_sig = sem("s_sig")
        s_ssm = sem("s_ssm")
        s_mixn = sem("s_mixn")
        s_mixtr = sem("s_mixtr")
        s_mixT = sem("s_mixT")
        s_wo = sem("s_wo")
        s_x1 = sem("s_x1")
        s_spill = sem("s_spill")
        s_wq = [sem(f"s_wq{i}") for i in range(2)]
        s_q = sem("s_q")
        s_qh = sem("s_qh")
        s_sc = sem("s_sc")
        s_sc_sb = sem("s_sc_sb")
        s_sc_used = sem("s_sc_used")
        s_topd = sem("s_topd")
        s_gexp = sem("s_gexp")
        s_sel = sem("s_sel")
        s_seltr = sem("s_seltr")
        s_selT = sem("s_selT")
        s_hhi = sem("s_hhi")
        s_hlo = sem("s_hlo")
        s_hot1 = sem("s_hot1")
        s_hot2 = sem("s_hot2")
        s_gated = sem("s_gated")
        s_hot_free = sem("s_hot_free")
        s_gmul = sem("s_gmul")
        s_gates = sem("s_gates")
        s_u_ld = [sem(f"s_u_ld{i}") for i in range(2)]
        s_v_ld = [sem(f"s_v_ld{i}") for i in range(2)]
        s_u_hi = sem("s_u_hi")
        s_v_hi = sem("s_v_hi")
        s_u_lo = sem("s_u_lo")
        s_v_lo = sem("s_v_lo")
        s_u_mm = sem("s_u_mm")
        s_v_mm = sem("s_v_mm")
        s_gelu = sem("s_gelu")
        s_wt = sem("s_wt")
        s_xback = sem("s_xback")
        s_gfin = sem("s_gfin")
        s_fin = sem("s_fin")
        s_out = sem("s_out")

        block = ctx.enter_context(nc.Block())

        def col(ap, i, n=1):
            return ap[:, bass.ds(i, n)]

        def over(ap, n):
            return ap.unsqueeze(1).broadcast_to([ap.shape[0], n, ap.shape[1]])

        @block.sync
        def _(sp):
            sp.dma_start(cst[:, :], consts).then_inc(s_const, 16)
            sp.dma_start(xs, x.rearrange("(a p) n -> p a n", p=P)).then_inc(s_xin, 16)
            sp.wait_ge(s_relones, 1)
            sp.dma_start(rel_sb[0:32, :], rel_bias).then_inc(s_rel, 16)
            sp.dma_start(rows_sb, bucket_rows).then_inc(s_rel, 16)
            sp.wait_ge(s_toep_sb, 1)
            sp.dma_start(toep_d.ap(), toep_sb).then_inc(s_toep_d, 16)
            sp.wait_ge(s_toep_d, 16)
            overlap = bass.AP(toep_d, 0, [[1, P], [TOEP, NH], [1, 3 * P]])

            def load_u(l, c, s):
                sp.dma_start(u_raw[s][:, :, :], expert_u[bass.ds(l * PK + c, 1), :, :]
                             .rearrange("o p n -> (o p) n").rearrange("p (k n) -> p k n", k=DC)).then_inc(s_u_ld[s], 16)

            def load_v(l, c, s):
                sp.dma_start(v_raw[s][:, :], expert_v[bass.ds(l * PK + c, 1), :, :]
                             .rearrange("o p n -> (o p) n")).then_inc(s_v_ld[s], 16)

            with sp.Fori(0, DEPTH) as l:
                sp.wait_ge(s_layer, 1 + l)
                sp.dma_start(gain[:, :], gains[bass.ds(l, 1), :, :].rearrange("o p n -> (o p) n"))\
                    .then_inc(s_gain, 16)
                sp.dma_start(par, ssm_par[bass.ds(l, 1), :, :, :].rearrange("o p k n -> (o p) k n"))\
                    .then_inc(s_par, 16)
                sp.dma_start(bias, overlap).then_inc(s_bias, 16)
                for s in range(2):
                    load_u(l, s, s)
                with sp.Fori(0, NQ) as q:
                    it = l * NQ + q
                    sp.wait_ge(s_proj, 1 + it * 3)
                    sp.dma_start(w_slot_f, w_in[bass.ds(it, 1), :, :].rearrange("o p n -> (o p) n"))\
                        .then_inc(s_w, 16)
                    sp.wait_ge(s_bu, 1 + it * NT)
                    sp.dma_start(b_f, ssm_b[bass.ds(it, 1), :, :].rearrange("o p n -> (o p) n"))\
                        .then_inc(s_bc, 16)
                    sp.wait_ge(s_c, 1 + it)
                    sp.dma_start(c_raw, ssm_c[bass.ds(it, 1), :, :].rearrange("o p n -> (o p) n")
                                 .rearrange("p (n r m) -> p n r m", n=NT, r=2)).then_inc(s_bc, 16)
                sp.wait_ge(s_proj, 1 + (l + 1) * 3 * NQ)
                sp.dma_start(w_glu_sb, w_glu[bass.ds(l, 1), :, :].rearrange("o p n -> (o p) n")
                             .rearrange("p (k n) -> p k n", k=4)).then_inc(s_wglu, 16)
                sp.wait_ge(s_y, 1 + (l + 1) * NT * NQ)
                sp.dma_start(w_out_sb, w_out[bass.ds(l, 1), :, :].rearrange("o p n -> (o p) n")
                             .rearrange("p (k n) -> p k n", k=DC)).then_inc(s_wout, 16)
                sp.wait_ge(s_x1, l + 1)
                sp.dma_start(x_d.ap(), xs_f).then_inc(s_spill, 16)

                def load_head(h, s):
                    ih = l * PH + h
                    sp.dma_start(wq_slot[:, s, :, :], w_query[bass.ds(ih, 1), :, :]
                                 .rearrange("o p n -> (o p) n").rearrange("p (k n) -> p k n", k=DC))\
                        .then_inc(s_wq[s], 16)
                    sp.dma_start(key_slot[:, s, :], keys[bass.ds(ih, 1), :, :]
                                 .rearrange("o p n -> (o p) n")).then_inc(s_wq[s], 16)

                def next_u(c, s):
                    sp.wait_ge(s_u_lo, l * PK + c - 1)
                    load_u(l, c, s)

                def next_v(c, s):
                    sp.wait_ge(s_v_lo, l * PK + c - 1)
                    load_v(l, c, s)

                for s in range(2):
                    load_head(s, s)
                with sp.Fori(0, PH // 2 - 1) as hp:
                    for s in range(2):
                        for j in range(4):
                            next_u(hp * 8 + s * 4 + j + 2, j % 2)
                        sp.wait_ge(s_sc, 1 + l * PH + hp * 2 + s + 1)
                        load_head(hp * 2 + s + 2, s)
                for j in range(8):
                    next_u(EARLY - 8 + j + 2, j % 2)
                sp.wait_ge(s_gates, 4 + (l + 1) * (S // 4))
                for s in range(2):
                    load_v(l, s, s)
                with sp.Fori(0, EARLY // 2) as i:
                    for s in range(2):
                        next_v(i * 2 + s + 2, s)
                with sp.Fori(0, (PK - EARLY) // 2 - 1) as i:
                    for s in range(2):
                        next_u(i * 2 + s + EARLY + 2, s)
                        next_v(i * 2 + s + EARLY + 2, s)
                sp.wait_ge(s_wt, (l + 1) * PK)
                sp.dma_start(xs_f, x_d.ap()).then_inc(s_xback, 16)
            sp.wait_ge(s_layer, 1 + DEPTH)
            sp.dma_start(gfin, norm_final.partition_broadcast(P)).then_inc(s_gfin, 16)
            sp.wait_ge(s_fin, 1)
            sp.dma_start(out.rearrange("(a p) n -> p a n", p=P), xn).then_inc(s_out, 16)
            sp.wait_ge(s_out, 16)

        @block.tensor
        def _(pe):
            pe.wait_ge(s_const, 16)
            pe.wait_ge(s_rel, 32)
            pe.matmul(ps[0:NH, 0, :], rel_sb, rows_sb, start=True, stop=True).then_inc(s_toep_mm, 1)

            def transposes(src, sem_done):
                for c in range(DC):
                    for a in range(TT):
                        m = pe.transpose(ps[:, c // 2, (c % 2) * S + a * P:(c % 2) * S + (a + 1) * P],
                                         src[:, a, c * P:(c + 1) * P], ident)
                    if c % 2:
                        m.then_inc(sem_done, 1)

            with pe.Fori(0, DEPTH) as l:
                pe.wait_ge(s_toep_sb, 1)
                pe.wait_ge(s_xn, 2 * l + 1)
                transposes(xn, s_tr)
                with pe.Fori(0, NQ) as q:
                    it = l * NQ + q
                    pe.wait_ge(s_hT, (2 * l + 1) * DC)
                    pe.wait_ge(s_bias, 16 * (l + 1))
                    pe.wait_ge(s_w, 16 * (it + 1))
                    pe.wait_ge(s_attn, 1 + it)
                    pe.wait_ge(s_pT, 1 + it * 2)
                    for kind, bank, o in ((3, 4, 0), (0, 0, 0), (1, 0, S)):
                        for k in range(DC):
                            m = pe.matmul(ps[:, bank, o:o + S], w_slot[:, k, kind, :], hT[:, k, :],
                                          start=(k == 0), stop=(k == DC - 1))
                        if kind != 0:
                            m.then_inc(s_proj, 1)
                    for a in range(TT):
                        for k in range(DC):
                            m = pe.matmul(ps[:, 1, a * P:(a + 1) * P], hT[:, k, a * P:(a + 1) * P],
                                          w_slot[:, k, 2, :], start=(k == 0), stop=(k == DC - 1))
                    m.then_inc(s_proj, 1)

                    def b_product(n):
                        if n < 2:
                            pe.wait_ge(s_pp, 1 + it * NT)
                        else:
                            pe.wait_ge(s_pp, 1 + it * NT + n - 1)
                        for r in range(2):
                            m = pe.matmul(ps[:, 5 + n % 2, r * S:(r + 1) * S], b_sb[:, n, r, :],
                                          uT if n % 2 == 0 else uTr, start=True, stop=True)
                        m.then_inc(s_bu, 1)

                    def c_product(n):
                        pe.wait_ge(s_outc, 1 + it * NT + n + 1)
                        pe.wait_ge(s_outs, it * NT + n + 1)
                        k, o = n // 2, (n % 2) * S
                        terms = ((0, outc[:, n % 2, 0, :]), (1, outs[:, n % 2, 1, :]),
                                 (2, outs[:, n % 2, 0, :]), (2, outc[:, n % 2, 1, :]))
                        for j, (kind, rhs) in enumerate(terms):
                            m = pe.matmul(ps[32 * k:32 * k + 32, 7, o:o + S], c_sb[:, kind, n, :], rhs,
                                          start=(j == 0), stop=(j == 3))
                        m.then_inc(s_y, 1)

                    def scores(head):
                        for a in range(TT):
                            dst = ps[:, 2 + head, a * S:(a + 1) * S]
                            pe.matmul(dst, antiident, bias[:, bass.ds(q * 2 + head, 1), P - a * P:P - a * P + S]
                                      .rearrange("p o n -> p (o n)"), start=True, stop=False)
                            m = pe.matmul(dst, qT[head * HD:(head + 1) * HD, a * P:(a + 1) * P],
                                          kT[head * HD:(head + 1) * HD, :], start=False, stop=True)
                        m.then_inc(s_score, 1)

                    def prob_transposes(head):
                        pe.wait_ge(s_exp, it * 2 + head + 1)
                        for a in range(TT):
                            for b in range(TT):
                                o = a * S + b * P
                                m = pe.transpose(ps[:, 4, o:o + P], probs[:, 2 * head + a, b * P:(b + 1) * P],
                                                 ident)
                        m.then_inc(s_ptr, 1)

                    def values(head):
                        pe.wait_ge(s_pT, 1 + it * 2 + head + 1)
                        for a in range(TT):
                            s = 2 * head + a
                            for b in range(TT):
                                m = pe.matmul(ps[:, 0, s * HD:(s + 1) * HD], pT[:, a, b, :],
                                              v_sb[:, b, head * HD:(head + 1) * HD],
                                              start=(b == 0), stop=(b == TT - 1))
                        if head:
                            m.then_inc(s_pv, 1)

                    pe.wait_ge(s_bc, 32 * (it + 1))
                    pe.wait_ge(s_u_sb, 2 * (it + 1))
                    b_product(0)
                    b_product(1)
                    pe.wait_ge(s_qkv_sb, 3 * (it + 1))
                    pe.wait_ge(s_ysum, 1 + it)
                    pe.wait_ge(s_c, 1 + it + 1)
                    for n in range(NT):
                        if n < 2:
                            scores(n)
                        if n + 2 < NT:
                            b_product(n + 2)
                        c_product(n)
                        if n in (2, 4):
                            prob_transposes(n // 2 - 1)
                        if n in (3, 5):
                            values(n // 2 - 1)

                pe.wait_ge(s_wglu, 16 * (l + 1))
                pe.wait_ge(s_yT, 1 + NQ * (l + 1))
                pe.wait_ge(s_attn, 1 + NQ * (l + 1))
                for a in range(TT):
                    for half in range(2):
                        for k in range(4):
                            m = pe.matmul(ps[:, 2 * a + half, :], yT[:, k, a * P:(a + 1) * P],
                                          w_glu_sb[:, k, half * AW:(half + 1) * AW],
                                          start=(k == 0), stop=(k == 3))
                    m.then_inc(s_glu, 1)
                pe.wait_ge(s_mixn, l + 1)
                transposes(mixn, s_mixtr)
                pe.wait_ge(s_mixT, (l + 1) * DC)
                pe.wait_ge(s_wout, 16 * (l + 1))
                for a in range(TT):
                    for half in range(2):
                        for k in range(DC):
                            m = pe.matmul(ps[:, 4 + 2 * a + half, :], mixT[:, k, a * P:(a + 1) * P],
                                          w_out_sb[:, k, half * 512:(half + 1) * 512],
                                          start=(k == 0), stop=(k == DC - 1))
                        m.then_inc(s_wo, 1)
                pe.wait_ge(s_xn, 2 * l + 2)
                transposes(xn, s_tr)

                def up(c, s):
                    n = l * PK + c
                    pe.wait_ge(s_u_lo, n + 1)
                    pe.wait_ge(s_gelu, 2 + n - 1)
                    terms = ((0, 0), (0, 1), (1, 0))
                    for k in range(DC):
                        for j, (wp, hp_) in enumerate(terms):
                            m = pe.matmul(ps[:, 4 + s, 0:S], u_hl[s][:, wp, k, :], h_hl[:, hp_, k, :],
                                          start=(k == 0 and j == 0), stop=(k == DC - 1 and j == 2))
                    m.then_inc(s_u_mm, 1)

                def down(c, s, first=False, last=False):
                    n = l * PK + c
                    pe.wait_ge(s_v_lo, n + 1)
                    pe.wait_ge(s_wt, n + 1)
                    terms = ((0, 0), (0, 1), (1, 0))
                    for a in range(TT):
                        for j, (wp, vp) in enumerate(terms):
                            for half in range(2):
                                m = pe.matmul(ps[:, 2 * a + half, :], w_hl[s][:, wp, a * P:(a + 1) * P],
                                              v_hl[s][:, vp, half * 512:(half + 1) * 512],
                                              start=(first and j == 0), stop=(last and j == 2))
                    m.then_inc(s_v_mm, 1)

                with pe.Fori(0, PH // 2) as hp:
                    for s in range(2):
                        ih = l * PH + hp * 2 + s
                        if s == 0:
                            pe.wait_ge(s_hT, (2 * l + 2) * DC)
                        pe.wait_ge(s_wq[s], 32 * (l * (PH // 2) + hp + 1))
                        for k in range(DC):
                            m = pe.matmul(ps[:, 6, 0:S], wq_slot[:, s, k, :], hT[:, k, :],
                                          start=(k == 0), stop=(k == DC - 1))
                        m.then_inc(s_q, 1)
                        pe.wait_ge(s_hlo, l + 1)
                        for j in range(2):
                            up(hp * 8 + s * 4 + j, j)
                        pe.wait_ge(s_qh, ih + 1)
                        pe.wait_ge(s_sc_sb, 1 + ih)
                        for half in range(2):
                            for a in range(TT):
                                m = pe.matmul(ps[:, half, a * PK:(a + 1) * PK],
                                              qh[half * 64:half * 64 + 64, a * P:(a + 1) * P],
                                              key_slot[half * 64:half * 64 + 64, s, :], start=True, stop=True)
                        m.then_inc(s_sc, 1)
                        for j in range(2):
                            up(hp * 8 + s * 4 + j + 2, j)
                pe.wait_ge(s_sel, l + 1)
                for k in range(3):
                    for a in range(TT):
                        m = pe.transpose(ps[:, 2 + k // 2, (k % 2) * S + a * P:(k % 2) * S + (a + 1) * P],
                                         sel[:, k, a, :, :].rearrange("p h j -> p (h j)"), ident)
                m.then_inc(s_seltr, 1)
                with pe.Fori(0, S // 16) as i:
                    pe.wait_ge(s_selT, l + 1)
                    for j in range(16):
                        if j % 4 == 0:
                            pe.wait_ge(s_gates, (l * (S // 16) + i) * 4 + j // 4 + 1)
                        if j % HOT == 0:
                            batch = (l * (S // 16) + i) * 2 + j // HOT
                            pe.wait_ge(s_hot2, batch + 1)
                            pe.wait_ge(s_gated, batch + 1)
                        m = pe.matmul(ps[:, j // 4, (j % 4) * P:(j % 4 + 1) * P], hot2[j // HOT][:, j % HOT, :],
                                      hot1[j // HOT][:, j % HOT, :], start=True, stop=True)
                        if j % 4 == 3:
                            m.then_inc(s_hot_free, 1)

                down(0, 0, first=True)
                down(1, 1)
                with pe.Fori(0, EARLY // 2 - 1) as i:
                    for s in range(2):
                        down(i * 2 + s + 2, s)
                up(EARLY, 0)
                with pe.Fori(0, (PK - EARLY) // 2 - 1) as i:
                    up(i * 2 + EARLY + 1, 1)
                    down(i * 2 + EARLY, 0)
                    up(i * 2 + EARLY + 2, 0)
                    down(i * 2 + EARLY + 1, 1)
                up(PK - 1, 1)
                down(PK - 2, 0)
                down(PK - 1, 1, last=True)

        @block.scalar
        def _(act):
            def fenced():
                act.activation(fence[0:1, 0:1], fence[0:1, 1:2], ACT.Copy)

            act.wait_ge(s_toep_mm, 1)
            act.activation(toep_sb, ps[0:NH, 0, :], ACT.Copy).then_inc(s_toep_sb, 1)
            act.wait_ge(s_memset, 1)

            def squares(src, n, j, scratch):
                return act.activation(scratch[:, 0:n], src, ACT.Square, accum_out=stat[:, j:j + 1])

            with act.Fori(0, DEPTH) as l:
                act.wait_ge(s_xin, 16)
                act.wait_ge(s_layer, 1 + l)
                for a in range(TT):
                    if a:
                        act.drain()
                    squares(xs[:, a, :], D, a, turn_f)
                act.drain()
                act.activation(stat[:, 2:4], stat[:, 0:2], ACT.Sqrt, bias=eps_c, scale=1.0 / D).then_inc(s_rms, 1)
                act.wait_ge(s_par, 16 * (l + 1))
                act.activation(sm[:, 0, :], par[:, 2, :], ACT.Exp).then_inc(s_p1, 1)
                act.wait_ge(s_p2, l + 1)
                act.activation(sm[:, 3, :], sm[:, 2, :], ACT.Exp)
                act.activation(sm[:, 9, :], sm[:, 7, :], ACT.Sin, scale=TWO_PI_BELOW)
                act.activation(sm[:, 8, :], sm[:, 7, :], ACT.Abs)
                act.drain()
                act.activation(sm[:, 10, :], sm[:, 8, :], ACT.Sin, scale=-TWO_PI_BELOW, bias=half_pi_c)\
                    .then_inc(s_p3, 1)
                act.wait_ge(s_gain, 16 * (l + 1))
                for c in range(DC):
                    act.wait_ge(s_tr, l * DC + c // 2 + 1)
                    act.activation(hT[:, c, :], ps[:, c // 2, (c % 2) * S:(c % 2 + 1) * S], ACT.Copy,
                                   scale=g_mix[:, c:c + 1]).then_inc(s_hT, 1)
                with act.Fori(0, NQ) as q:
                    it = l * NQ + q
                    act.wait_ge(s_turns, it + 1)
                    act.activation(tab[:, 1, :, :], tab[:, 0, :, :], ACT.Abs)
                    act.drain()
                    act.activation(tab[:, 0, :, :], tab[:, 0, :, :], ACT.Sin, scale=TWO_PI_BELOW)
                    act.activation(tab[:, 1, :, :], tab[:, 1, :, :], ACT.Sin, scale=-TWO_PI_BELOW,
                                   bias=half_pi_c).then_inc(s_tab, 1)
                    act.wait_ge(s_proj, 1 + it * 3 + 1)
                    act.wait_ge(s_ysum, 1 + it)
                    act.activation(uT, ps[:, 4, 0:S], ACT.Copy).then_inc(s_u_sb, 1)
                    act.activation(uTr, ps[:, 4, 0:S][:, ::-1], ACT.Copy).then_inc(s_u_sb, 1)
                    act.wait_ge(s_proj, 1 + it * 3 + 2)
                    act.activation(qT, ps[:, 0, 0:S], ACT.Copy, scale=HD ** -0.5).then_inc(s_qkv_sb, 1)
                    act.activation(kT, ps[:, 0, S:2 * S], ACT.Copy).then_inc(s_qkv_sb, 1)
                    act.wait_ge(s_proj, 1 + it * 3 + 3)
                    act.activation(v_sb, ps[:, 1, 0:S].rearrange("p (a n) -> p a n", a=TT), ACT.Copy)\
                        .then_inc(s_qkv_sb, 1)
                    for head in range(2):
                        act.wait_ge(s_max, it * 2 + head + 1)
                        for a in range(TT):
                            s = 2 * head + a
                            m = act.activation(probs[:, s, :], ps[:, 2 + head, a * S:(a + 1) * S], ACT.Exp,
                                               bias=stat[:, 8 + s:9 + s], accum_out=stat[:, 12 + s:13 + s])
                        m.then_inc(s_exp, 1)
                    for head in range(2):
                        act.wait_ge(s_ptr, 1 + it * 2 + head + 1)
                        act.activation(pT, ps[:, 4, :].rearrange("p (s a n) -> p s a n", s=2, a=TT), ACT.Copy)\
                            .then_inc(s_pT, 1)
                    act.drain()
                    act.wait_ge(s_ysum, 1 + it + 1)
                    fenced()
                    act.activation(yT[:, bass.ds(q, 1), :].rearrange("p o n -> p (o n)"), ysum[:, 1, :],
                                   ACT.Gelu).then_inc(s_yT, 1)

                for a in range(TT):
                    act.wait_ge(s_glu, l * TT + a + 1)
                    act.activation(ssm[:, a, :], ps[:, 2 * a + 1, :], ACT.Sigmoid).then_inc(s_sig, 1)
                act.wait_ge(s_attn, 1 + NQ * (l + 1))
                for a in range(TT):
                    squares(attn[:, a, :], AW, 16 + a, probs_f[:, a * AW:(a + 1) * AW])
                act.drain()
                for a in range(TT):
                    act.wait_ge(s_ssm, l * TT + a + 1)
                    squares(ssm[:, a, :], AW, 18 + a, probs_f[:, a * AW:(a + 1) * AW])
                act.drain()
                act.activation(stat[:, 20:24], stat[:, 16:20], ACT.Sqrt, bias=eps_c, scale=1.0 / AW)\
                    .then_inc(s_rms, 1)
                for c in range(DC):
                    act.wait_ge(s_mixtr, l * (DC // 2) + c // 2 + 1)
                    act.activation(mixT[:, c, :], ps[:, c // 2, (c % 2) * S:(c % 2 + 1) * S], ACT.Copy,
                                   scale=g_cat[:, c:c + 1]).then_inc(s_mixT, 1)
                act.wait_ge(s_x1, l + 1)
                for a in range(TT):
                    if a:
                        act.drain()
                    squares(xs[:, a, :], D, a, probs_f)
                act.drain()
                act.activation(stat[:, 2:4], stat[:, 0:2], ACT.Sqrt, bias=eps_c, scale=1.0 / D).then_inc(s_rms, 1)
                for c in range(DC):
                    act.wait_ge(s_tr, l * DC + DC // 2 + c // 2 + 1)
                    act.activation(hT[:, c, :], ps[:, c // 2, (c % 2) * S:(c % 2 + 1) * S], ACT.Copy,
                                   scale=g_ffn[:, c:c + 1]).then_inc(s_hT, 1)
                act.drain()
                act.activation(h_hl[:, 0, :, :], hT, ACT.Copy).then_inc(s_hhi, 1)

                def high_u(c, s, pair):
                    act.wait_ge(s_u_ld[s], 16 * (l * (PK // 2) + pair + 1))
                    act.wait_ge(s_u_mm, 2 + l * PK + c - 1)
                    act.activation(u_hl[s][:, 0, :, :], u_raw[s][:, :, :], ACT.Copy).then_inc(s_u_hi, 1)

                def high_v(c, s, pair):
                    act.wait_ge(s_v_ld[s], 16 * (l * (PK // 2) + pair + 1))
                    act.wait_ge(s_v_mm, 2 + l * PK + c - 1)
                    act.activation(v_hl[s][:, 0, :], v_raw[s][:, :], ACT.Copy).then_inc(s_v_hi, 1)

                def gelu_early(c, s):
                    act.drain()
                    act.wait_ge(s_u_mm, 2 + l * PK + c + 1)
                    fenced()
                    act.activation(gates[:, bass.ds(c, 1), :].rearrange("p o t -> p (o t)"), ps[:, 4 + s, 0:S],
                                   ACT.Gelu).then_inc(s_gelu, 1)

                def gelu(c, s):
                    n = l * PK + c
                    act.wait_ge(s_u_mm, 2 + n + 1)
                    act.wait_ge(s_wt, n - 1)
                    act.activation(act_w[:, s, :], ps[:, 4 + s, 0:S], ACT.Gelu).then_inc(s_gelu, 1)

                high_u(0, 0, 0)
                high_u(1, 1, 0)
                with act.Fori(0, PH // 2) as hp:
                    for s in range(2):
                        ih = l * PH + hp * 2 + s
                        if s == 0:
                            act.wait_ge(s_spill, 16 * (l + 1))
                        act.wait_ge(s_q, ih + 1)
                        act.activation(qh, ps[:, 6, 0:S], ACT.Copy).then_inc(s_qh, 1)
                        for j in range(2):
                            c = hp * 8 + s * 4 + j
                            gelu_early(c, j)
                            high_u(c + 2, j, hp * 4 + s * 2 + 1)
                        act.wait_ge(s_sc, 1 + ih + 1)
                        act.wait_ge(s_sc_used, 1 + ih)
                        act.activation(sc, ps[:, 0:2, 0:S].rearrange("p b (a n) -> p b a n", a=TT), ACT.Copy)\
                            .then_inc(s_sc_sb, 1)
                        for j in range(2):
                            c = hp * 8 + s * 4 + j + 2
                            gelu_early(c, j)
                            high_u(c + 2, j, hp * 4 + s * 2 + 2)
                act.wait_ge(s_topd, l + 1)
                act.activation(sel[:, 2, :, :, :], sel[:, 2, :, :, :], ACT.Exp).then_inc(s_gexp, 1)
                act.wait_ge(s_seltr, l + 1)
                act.activation(sel_T[:, 0:2, :], ps[:, 2, :].rearrange("p (k t) -> p k t", k=2), ACT.Copy)
                act.activation(sel_T[:, 2, :], ps[:, 3, 0:S], ACT.Copy).then_inc(s_selT, 1)
                with act.Fori(0, S // 16) as i:
                    for j in range(4):
                        act.drain()
                        act.wait_ge(s_gmul, (l * (S // 16) + i) * 4 + j + 1)
                        fenced()
                        act.activation(gates[:, EARLY:PK, bass.ds(i * 16 + j * 4, 4)],
                                       ps[:, j, :].rearrange("p (t c) -> p c t", c=PK)[:, EARLY:PK, :],
                                       ACT.Copy).then_inc(s_gates, 1)

                high_v(0, 0, 0)
                high_v(1, 1, 0)
                with act.Fori(0, EARLY // 2 - 1) as i:
                    for s in range(2):
                        high_v(i * 2 + s + 2, s, i + 1)
                high_v(EARLY, 0, EARLY // 2)
                with act.Fori(0, (PK - EARLY) // 2 - 1) as i:
                    for s in range(2):
                        c = i * 2 + s + EARLY
                        gelu(c, s)
                        high_u(c + 2, s, i + EARLY // 2 + 1)
                        high_v(c + 1, 1 - s, i + EARLY // 2 + s)
                gelu(PK - 2, 0)
                high_v(PK - 1, 1, PK // 2 - 1)
                gelu(PK - 1, 1)

            act.wait_ge(s_layer, 1 + DEPTH)
            for a in range(TT):
                if a:
                    act.drain()
                squares(xs[:, a, :], D, a, turn_f)
            act.drain()
            act.activation(stat[:, 2:4], stat[:, 0:2], ACT.Sqrt, bias=eps_c, scale=1.0 / D).then_inc(s_rms, 1)

        @block.vector
        def _(dve):
            dve.memset(rel_sb, 1.0).then_inc(s_relones, 1)
            dve.memset(fence[:, :], 0.0)
            dve.memset(eps_c, EPS)
            dve.memset(half_pi_c, HALF_PI).then_inc(s_memset, 1)
            dve.sem_inc(s_hot_free, 4)
            dve.sem_inc(s_gates, 4)
            for counter in (s_u_mm, s_v_mm, s_gelu):
                dve.sem_inc(counter, 2)
            for counter in (s_layer, s_proj, s_bu, s_c, s_attn, s_pT, s_pp, s_drive, s_y, s_state, s_outc, s_ysum, s_yT, s_ptr, s_sc, s_sc_sb, s_sc_used):
                dve.sem_inc(counter, 1)

            def tt(o, a, b, op):
                return dve.tensor_tensor(o, a, b, op)

            with dve.Fori(0, DEPTH) as l:
                dve.wait_ge(s_rms, 3 * l + 1)
                dve.reciprocal(stat[:, 4:6], stat[:, 2:4])
                dve.drain()
                for a in range(TT):
                    m = dve.tensor_scalar(xn[:, a, :], xs[:, a, :], stat[:, 4 + a:5 + a], None, ALU.mult)
                m.then_inc(s_xn, 1)

                lr, li, step = par[:, 0, :], par[:, 1, :], sm[:, 0, :]
                theta, sig, mag, turns, whole, phi = (sm[:, i, :] for i in (1, 2, 3, 4, 5, 7))
                dve.wait_ge(s_p1, l + 1)
                tt(theta, li, step, ALU.mult)
                tt(sig, lr, step, ALU.mult)
                dve.drain()
                dve.tensor_scalar(turns, theta, INV_TWO_PI, None, ALU.mult)
                dve.drain()
                dve.tensor_scalar(whole, turns, ROUND, ROUND, ALU.add, ALU.subtract)
                dve.drain()
                dve.scalar_tensor_tensor(theta, whole, -TWO_PI_A, theta, ALU.mult, ALU.add)
                dve.drain()
                dve.scalar_tensor_tensor(theta, whole, -TWO_PI_B, theta, ALU.mult, ALU.add)
                dve.drain()
                dve.tensor_scalar(sm[:, 6, :], theta, INV_TWO_PI, None, ALU.mult)
                dve.drain()
                dve.tensor_scalar(sm[:, 6, :], sm[:, 6, :], 0.5, -0.5, ALU.min, ALU.max)
                dve.drain()
                dve.tensor_copy(phi, sm[:, 6, :]).then_inc(s_p2, 1)
                dve.tensor_scalar(sm[:, 11, :], sm[:, 6, :], GRID14, GRID14, ALU.add, ALU.subtract)
                dve.drain()
                dve.tensor_tensor(sm[:, 12, :], sm[:, 6, :], sm[:, 11, :], ALU.subtract)
                dve.drain()
                n_all = NQ * NT

                def wide(i):
                    return sm[:, i, :].unsqueeze(2).broadcast_to([P, n_all, 32])

                ab = over(steps_ab, n_all)
                tt(angle, wide(11), ab, ALU.mult)
                dve.drain()
                dve.tensor_scalar(angle_t, angle, ROUND, ROUND, ALU.add, ALU.subtract)
                dve.drain()
                tt(angle, angle, angle_t, ALU.subtract)
                dve.drain()
                tt(angle_t, wide(12), ab, ALU.mult)
                dve.drain()
                tt(angle, angle, angle_t, ALU.add)
                dve.wait_ge(s_p3, l + 1)
                sin, cos = sm[:, 9, :], sm[:, 10, :]
                re, im, den, tmp = (sm[:, i, :] for i in (13, 14, 15, 16))
                f_re, f_im, nf_re, nf_im = (sm[:, i, :] for i in (17, 18, 19, 20))
                tt(re, mag, cos, ALU.mult)
                tt(im, mag, sin, ALU.mult)
                tt(den, lr, lr, ALU.mult)
                tt(tmp, li, li, ALU.mult)
                dve.drain()
                dve.tensor_scalar(re, re, -1.0, None, ALU.add)
                tt(den, den, tmp, ALU.add)
                dve.drain()
                dve.reciprocal(den, den)
                tt(f_re, re, lr, ALU.mult)
                tt(tmp, im, li, ALU.mult)
                dve.drain()
                tt(f_re, f_re, tmp, ALU.add)
                tt(f_im, im, lr, ALU.mult)
                dve.drain()
                tt(tmp, re, li, ALU.mult)
                dve.drain()
                tt(f_im, f_im, tmp, ALU.subtract)
                tt(f_re, f_re, den, ALU.mult)
                dve.drain()
                tt(f_im, f_im, den, ALU.mult)
                dve.tensor_scalar(nf_re, f_re, -1.0, None, ALU.mult)
                dve.drain()
                dve.tensor_scalar(nf_im, f_im, -1.0, None, ALU.mult).then_inc(s_coef, 1)

                with dve.Fori(0, NQ) as q:
                    it = l * NQ + q
                    a_part = angle[:, bass.ds(q * NT, NT), 0:16].unsqueeze(3).broadcast_to([P, NT, 16, 16])
                    b_part = angle[:, bass.ds(q * NT, NT), 16:32].unsqueeze(2).broadcast_to([P, NT, 16, 16])
                    t0 = tab[:, 0, :, :].rearrange("p n (a b) -> p n a b", a=16)
                    dve.wait_ge(s_outc, 1 + it * NT)
                    dve.wait_ge(s_tr, l * DC + DC // 2)
                    tt(t0, a_part, b_part, ALU.add)
                    dve.drain()
                    dve.tensor_scalar(tab[:, 1, :, :], tab[:, 0, :, :], ROUND, ROUND, ALU.add, ALU.subtract)
                    dve.drain()
                    tt(tab[:, 0, :, :], tab[:, 0, :, :], tab[:, 1, :, :], ALU.subtract).then_inc(s_turns, 1)
                    dve.wait_ge(s_tab, it + 1)

                    def two(j, n):
                        return over(tab[:, j, n, :], 2)

                    def turn_in(n):
                        s = n % 2
                        dve.wait_ge(s_bu, 1 + it * NT + n + 1)
                        if n < 2:
                            dve.wait_ge(s_drive, 1 + it * NT)
                        else:
                            dve.wait_ge(s_drive, 1 + it * NT + n - 1)
                        src = ps[:, 5 + s, :].rearrange("p (r t) -> p r t", r=2)
                        tt(turn[:, s, :, :], src, two(1, n), ALU.mult)
                        tt(turn2[:, s, :, :], src, two(0, n), ALU.mult).then_inc(s_pp, 1)

                    def scan(n):
                        s = n % 2
                        dve.wait_ge(s_drive, 1 + it * NT + n + 1)
                        if n < 2:
                            dve.wait_ge(s_y, 1 + it * NT)
                        else:
                            dve.wait_ge(s_y, 1 + it * NT + n - 1)
                        r_all = col(mag, q * NT + n).broadcast_to([P, S])
                        for r in range(2):
                            dve.tensor_tensor_scan(state[:, s, r, :], r_all, drive[:, s, r, :], 0.0,
                                                   ALU.mult, ALU.add).then_inc(s_state, 1)
                        dve.wait_ge(s_state, 1 + 2 * (it * NT + n + 1))
                        tt(outs[:, s, :, :], state[:, s, :, :], two(0, n), ALU.mult).then_inc(s_outs, 1)

                    def row_max(head):
                        dve.wait_ge(s_score, it * 2 + head + 1)
                        dve.tensor_reduce(stat[:, 8 + 2 * head:10 + 2 * head],
                                          ps[:, 2 + head, :].rearrange("p (a n) -> p a n", a=TT), AX.X, ALU.max,
                                          negate=True).then_inc(s_max, 1)

                    def attn_out():
                        dve.wait_ge(s_pv, it + 1)
                        dve.reciprocal(stat[:, 24:28], stat[:, 12:16])
                        dve.drain()
                        for s in range(4):
                            m = dve.tensor_scalar(attn[:, s % 2, bass.ds((q * 2 + s // 2) * HD, HD)],
                                                  ps[:, 0, s * HD:(s + 1) * HD], stat[:, 24 + s:25 + s], None,
                                                  ALU.mult)
                        m.then_inc(s_attn, 1)

                    turn_in(0)
                    for n in range(NT):
                        if n + 1 < NT:
                            turn_in(n + 1)
                        if n in (1, 2):
                            row_max(n - 1)
                        scan(n)
                        if n == 6:
                            attn_out()
                    dve.wait_ge(s_y, 1 + (it + 1) * NT)
                    dve.scalar_tensor_tensor(ysum[:, 0, :], uT, col(d_skip, q), ps[:, 7, 0:S], ALU.mult, ALU.add)
                    dve.drain()
                    dve.wait_ge(s_yT, 1 + it)
                    tt(ysum[:, 1, :], ysum[:, 0, :], ps[:, 7, S:2 * S][:, ::-1], ALU.add).then_inc(s_ysum, 1)

                for a in range(TT):
                    dve.wait_ge(s_sig, l * TT + a + 1)
                    tt(ssm[:, a, :], ps[:, 2 * a, :], ssm[:, a, :], ALU.mult).then_inc(s_ssm, 1)
                dve.wait_ge(s_rms, 3 * l + 2)
                dve.reciprocal(stat[:, 20:24], stat[:, 20:24])
                dve.drain()
                for a in range(TT):
                    dve.tensor_scalar(mixn[:, a, 0:AW], attn[:, a, :], stat[:, 20 + a:21 + a], None, ALU.mult)
                    m = dve.tensor_scalar(mixn[:, a, AW:D], ssm[:, a, :], stat[:, 22 + a:23 + a], None, ALU.mult)
                m.then_inc(s_mixn, 1)
                for a in range(TT):
                    for half in range(2):
                        dve.wait_ge(s_wo, 4 * l + 2 * a + half + 1)
                        o = xs[:, a, half * 512:(half + 1) * 512]
                        m = tt(o, o, ps[:, 4 + 2 * a + half, :], ALU.add)
                m.then_inc(s_x1, 1)
                dve.wait_ge(s_rms, 3 * l + 3)
                dve.reciprocal(stat[:, 4:6], stat[:, 2:4])
                dve.drain()
                for a in range(TT):
                    m = dve.tensor_scalar(xn[:, a, :], xs[:, a, :], stat[:, 4 + a:5 + a], None, ALU.mult)
                m.then_inc(s_xn, 1)
                dve.wait_ge(s_hhi, l + 1)
                tt(h_hl[:, 1, :, :], hT, h_hl[:, 0, :, :].bitcast(F32), ALU.subtract).then_inc(s_hlo, 1)

                def top16(src, spare, vals, idx):
                    for a, b, v, i in zip(src, spare, vals, idx):
                        dve.max(v[:, 0:8], a)
                    dve.drain()
                    for a, b, v, i in zip(src, spare, vals, idx):
                        dve.match_replace(b, v[:, 0:8], a, LOWEST)
                        dve.max_index(i[:, 0:8], v[:, 0:8], a)
                    dve.drain()
                    for a, b, v, i in zip(src, spare, vals, idx):
                        dve.max(v[:, 8:16], b)
                    dve.drain()
                    for a, b, v, i in zip(src, spare, vals, idx):
                        m = dve.max_index(i[:, 8:16], v[:, 8:16], b)
                    return m

                with dve.Fori(0, PH) as h:
                    ih = l * PH + h
                    dve.wait_ge(s_sc_sb, 1 + ih + 1)
                    dve.memset(fence[:, 2:3], 0.0)
                    pairs = [(b, a) for b in range(2) for a in range(TT)]
                    top16([sc[:, b, a, :] for b, a in pairs], [sc2[:, b, a, :] for b, a in pairs],
                          [t16[:, b, a, :] for b, a in pairs], [i16u[:, b, a, :] for b, a in pairs])\
                        .then_inc(s_sc_used, 1)
                    dve.drain()
                    dve.tensor_copy(i16, i16u)
                    tt(cand, t16[:, 0, :, :].unsqueeze(3).broadcast_to([P, TT, 16, 16]),
                       t16[:, 1, :, :].unsqueeze(2).broadcast_to([P, TT, 16, 16]), ALU.add)
                    dve.drain()
                    cf = [cand[:, a, :, :].rearrange("p i j -> p (i j)") for a in range(TT)]
                    top16(cf, [cand2[:, a, :] for a in range(TT)], [top[:, a, :] for a in range(TT)],
                          [cu[:, a, :] for a in range(TT)])
                    dve.drain()
                    dve.tensor_scalar(rank_u[:, 0, :, :], cu, 4, None, ALU.logical_shift_right)
                    dve.tensor_scalar(rank_u[:, 1, :, :], cu, 15, None, ALU.bitwise_and)
                    tt(sel[:, 2, :, bass.ds(h, 1), :].rearrange("p a o j -> p a (o j)"), top,
                       top[:, :, 0:1].broadcast_to([P, TT, TOPK]), ALU.subtract)
                    dve.drain()
                    dve.tensor_copy(rank, rank_u)
                    dve.drain()
                    for b in range(2):
                        for a in range(TT):
                            tt(pick[:, b, a, :, :], rank[:, b, a, :].unsqueeze(2).broadcast_to([P, 16, 16]),
                               over(iota16, 16), ALU.is_equal)
                    dve.drain()
                    for b in range(2):
                        for a in range(TT):
                            tt(pick[:, b, a, :, :], pick[:, b, a, :, :], over(i16[:, b, a, :], 16), ALU.mult)
                    dve.drain()
                    for b in range(2):
                        dve.tensor_reduce(sel[:, b, :, bass.ds(h, 1), :].rearrange("p a o j -> p a (o j)"),
                                          pick[:, b, :, :, :], AX.X, ALU.add)
                    dve.drain()
                dve.memset(fence[:, 2:3], 0.0).then_inc(s_topd, 1)
                dve.wait_ge(s_gexp, l + 1)
                dve.tensor_reduce(gsum, sel[:, 2, :, :, :], AX.X, ALU.add)
                dve.drain()
                dve.reciprocal(gsum, gsum)
                dve.drain()
                tt(sel[:, 2, :, :, :], sel[:, 2, :, :, :], gsum.unsqueeze(3).broadcast_to([P, TT, PH, TOPK]),
                   ALU.mult).then_inc(s_sel, 1)

                def hot_rows(i, b):
                    n = (l * (S // 16) + i) * 2 + b
                    t = i * 16 + b * HOT
                    for j, (rows, done) in enumerate(((hot1, s_hot1), (hot2, s_hot2))):
                        dve.wait_ge(s_hot_free, 2 * n + 2)
                        tt(rows[b], over(iota, HOT),
                           sel_T[:, j, bass.ds(t, HOT)].unsqueeze(2).broadcast_to([P, HOT, PK]),
                           ALU.is_equal).then_inc(done, 1)

                def gate_early(i, b):
                    for g in (2 * b, 2 * b + 1):
                        dve.wait_ge(s_hot_free, 4 + (l * (S // 16) + i) * 4 + g + 1)
                        place = gates[:, 0:EARLY, bass.ds(i * 16 + g * 4, 4)]
                        tt(place, place, ps[:, g, :].rearrange("p (t c) -> p c t", c=PK)[:, 0:EARLY, :],
                           ALU.mult).then_inc(s_gmul, 1)

                dve.wait_ge(s_selT, l + 1)
                dve.memset(fence[:, 2:3], 0.0)
                dve.wait_ge(s_u_lo, l * PK + EARLY + 2)
                dve.wait_ge(s_gelu, 2 + l * PK + EARLY)
                hot_rows(0, 0)
                with dve.Fori(0, S // 16 - 1) as i:
                    hot_rows(i, 1)
                    gate_early(i, 0)
                    hot_rows(i + 1, 0)
                    gate_early(i, 1)
                hot_rows(S // 16 - 1, 1)
                gate_early(S // 16 - 1, 0)
                gate_early(S // 16 - 1, 1)

                def low_v(c, s):
                    dve.wait_ge(s_v_hi, l * PK + c + 1)
                    tt(v_hl[s][:, 1, :], v_raw[s][:, :], v_hl[s][:, 0, :].bitcast(F32), ALU.subtract)\
                        .then_inc(s_v_lo, 1)

                def weights_early(c, s):
                    dve.wait_ge(s_v_mm, 2 + l * PK + c - 1)
                    g = gates[:, bass.ds(c, 1), :].rearrange("p o t -> p (o t)")
                    dve.tensor_scalar(w_hl[s][:, 0, :], g, 1.0, None, ALU.mult)
                    dve.drain()
                    tt(w_hl[s][:, 1, :], g, w_hl[s][:, 0, :].bitcast(F32), ALU.subtract).then_inc(s_wt, 1)

                def weights(c, s):
                    n = l * PK + c
                    dve.wait_ge(s_gelu, 2 + n + 1)
                    dve.wait_ge(s_v_mm, 2 + n - 1)
                    g = gates[:, bass.ds(c, 1), :].rearrange("p o t -> p (o t)")
                    tt(w_hl[s][:, 0, :], act_w[:, s, :], g, ALU.mult)
                    tt(act_w[:, s, :], act_w[:, s, :], g, ALU.mult)
                    dve.drain()
                    tt(w_hl[s][:, 1, :], act_w[:, s, :], w_hl[s][:, 0, :].bitcast(F32), ALU.subtract)\
                        .then_inc(s_wt, 1)

                dve.drain()
                with dve.Fori(0, EARLY // 2) as i:
                    for s in range(2):
                        weights_early(i * 2 + s, s)
                        low_v(i * 2 + s, s)
                low_v(EARLY, 0)
                with dve.Fori(0, (PK - EARLY) // 2 - 1) as i:
                    dve.wait_ge(s_gates, 4 + (l + 1) * (S // 4))
                    for s in range(2):
                        c = i * 2 + s + EARLY
                        weights(c, s)
                        low_v(c + 1, 1 - s)
                weights(PK - 2, 0)
                low_v(PK - 1, 1)
                weights(PK - 1, 1)
                dve.wait_ge(s_v_mm, 2 + (l + 1) * PK)
                dve.wait_ge(s_xback, 16 * (l + 1))
                for a in range(TT):
                    for half in range(2):
                        o = xs[:, a, half * 512:(half + 1) * 512]
                        m = tt(o, o, ps[:, 2 * a + half, :], ALU.add)
                m.then_inc(s_layer, 1)

            dve.wait_ge(s_rms, 3 * DEPTH + 1)
            dve.reciprocal(stat[:, 4:6], stat[:, 2:4])
            dve.wait_ge(s_gfin, 16)
            dve.drain()
            for a in range(TT):
                m = dve.scalar_tensor_tensor(xn[:, a, :], xs[:, a, :], stat[:, 4 + a:5 + a], gfin,
                                             ALU.mult, ALU.mult)
            m.then_inc(s_fin, 1)

        @block.gpsimd
        def _(pool):
            def tt(o, a, b, op):
                return pool.tensor_tensor(o, a, b, op)

            def low_u(l, c, s):
                pool.wait_ge(s_u_hi, l * PK + c + 1)
                tt(u_hl[s][:, 1, :, :], u_raw[s][:, :, :], u_hl[s][:, 0, :, :].bitcast(F32), ALU.subtract)\
                    .then_inc(s_u_lo, 1)

            with pool.Fori(0, DEPTH) as l:
                with pool.Fori(0, NQ) as q:
                    it = l * NQ + q

                    def f(i):
                        return sm[:, i, bass.ds(q * NT, NT)].unsqueeze(2).broadcast_to([P, NT, 32])

                    pool.wait_ge(s_coef, l + 1)
                    pool.wait_ge(s_bc, 32 * (it + 1))
                    cre, cim = c_raw[:, :, 0, :], c_raw[:, :, 1, :]
                    pool.wait_ge(s_ptr, 1 + it * 2)
                    tt(c_tmp[:, 0, :, :], cre, f(17), ALU.mult)
                    tt(c_tmp[:, 1, :, :], cim, f(18), ALU.mult)
                    tt(c_tmp[:, 2, :, :], cre, f(20), ALU.mult)
                    tt(c_tmp[:, 3, :, :], cim, f(19), ALU.mult)
                    pool.drain()
                    pool.wait_ge(s_y, 1 + it * NT)
                    tt(c_sb[:, 0, :, :], c_tmp[:, 0, :, :], c_tmp[:, 1, :, :], ALU.subtract)
                    tt(c_sb[:, 1, :, :], c_tmp[:, 1, :, :], c_tmp[:, 0, :, :], ALU.subtract)
                    tt(c_sb[:, 2, :, :], c_tmp[:, 2, :, :], c_tmp[:, 3, :, :], ALU.add).then_inc(s_c, 1)

                    def drives(n):
                        s = n % 2
                        pool.wait_ge(s_pp, 1 + it * NT + n + 1)
                        if n < 2:
                            pool.wait_ge(s_state, 1 + 2 * it * NT)
                        else:
                            pool.wait_ge(s_state, 1 + 2 * (it * NT + n - 1))
                        tt(drive[:, s, 0, :], turn[:, s, 0, :], turn2[:, s, 1, :], ALU.add)
                        tt(drive[:, s, 1, :], turn[:, s, 1, :], turn2[:, s, 0, :], ALU.subtract)\
                            .then_inc(s_drive, 1)

                    drives(0)
                    for n in range(NT):
                        if n + 1 < NT:
                            drives(n + 1)
                        pool.wait_ge(s_state, 1 + 2 * (it * NT + n + 1))
                        if n < 2:
                            pool.wait_ge(s_y, 1 + it * NT)
                        else:
                            pool.wait_ge(s_y, 1 + it * NT + n - 1)
                        tt(outc[:, n % 2, :, :], state[:, n % 2, :, :], over(tab[:, 1, n, :], 2), ALU.mult)\
                            .then_inc(s_outc, 1)

                with pool.Fori(0, EARLY // 2 + 1) as i:
                    for s in range(2):
                        low_u(l, i * 2 + s, s)
                with pool.Fori(0, S // 16) as i:
                    for b in range(2):
                        pool.drain()
                        pool.wait_ge(s_hot1, (l * (S // 16) + i) * 2 + b + 1)
                        tt(fence[:, 3:4], fence[:, 4:5], fence[:, 4:5], ALU.add)
                        tt(hot1[b], hot1[b], sel_T[:, 2, bass.ds(i * 16 + b * HOT, HOT)].unsqueeze(2)
                           .broadcast_to([P, HOT, PK]), ALU.mult).then_inc(s_gated, 1)
                with pool.Fori(0, (PK - EARLY) // 2 - 1) as i:
                    for s in range(2):
                        low_u(l, i * 2 + s + EARLY + 2, s)


def kernel(x, w_in, w_out, rel_bias, g_attn, g_ssm, norm_mix, norm_ffn, lam_re, lam_im, log_step,
           b_re, b_im, c_re, c_im, d_skip, w_glu, w_query, sub_keys, expert_u, expert_v, norm_final):
    import numpy as np
    import concourse.bacc as bacc
    from concourse.bass_utils import run_bass_kernel_spmd

    f32 = np.float32
    L = DEPTH

    def lay(a, shape, perm, to):
        return np.ascontiguousarray(np.asarray(a).reshape(shape).transpose(perm).reshape(to))

    def columns(a, n):
        return np.asarray(a).reshape(L, n, P).transpose(0, 2, 1)

    a_w_in = lay(w_in, (L, DC, P, 4, NQ, P), (0, 4, 2, 1, 3, 5), (L * NQ, P, DC * 512))
    a_w_out = lay(w_out, (L, DC, P, D), (0, 2, 1, 3), (L, P, DC * D))
    a_w_glu = lay(w_glu, (L, 4, P, D), (0, 2, 1, 3), (L, P, 4 * D))
    a_w_query = lay(w_query, (L, DC, P, PH, P), (0, 3, 2, 1, 4), (L * PH, P, DC * P))
    a_keys = lay(sub_keys, (L, 2, PH, PK, 64), (0, 2, 1, 4, 3), (L * PH, P, PK))
    a_u = lay(expert_u, (L, PK, PK, DC, P), (0, 1, 4, 3, 2), (L * PK, P, DC * P))
    a_v = lay(expert_v, (L, PK, PK, D), (0, 1, 2, 3), (L * PK, PK, D))
    a_gain = np.ascontiguousarray(np.concatenate(
        [columns(norm_mix, 8), columns(norm_ffn, 8), columns(g_attn, 4), columns(g_ssm, 4),
         columns(d_skip, 4)], axis=2))
    def per_state(a):
        return np.asarray(a).reshape(L, 2, NQ, 4, 2, 64).transpose(0, 4, 5, 2, 3, 1).reshape(L, P, 32)
    steps = np.broadcast_to(np.asarray(log_step)[..., None], (L, 2, 32, 64))
    a_par = np.ascontiguousarray(np.stack([per_state(lam_re), per_state(lam_im), per_state(steps)], axis=2))
    a_b = np.zeros((L, NQ, 4, 2, 16, 4, 2, 2, 2, 64), f32)
    a_c = np.zeros((L, NQ, 2, 64, 4, 2, 2, 2, 16), f32)
    for r, (b, c) in enumerate(((b_re, c_re), (b_im, c_im))):
        b = np.asarray(b).reshape(L, 2, NQ, 4, 2, 64, 16)
        c = np.asarray(c).reshape(L, 2, NQ, 4, 2, 16, 64)
        for k in range(4):
            for g in range(2):
                a_b[:, :, k, g, :, k, :, r, g, :] = b[:, :, :, k, g].transpose(0, 2, 4, 1, 3)
                a_c[:, :, g, :, k, :, r, g, :] = c[:, :, :, k, g].transpose(0, 2, 4, 1, 3)
    a_b = a_b.reshape(L * NQ, P, NT * 2 * P)
    a_c = a_c.reshape(L * NQ, P, NT * 2 * 32)

    a_const = np.zeros((P, NCONST), f32)
    a_const[:, 0:P] = np.eye(P)
    a_const[:, P:2 * P] = np.eye(P)[::-1]
    a_const[:, 2 * P:3 * P] = np.arange(P)
    a_const[:, 3 * P:3 * P + 16] = 16 * np.arange(16)
    a_const[:, 3 * P + 16:] = np.arange(16)
    delta = np.arange(TOEP) - (S - 1)
    n = np.abs(delta)
    large = 8 + (np.log(np.maximum(n, 1) / 8) / np.log(1024 / 8) * 8).astype(np.int32)
    bucket = np.where(delta > 0, 16, 0) + np.where(n < 8, n, np.minimum(large, 15))
    count = sum(((n % dil == 0) & (n <= win // 2)).astype(np.int64)
                for win, dil in ((128, 1), (512, 4), (2048, 16)))
    a_rows = np.zeros((33, TOEP), f32)
    a_rows[bucket, np.arange(TOEP)] = 1.0
    a_rows[32] = np.where(count > 0, np.log(np.maximum(count, 1)), -1e30)

    ins = {
        "x_in": np.ascontiguousarray(np.asarray(x).reshape(S, D)), "w_in": a_w_in, "w_out": a_w_out,
        "w_glu": a_w_glu, "w_query": a_w_query, "keys": a_keys, "expert_u": a_u, "expert_v": a_v,
        "rel_bias": np.ascontiguousarray(rel_bias), "gains": a_gain,
        "norm_final": np.ascontiguousarray(norm_final), "ssm_par": a_par, "ssm_b": a_b, "ssm_c": a_c,
        "consts": a_const, "bucket_rows": a_rows,
    }
    nc = bacc.Bacc("TRN2", target_bir_lowering=False, num_devices=1)
    args = [nc.dram_tensor(f"in_{k}", a.shape, mybir.dt.from_np(a.dtype), kind="ExternalInput").ap()
            for k, a in ins.items()]
    args.append(nc.dram_tensor("out_x", (S, D), F32, kind="ExternalOutput").ap())
    encoder(nc, *args)
    r = run_bass_kernel_spmd(nc, [{f"in_{k}": a for k, a in ins.items()}], core_ids=[0])
    return r.results[0]["out_x"].reshape(1, S, D)
```

```python
import concourse.bass as bass
from concourse import mybir
from contextlib import ExitStack

F32 = mybir.dt.float32
F32R = mybir.dt.float32r
U32 = mybir.dt.uint32
ALU = mybir.AluOpType
ACT = mybir.ActivationFunctionType
AX = mybir.AxisListType

P = 128
D = 1024
S = 256
DEPTH = 2
AW = 512
HD = 64
NH = 8
NQ = 4
DC = D // P
TT = S // P
NT = 8
PH = 8
PK = 128
TOPK = 16
EPS = 1e-6
ROUND = 12582912.0
GRID14 = 768.0
TWO_PI_A = 6.28125
TWO_PI_B = 0.0019353071795864769
INV_TWO_PI = 0.15915494309189535
TWO_PI_BELOW = 6.28318501
HALF_PI = 1.5707963267948966
LOWEST = -3.0e38
NCONST = 3 * P + 32
TOEP = 2 * S
WITH_HEADS = 4 * PH
EARLY = WITH_HEADS + 4
HOT = 4
BATCHES = 4
assert HOT * BATCHES * PK == 2 * D


def encoder(nc, x, w_in, w_out, w_glu, w_query, keys, expert_u, expert_v, rel_bias, gains,
            norm_final, ssm_par, ssm_b, ssm_c, consts, bucket_rows, out):
    ctx = ExitStack()
    with ctx:
        def sb(name, shape, dt=F32):
            return ctx.enter_context(nc.sbuf_tensor(name, shape, dt))

        def sem(name):
            return ctx.enter_context(nc.semaphore(name))

        cst = sb("cst", [P, NCONST])
        ident, antiident, iota = cst[:, 0:P], cst[:, P:2 * P], cst[:, 2 * P:3 * P]
        steps_ab = cst[:, 3 * P:3 * P + 32]
        iota16 = cst[:, 2 * P:2 * P + TOPK]
        gain = sb("gain", [P, 28])
        g_mix, g_ffn, g_cat, d_skip = gain[:, 0:8], gain[:, 8:16], gain[:, 16:24], gain[:, 24:28]
        tiny = sb("tiny", [P, 4])
        eps_c, half_pi_c = tiny[:, 0:1], tiny[:, 1:2]
        fence = sb("fence", [P, 5])
        sel_T = sb("sel_T", [P, 3, S])
        h_hl = sb("h_hl", [P, 2, DC, S], F32R)
        u_hl = [sb(f"u_hl{i}", [P, 2, DC, P], F32R) for i in range(2)]
        v_hl = [sb(f"v_hl{i}", [P, 2, D], F32R) for i in range(2)]
        w_hl = [sb(f"w_hl{i}", [P, 2, S], F32R) for i in range(2)]
        u_raw = [sb(f"u_raw{i}", [P, DC, P]) for i in range(2)]
        v_raw_all = sb("v_raw", [P, 2 * D])
        v_raw = [v_raw_all[:, i * D:(i + 1) * D] for i in range(2)]
        u_all = v_raw_all[:, :].rearrange("p (q r t) -> p q r t", q=NQ, r=2)
        act_w = sb("act_w", [P, 2, S])
        hot1 = [v_raw[b // 2][:, b % 2 * HOT * PK:(b % 2 + 1) * HOT * PK].rearrange("p (j n) -> p j n", j=HOT)
                for b in range(BATCHES)]
        hot2 = [u_raw[b // 2][:, b % 2 * HOT:(b % 2 + 1) * HOT, :] for b in range(BATCHES)]

        arena = sb("arena", [P, PK * S])
        gates = arena[:, :].rearrange("p (c t) -> p c t", t=S)
        at = [0]

        def take(words):
            at[0] += words
            assert at[0] <= PK * S
            return arena[:, at[0] - words:at[0]]

        xs_f = take(TT * D)
        xs = xs_f.rearrange("p (a n) -> p a n", a=TT)
        w_slot_f = take(DC * 512)
        w_slot = w_slot_f.rearrange("p (m k n) -> p m k n", k=DC, m=4)
        w_glu_sb = w_slot_f.rearrange("p (k n) -> p k n", k=4)
        slots = take(4 * S)
        c_raw = slots[:, 0:NT * 2 * 32].rearrange("p (n r m) -> p n r m", n=NT, r=2)
        qT, kT = (slots[:, i * S:(i + 1) * S] for i in (2, 3))
        ssm = slots.rearrange("p (a n) -> p a n", a=TT)
        v_sb = take(TT * P).rearrange("p (a n) -> p a n", a=TT)
        attn = take(TT * AW).rearrange("p (a n) -> p a n", a=TT)
        assert at[0] >= WITH_HEADS * S
        hT_f = take(DC * S)
        hT = hT_f.rearrange("p (k t) -> p k t", k=DC)
        mixn = hT_f.rearrange("p (a n) -> p a n", a=TT)
        assert at[0] >= EARLY * S
        bias_f = take(NH * 3 * P)
        FIRST_READ = -(-at[0] // S)
        bias = bias_f.rearrange("p (h n) -> p h n", h=NH)
        big = at[0]
        tab = take(2 * NT * S).rearrange("p (s n t) -> p s n t", s=2, n=NT)
        turn_f = take(2 * 2 * S)
        turn = turn_f.rearrange("p (s r t) -> p s r t", s=2, r=2)
        turn2 = take(2 * 2 * S).rearrange("p (s r t) -> p s r t", s=2, r=2)
        drive = take(2 * 2 * S).rearrange("p (s r t) -> p s r t", s=2, r=2)
        state = take(2 * 2 * S).rearrange("p (s r t) -> p s r t", s=2, r=2)
        outc = take(2 * 2 * S).rearrange("p (s r t) -> p s r t", s=2, r=2)
        outs = take(2 * 2 * S).rearrange("p (s r t) -> p s r t", s=2, r=2)
        w_out_sb = arena[:, big:big + DC * D].rearrange("p (k n) -> p k n", k=DC)
        xn = arena[:, big + DC * D:big + DC * D + TT * D].rearrange("p (a n) -> p a n", a=TT)
        b_f = take(NT * 2 * P)
        b_sb = b_f.rearrange("p (n r m) -> p n r m", n=NT, r=2)
        mixT = b_f.rearrange("p (k t) -> p k t", k=DC)
        c_sb = take(3 * NT * 32).rearrange("p (j n m) -> p j n m", j=3, n=NT)
        probs_f = take(4 * S)
        probs = probs_f.rearrange("p (s t) -> p s t", s=4)
        c_tmp = take(4 * NT * 32).rearrange("p (j n m) -> p j n m", j=4, n=NT)
        angle_t = probs_f.rearrange("p (n j) -> p n j", j=32)
        pT = take(2 * S).rearrange("p (s a t) -> p s a t", s=2, a=TT)
        yT = take(4 * S).rearrange("p (k t) -> p k t", k=4)
        ysum = take(2 * S).rearrange("p (s t) -> p s t", s=2)
        angle = take(NQ * NT * 32).rearrange("p (n j) -> p n j", j=32)
        par = take(3 * 32).rearrange("p (k n) -> p k n", k=3)
        sm = take(24 * 32).rearrange("p (k n) -> p k n", k=24)
        stat = take(32)
        sel0 = at[0]
        wq_slot = bias_f[:, 0:2048].rearrange("p (s k n) -> p s k n", s=2, k=DC)
        key_slot = bias_f[:, 2048:2048 + 2 * P].rearrange("p (s n) -> p s n", s=2)
        at[0] = big

        def again(words):
            return take(words)

        qh = again(S)
        sc = again(2 * TT * PK).rearrange("p (b a n) -> p b a n", b=2, a=TT)
        sc2 = again(2 * TT * PK).rearrange("p (b a n) -> p b a n", b=2, a=TT)
        t16 = again(4 * TOPK).rearrange("p (b a n) -> p b a n", b=2, a=TT)
        i16u = again(4 * TOPK).bitcast(U32).rearrange("p (b a n) -> p b a n", b=2, a=TT)
        i16 = again(4 * TOPK).rearrange("p (b a n) -> p b a n", b=2, a=TT)
        cand = again(TT * S).rearrange("p (a i j) -> p a i j", a=TT, i=TOPK)
        cand2 = again(TT * S).rearrange("p (a n) -> p a n", a=TT)
        top = again(TT * TOPK).rearrange("p (a n) -> p a n", a=TT)
        cu = again(TT * TOPK).bitcast(U32).rearrange("p (a n) -> p a n", a=TT)
        rank_u = again(2 * TT * TOPK).bitcast(U32).rearrange("p (b a n) -> p b a n", b=2, a=TT)
        rank = again(2 * TT * TOPK).rearrange("p (b a n) -> p b a n", b=2, a=TT)
        pick = again(2 * TT * S).rearrange("p (b a i j) -> p b a i j", b=2, a=TT, i=TOPK)
        sel = again(3 * TT * PH * TOPK).rearrange("p (k a h j) -> p k a h j", k=3, a=TT, h=PH)
        gsum = again(TT * PH).rearrange("p (a h) -> p a h", a=TT)
        assert at[0] <= big + DC * D
        xb = xs
        gfin = arena[:, TT * D:TT * D + D]
        rows_sb = sel_T[0:33, 0:2, :].rearrange("p k t -> p (k t)")
        rel_sb = sel_T[0:33, 2, 0:NH]
        toep_sb = act_w[0:NH, :, :].rearrange("p k t -> p (k t)")

        ps = ctx.enter_context(nc.psum_tensor("ps", [P, 8, 512], F32))

        toep_d = nc.dram_tensor("toep_scratch", [NH, TOEP], F32, kind="Internal")
        x_d = nc.dram_tensor("x_scratch", [P, TT * D], F32, kind="Internal")

        s_const = sem("s_const")
        s_memset = sem("s_memset")
        s_xin = sem("s_xin")
        s_rel = sem("s_rel")
        s_relones = sem("s_relones")
        s_toep_mm = sem("s_toep_mm")
        s_toep_sb = sem("s_toep_sb")
        s_toep_d = sem("s_toep_d")
        s_gain = sem("s_gain")
        s_par = sem("s_par")
        s_bias = sem("s_bias")
        s_layer = sem("s_layer")
        s_rms = sem("s_rms")
        s_rstd = sem("s_rstd")
        s_xn = sem("s_xn")
        s_tr = sem("s_tr")
        s_hT = sem("s_hT")
        s_p1 = sem("s_p1")
        s_p2 = sem("s_p2")
        s_p3 = sem("s_p3")
        s_coef = sem("s_coef")
        s_w_free = sem("s_w_free")
        s_w_u = sem("s_w_u")
        s_w_qk = sem("s_w_qk")
        s_w_v = sem("s_w_v")
        s_b_ld = [sem(f"s_b_ld{i}") for i in range(2)]
        s_c_ld = sem("s_c_ld")
        s_c_tmp = sem("s_c_tmp")
        s_proj = sem("s_proj")
        s_u_sb = sem("s_u_sb")
        s_qk_sb = sem("s_qk_sb")
        s_v_sb = sem("s_v_sb")
        s_turns = sem("s_turns")
        s_tab = sem("s_tab")
        s_c = sem("s_c")
        s_bu = sem("s_bu")
        s_pp = sem("s_pp")
        s_drive = sem("s_drive")
        s_state = sem("s_state")
        s_outs = sem("s_outs")
        s_outc = sem("s_outc")
        s_y = sem("s_y")
        s_ysum = sem("s_ysum")
        s_yT = sem("s_yT")
        s_score = sem("s_score")
        s_max = sem("s_max")
        s_exp = sem("s_exp")
        s_ptr = sem("s_ptr")
        s_pT = sem("s_pT")
        s_pv = sem("s_pv")
        s_attn = sem("s_attn")
        s_wglu = sem("s_wglu")
        s_wout = sem("s_wout")
        s_glu = sem("s_glu")
        s_sig = sem("s_sig")
        s_ssm = sem("s_ssm")
        s_mixn = sem("s_mixn")
        s_mixtr = sem("s_mixtr")
        s_mixT = sem("s_mixT")
        s_wo = sem("s_wo")
        s_x1 = sem("s_x1")
        s_spill = sem("s_spill")
        s_wq = [sem(f"s_wq{i}") for i in range(2)]
        s_q = sem("s_q")
        s_qh = sem("s_qh")
        s_sc = sem("s_sc")
        s_sc_sb = sem("s_sc_sb")
        s_sc_used = sem("s_sc_used")
        s_topd = sem("s_topd")
        s_gexp = sem("s_gexp")
        s_sel = sem("s_sel")
        s_seltr = sem("s_seltr")
        s_selT = sem("s_selT")
        s_hhi = sem("s_hhi")
        s_hlo = sem("s_hlo")
        s_hot1 = sem("s_hot1")
        s_hot2 = sem("s_hot2")
        s_gated = sem("s_gated")
        s_hot_free = sem("s_hot_free")
        s_gmul = sem("s_gmul")
        s_gates = sem("s_gates")
        s_u_ld = [sem(f"s_u_ld{i}") for i in range(2)]
        s_v_ld = [sem(f"s_v_ld{i}") for i in range(2)]
        s_u_hi = sem("s_u_hi")
        s_v_hi = sem("s_v_hi")
        s_u_lo = sem("s_u_lo")
        s_v_lo = sem("s_v_lo")
        s_u_mm = sem("s_u_mm")
        s_v_mm = sem("s_v_mm")
        s_gelu = sem("s_gelu")
        s_wt = sem("s_wt")
        s_xback = sem("s_xback")
        s_gfin = sem("s_gfin")
        s_fin = sem("s_fin")
        s_out = sem("s_out")

        block = ctx.enter_context(nc.Block())

        def col(ap, i, n=1):
            return ap[:, bass.ds(i, n)]

        def over(ap, n):
            return ap.unsqueeze(1).broadcast_to([ap.shape[0], n, ap.shape[1]])

        @block.sync
        def _(sp):
            for a in range(TT):
                sp.dma_start(xs[:, a, :], x[a * P:(a + 1) * P, :]).then_inc(s_xin, 16)
            sp.dma_start(cst[:, :], consts).then_inc(s_const, 16)
            sp.wait_ge(s_relones, 1)
            sp.dma_start(rel_sb[0:32, :], rel_bias).then_inc(s_rel, 16)
            sp.dma_start(rows_sb, bucket_rows).then_inc(s_rel, 16)
            overlap = bass.AP(toep_d, 0, [[1, P], [TOEP, NH], [1, 3 * P]])

            def load_u(l, c, s):
                sp.dma_start(u_raw[s][:, :, :], expert_u[bass.ds(l * PK + c, 1), :, :]
                             .rearrange("o p n -> (o p) n").rearrange("p (k n) -> p k n", k=DC)).then_inc(s_u_ld[s], 16)

            def load_v(l, c, s):
                sp.dma_start(v_raw[s][:, :], expert_v[bass.ds(l * PK + c, 1), :, :]
                             .rearrange("o p n -> (o p) n")).then_inc(s_v_ld[s], 16)

            def load_w(it, kind, n, signal):
                sp.dma_start(w_slot[:, kind:kind + n, :, :],
                             w_in[bass.ds(it, 1), :, kind * D:(kind + n) * D].rearrange("o p n -> (o p) n")
                             .rearrange("p (m k n) -> p m k n", m=n, k=DC)).then_inc(signal, 16)

            def load_c(it):
                sp.dma_start(c_raw, ssm_c[bass.ds(it, 1), :, :].rearrange("o p n -> (o p) n")
                             .rearrange("p (n r m) -> p n r m", n=NT, r=2)).then_inc(s_c_ld, 16)

            def load_b(it, half):
                sp.wait_ge(s_bu, NT * it + 4 + 4 * half)
                n = NT * P
                sp.dma_start(b_f[:, half * n:(half + 1) * n],
                             ssm_b[bass.ds(it, 1), :, half * n:(half + 1) * n].rearrange("o p n -> (o p) n"))\
                    .then_inc(s_b_ld[half], 16)

            def first_loads(l):
                sp.dma_start(gain[:, :], gains[bass.ds(l, 1), :, :].rearrange("o p n -> (o p) n"))\
                    .then_inc(s_gain, 16)
                load_w(l * NQ, 3, 1, s_w_u)
                load_w(l * NQ, 0, 2, s_w_qk)
                load_c(l * NQ)
                load_w(l * NQ, 2, 1, s_w_v)
                sp.wait_ge(s_toep_d, 16)
                sp.dma_start(bias, overlap).then_inc(s_bias, 16)

            def layer(l, more):
                sp.wait_ge(s_layer, 1 + l)
                sp.dma_start(par, ssm_par[bass.ds(l, 1), :, :, :].rearrange("o p k n -> (o p) k n"))\
                    .then_inc(s_par, 16)
                with sp.Fori(0, NQ - 1) as q:
                    it = l * NQ + q
                    load_b(it, 0)
                    sp.wait_ge(s_proj, 3 * it + 4)
                    load_w(it + 1, 3, 1, s_w_u)
                    load_b(it, 1)
                    sp.wait_ge(s_proj, 3 * it + 5)
                    sp.sem_inc(s_w_free, 1)
                    load_w(it + 1, 0, 2, s_w_qk)
                    sp.wait_ge(s_c_tmp, 1 + it + 1)
                    load_c(it + 1)
                    sp.wait_ge(s_proj, 3 * it + 6)
                    load_w(it + 1, 2, 1, s_w_v)
                load_b(l * NQ + NQ - 1, 0)
                load_b(l * NQ + NQ - 1, 1)
                sp.wait_ge(s_proj, 3 + (l + 1) * 3 * NQ)
                sp.dma_start(w_glu_sb, w_glu[bass.ds(l, 1), :, :].rearrange("o p n -> (o p) n")
                             .rearrange("p (k n) -> p k n", k=4)).then_inc(s_wglu, 16)
                sp.wait_ge(s_y, 2 + (l + 1) * NT * NQ)
                sp.dma_start(w_out_sb, w_out[bass.ds(l, 1), :, :].rearrange("o p n -> (o p) n")
                             .rearrange("p (k n) -> p k n", k=DC)).then_inc(s_wout, 16)
                sp.wait_ge(s_x1, TT * (l + 1))
                sp.dma_start(x_d.ap(), xs_f).then_inc(s_spill, 16)

                def load_head(h, s):
                    ih = l * PH + h
                    sp.dma_start(wq_slot[:, s, :, :], w_query[bass.ds(ih, 1), :, :]
                                 .rearrange("o p n -> (o p) n").rearrange("p (k n) -> p k n", k=DC))\
                        .then_inc(s_wq[s], 16)
                    sp.dma_start(key_slot[:, s, :], keys[bass.ds(ih, 1), :, :]
                                 .rearrange("o p n -> (o p) n")).then_inc(s_wq[s], 16)

                def next_u(c, s):
                    sp.wait_ge(s_u_lo, l * PK + c - 1)
                    load_u(l, c, s)

                def next_v(c, s):
                    sp.wait_ge(s_v_lo, l * PK + c - 1)
                    load_v(l, c, s)

                for s in range(2):
                    load_head(s, s)
                with sp.Fori(0, PH // 2 - 1) as hp:
                    for s in range(2):
                        for j in range(4):
                            next_u(hp * 8 + s * 4 + j + 2, j % 2)
                        sp.wait_ge(s_sc, 1 + l * PH + hp * 2 + s + 1)
                        load_head(hp * 2 + s + 2, s)
                for c in range(WITH_HEADS - 8, EARLY):
                    next_u(c + 2, c % 2)
                sp.wait_ge(s_gates, 4 + (l + 1) * (S // 4))
                for s in range(2):
                    load_v(l, s, s)
                with sp.Fori(0, EARLY // 2) as i:
                    for s in range(2):
                        next_v(i * 2 + s + 2, s)
                with sp.Fori(0, (PK - EARLY) // 2 - 1) as i:
                    for s in range(2):
                        next_u(i * 2 + s + EARLY + 2, s)
                        next_v(i * 2 + s + EARLY + 2, s)
                sp.wait_ge(s_wt, l * PK + FIRST_READ)
                sp.dma_start(xs_f, x_d.ap()).then_inc(s_xback, 16)
                if more:
                    first_loads(l + 1)
                    for s in range(2):
                        sp.wait_ge(s_u_lo, (l + 1) * PK)
                        load_u(l + 1, s, s)

            first_loads(0)
            for s in range(2):
                load_u(0, s, s)
            with sp.Fori(0, DEPTH - 1) as l:
                layer(l, True)
            layer(DEPTH - 1, False)
            sp.wait_ge(s_layer, 1 + DEPTH)
            sp.dma_start(gfin, norm_final.partition_broadcast(P)).then_inc(s_gfin, 16)
            sp.wait_ge(s_fin, 1)
            sp.dma_start(out.rearrange("(a p) n -> p a n", p=P), xn).then_inc(s_out, 16)
            sp.wait_ge(s_out, 16)

        @block.tensor
        def _(pe):
            pe.wait_ge(s_const, 16)
            pe.wait_ge(s_rel, 32)
            pe.matmul(ps[0:NH, 0, :], rel_sb, rows_sb, start=True, stop=True).then_inc(s_toep_mm, 1)

            def transposes(src, a, sem_done):
                for c in range(DC):
                    m = pe.transpose(ps[:, 2 * a + c // 4, (c % 4) * P:(c % 4 + 1) * P],
                                     src[:, a, c * P:(c + 1) * P], ident)
                    if c % 4 == 3:
                        m.then_inc(sem_done, 1)

            with pe.Fori(0, DEPTH) as l:
                pe.wait_ge(s_toep_sb, 1)
                for a in range(TT):
                    pe.wait_ge(s_xn, 4 * l + a + 1)
                    transposes(xn, a, s_tr)

                def project(q, kind, lo, hi):
                    it = l * NQ + q
                    if lo == 0 and kind == 3:
                        pe.wait_ge(s_w_u, 16 * (it + 1))
                        pe.wait_ge(s_v_sb, 1 + it)
                    if lo == 0 and kind == 0:
                        pe.wait_ge(s_w_qk, 16 * (it + 1))
                        pe.wait_ge(s_qk_sb, 1 + it)
                    if lo == 0 and kind == 2:
                        pe.wait_ge(s_w_v, 16 * (it + 1))
                        pe.wait_ge(s_u_sb, it + 1)
                    if kind == 2:
                        for a in range(lo, hi):
                            for k in range(DC):
                                m = pe.matmul(ps[:, 1, a * P:(a + 1) * P], hT[:, k, a * P:(a + 1) * P],
                                              w_slot[:, 2, k, :], start=(k == 0), stop=(k == DC - 1))
                    else:
                        bank, o = {3: (1, S), 0: (0, 0), 1: (0, S)}[kind]
                        for k in range(lo, hi):
                            m = pe.matmul(ps[:, bank, o:o + S], w_slot[:, kind, k, :], hT[:, k, :],
                                          start=(k == 0), stop=(k == DC - 1))
                    if hi == (TT if kind == 2 else DC) and kind != 0:
                        m.then_inc(s_proj, 1)

                def b_product(q, n):
                    it = l * NQ + q
                    if n % 4 == 0:
                        pe.wait_ge(s_b_ld[n // 4 % 2], 16 * (it + n // NT + 1))
                    if n % NT == 0:
                        pe.wait_ge(s_u_sb, it + n // NT + 1)
                    pe.wait_ge(s_pp, it * NT + n + 1)
                    for r in range(2):
                        m = pe.matmul(ps[:, 5 + n % 2, r * S:(r + 1) * S], b_sb[:, n % NT, r, :],
                                      u_all[:, bass.ds(q + n // NT, 1), n % 2, :].rearrange("p o t -> p (o t)"),
                                      start=True, stop=True)
                    m.then_inc(s_bu, 1)

                def c_product(q, n):
                    it = l * NQ + q
                    if n % NT == 0:
                        pe.wait_ge(s_ysum, 1 + it + n // NT)
                        pe.wait_ge(s_c, 1 + it + n // NT + 1)
                    pe.wait_ge(s_outc, 1 + it * NT + n + 1)
                    pe.wait_ge(s_outs, it * NT + n + 1)
                    k, o = n % NT // 2, (n % 2) * S
                    terms = ((0, outc[:, n % 2, 0, :]), (1, outs[:, n % 2, 1, :]),
                             (2, outs[:, n % 2, 0, :]), (2, outc[:, n % 2, 1, :]))
                    for j, (kind, rhs) in enumerate(terms):
                        m = pe.matmul(ps[32 * k:32 * k + 32, 7, o:o + S], c_sb[:, kind, n % NT, :], rhs,
                                      start=(j == 0), stop=(j == 3))
                    m.then_inc(s_y, 1)

                def scores(q, head):
                    it = l * NQ + q
                    pe.wait_ge(s_qk_sb, 1 + it + 1)
                    pe.wait_ge(s_attn, 1 + it)
                    for a in range(TT):
                        dst = ps[:, 2 + head, a * S:(a + 1) * S]
                        pe.matmul(dst, antiident, bias[:, bass.ds(q * 2 + head, 1), P - a * P:P - a * P + S]
                                  .rearrange("p o n -> p (o n)"), start=True, stop=False)
                        m = pe.matmul(dst, qT[head * HD:(head + 1) * HD, a * P:(a + 1) * P],
                                      kT[head * HD:(head + 1) * HD, :], start=False, stop=True)
                    m.then_inc(s_score, 1)

                def prob_transposes(q, head):
                    it = l * NQ + q
                    pe.wait_ge(s_exp, it * 2 + head + 1)
                    pe.wait_ge(s_pT, 1 + it * 2 + head)
                    for a in range(TT):
                        for b in range(TT):
                            o = a * S + b * P
                            m = pe.transpose(ps[:, 4, o:o + P], probs[:, 2 * head + a, b * P:(b + 1) * P],
                                             ident)
                    m.then_inc(s_ptr, 1)

                def values(q, head):
                    it = l * NQ + q
                    pe.wait_ge(s_v_sb, 1 + it + 1)
                    pe.wait_ge(s_pT, 1 + it * 2 + head + 1)
                    for a in range(TT):
                        s = 2 * head + a
                        for b in range(TT):
                            m = pe.matmul(ps[:, 2, s * HD:(s + 1) * HD], pT[:, a, b, :],
                                          v_sb[:, b, head * HD:(head + 1) * HD],
                                          start=(b == 0), stop=(b == TT - 1))
                    if head:
                        m.then_inc(s_pv, 1)

                def mix_block(q, more):
                    for n in range(1, NT + 1 if more else NT):
                        if n + 2 < NT or more:
                            b_product(q, n + 2)
                        if n in (1, 2):
                            scores(q, n - 1)
                        if more:
                            for kind, lo, hi in {1: ((3, 0, 6),), 2: ((3, 6, 8), (0, 0, 2)), 3: ((0, 2, 6),),
                                                 4: ((0, 6, 8), (1, 0, 2)), 5: ((1, 2, 5),),
                                                 6: ((1, 5, 8),), 7: ((2, 0, 1),), 8: ((2, 1, 2),)}[n]:
                                project(q + 1, kind, lo, hi)
                        c_product(q, n)
                        if n in (5, 6):
                            values(q, n - 5)
                        if n in (4, 5):
                            prob_transposes(q, n - 4)

                pe.wait_ge(s_hT, (2 * l + 1) * 4)
                for kind in (3, 0, 1, 2):
                    project(0, kind, 0, TT if kind == 2 else DC)
                b_product(0, 0)
                b_product(0, 1)
                b_product(0, 2)
                c_product(0, 0)
                with pe.Fori(0, NQ - 1) as q:
                    pe.wait_ge(s_bias, 16 * (l + 1))
                    mix_block(q, True)
                mix_block(NQ - 1, False)

                pe.wait_ge(s_wglu, 16 * (l + 1))
                pe.wait_ge(s_yT, 1 + NQ * (l + 1))
                pe.wait_ge(s_attn, 1 + NQ * (l + 1))
                for a in range(TT):
                    for half in range(2):
                        for k in range(4):
                            m = pe.matmul(ps[:, 2 * a + half, :], yT[:, k, a * P:(a + 1) * P],
                                          w_glu_sb[:, k, half * AW:(half + 1) * AW],
                                          start=(k == 0), stop=(k == 3))
                    m.then_inc(s_glu, 1)
                def w_out_half(a, half):
                    for k in range(DC):
                        m = pe.matmul(ps[:, 4 + 2 * a + half, :], mixT[:, k, a * P:(a + 1) * P],
                                      w_out_sb[:, k, half * 512:(half + 1) * 512],
                                      start=(k == 0), stop=(k == DC - 1))
                    m.then_inc(s_wo, 1)

                pe.wait_ge(s_mixn, 2 * l + 1)
                transposes(mixn, 0, s_mixtr)
                pe.wait_ge(s_mixT, 4 * l + 2)
                pe.wait_ge(s_wout, 16 * (l + 1))
                w_out_half(0, 0)
                pe.wait_ge(s_mixn, 2 * l + 2)
                transposes(mixn, 1, s_mixtr)
                w_out_half(0, 1)
                pe.wait_ge(s_mixT, 4 * l + 4)
                w_out_half(1, 0)
                pe.wait_ge(s_xn, 4 * l + 3)
                transposes(xn, 0, s_tr)
                w_out_half(1, 1)
                pe.wait_ge(s_xn, 4 * l + 4)
                transposes(xn, 1, s_tr)

                def up(c, s):
                    n = l * PK + c
                    pe.wait_ge(s_u_lo, n + 1)
                    pe.wait_ge(s_gelu, 2 + n - 1)
                    terms = ((0, 0), (0, 1), (1, 0))
                    for k in range(DC):
                        for j, (wp, hp_) in enumerate(terms):
                            m = pe.matmul(ps[:, 4 + s, 0:S], u_hl[s][:, wp, k, :], h_hl[:, hp_, k, :],
                                          start=(k == 0 and j == 0), stop=(k == DC - 1 and j == 2))
                    m.then_inc(s_u_mm, 1)

                def down(c, s, first=False, last=False):
                    n = l * PK + c
                    pe.wait_ge(s_v_lo, n + 1)
                    pe.wait_ge(s_wt, n + 1)
                    terms = ((0, 0), (0, 1), (1, 0))
                    for a in range(TT):
                        for j, (wp, vp) in enumerate(terms):
                            for half in range(2):
                                m = pe.matmul(ps[:, 2 * a + half, :], w_hl[s][:, wp, a * P:(a + 1) * P],
                                              v_hl[s][:, vp, half * 512:(half + 1) * 512],
                                              start=(first and j == 0), stop=(last and j == 2))
                    m.then_inc(s_v_mm, 1)

                with pe.Fori(0, PH // 2) as hp:
                    for s in range(2):
                        ih = l * PH + hp * 2 + s
                        if s == 0:
                            pe.wait_ge(s_hT, (2 * l + 2) * 4)
                        pe.wait_ge(s_wq[s], 32 * (l * (PH // 2) + hp + 1))
                        for k in range(DC):
                            m = pe.matmul(ps[:, 6, 0:S], wq_slot[:, s, k, :], hT[:, k, :],
                                          start=(k == 0), stop=(k == DC - 1))
                        m.then_inc(s_q, 1)
                        pe.wait_ge(s_hlo, TT * (l + 1))
                        for j in range(2):
                            up(hp * 8 + s * 4 + j, j)
                        pe.wait_ge(s_qh, ih + 1)
                        pe.wait_ge(s_sc_sb, 1 + ih)
                        for half in range(2):
                            for a in range(TT):
                                m = pe.matmul(ps[:, half, a * PK:(a + 1) * PK],
                                              qh[half * 64:half * 64 + 64, a * P:(a + 1) * P],
                                              key_slot[half * 64:half * 64 + 64, s, :], start=True, stop=True)
                        m.then_inc(s_sc, 1)
                        for j in range(2):
                            up(hp * 8 + s * 4 + j + 2, j)
                for j in range(EARLY - WITH_HEADS):
                    up(WITH_HEADS + j, j % 2)
                pe.wait_ge(s_sel, l + 1)
                for k in range(3):
                    for a in range(TT):
                        m = pe.transpose(ps[:, 2 + k // 2, (k % 2) * S + a * P:(k % 2) * S + (a + 1) * P],
                                         sel[:, k, a, :, :].rearrange("p h j -> p (h j)"), ident)
                m.then_inc(s_seltr, 1)
                with pe.Fori(0, S // 16) as i:
                    pe.wait_ge(s_selT, l + 1)
                    for b in range(BATCHES):
                        batch = (l * (S // 16) + i) * BATCHES + b
                        pe.wait_ge(s_gates, batch + 1)
                        pe.wait_ge(s_hot2, batch + 1)
                        pe.wait_ge(s_gated, batch + 1)
                        for j in range(HOT):
                            m = pe.matmul(ps[:, b, j * P:(j + 1) * P], hot2[b][:, j, :], hot1[b][:, j, :],
                                          start=True, stop=True)
                        m.then_inc(s_hot_free, 1)

                for s in range(2):
                    up(EARLY + s, s)
                down(0, 0, first=True)
                down(1, 1)
                with pe.Fori(0, EARLY // 2 - 1) as i:
                    for s in range(2):
                        down(i * 2 + s + 2, s)
                with pe.Fori(0, (PK - EARLY) // 2 - 1) as i:
                    for s in range(2):
                        down(i * 2 + EARLY + s, s)
                        up(i * 2 + EARLY + s + 2, s)
                down(PK - 2, 0)
                down(PK - 1, 1, last=True)

        @block.scalar
        def _(act):
            def fenced(func=ACT.Copy):
                act.activation(fence[0:1, 0:1], fence[0:1, 1:2], func)

            def table_of(func):
                act.drain()
                act.activation(fence[0:1, 0:1], fence[0:1, 1:2], func)

            act.wait_ge(s_toep_mm, 1)
            act.activation(toep_sb, ps[0:NH, 0, :], ACT.Copy).then_inc(s_toep_sb, 1)
            act.wait_ge(s_toep_sb, 1)
            act.dma_start(toep_d.ap(), toep_sb).then_inc(s_toep_d, 16)
            act.wait_ge(s_memset, 1)

            def squares(src, n, j, scratch):
                return act.activation(scratch[:, 0:n], src, ACT.Square, accum_out=stat[:, j:j + 1])

            with act.Fori(0, DEPTH) as l:
                table_of(ACT.Sqrt)
                act.wait_ge(s_layer, 1 + l)
                for a in range(TT):
                    act.wait_ge(s_xin, 16 * (a + 1))
                    squares(xs[:, a, :], D, a, turn_f)
                    act.drain()
                    act.activation(stat[:, 2 + a:3 + a], stat[:, a:a + 1], ACT.Sqrt, bias=eps_c,
                                   scale=1.0 / D).then_inc(s_rms, 1)
                act.wait_ge(s_par, 16 * (l + 1))
                act.activation(sm[:, 0, :], par[:, 2, :], ACT.Exp).then_inc(s_p1, 1)
                act.wait_ge(s_p2, l + 1)
                act.activation(sm[:, 3, :], sm[:, 2, :], ACT.Exp)
                act.activation(sm[:, 9, :], sm[:, 7, :], ACT.Sin, scale=TWO_PI_BELOW)
                act.activation(sm[:, 8, :], sm[:, 7, :], ACT.Abs)
                act.drain()
                act.activation(sm[:, 10, :], sm[:, 8, :], ACT.Sin, scale=-TWO_PI_BELOW, bias=half_pi_c)\
                    .then_inc(s_p3, 1)

                def angles(q, half):
                    tiles = slice(half * NT // 2, (half + 1) * NT // 2)
                    act.wait_ge(s_turns, 2 * (l * NQ + q) + half + 1)
                    act.activation(tab[:, 1, tiles, :], tab[:, 0, tiles, :], ACT.Abs)
                    act.drain()
                    act.activation(tab[:, 0, tiles, :], tab[:, 0, tiles, :], ACT.Sin, scale=TWO_PI_BELOW)
                    act.activation(tab[:, 1, tiles, :], tab[:, 1, tiles, :], ACT.Sin, scale=-TWO_PI_BELOW,
                                   bias=half_pi_c).then_inc(s_tab, 1)

                def copy_u(q):
                    act.drain()
                    act.wait_ge(s_proj, 3 + 3 * (l * NQ + q) + 1)
                    fenced()
                    for r, src in enumerate((ps[:, 1, S:2 * S], ps[:, 1, S:2 * S][:, ::-1])):
                        m = act.activation(u_all[:, bass.ds(q, 1), r, :].rearrange("p o t -> p (o t)"), src, ACT.Copy)
                    m.then_inc(s_u_sb, 1)

                def copy_qk(q):
                    act.wait_ge(s_proj, 3 + 3 * (l * NQ + q) + 2)
                    act.activation(qT, ps[:, 0, 0:S], ACT.Copy, scale=HD ** -0.5)
                    act.activation(kT, ps[:, 0, S:2 * S], ACT.Copy).then_inc(s_qk_sb, 1)

                def copy_v(q):
                    act.wait_ge(s_proj, 3 + 3 * (l * NQ + q) + 3)
                    act.wait_ge(s_pv, 1 + l * NQ + q)
                    act.activation(v_sb, ps[:, 1, 0:S].rearrange("p (a n) -> p a n", a=TT), ACT.Copy)\
                        .then_inc(s_v_sb, 1)

                def copy_c(q):
                    it = l * NQ + q
                    act.wait_ge(s_c_tmp, 1 + it + 1)
                    act.wait_ge(s_y, 2 + it * NT)
                    act.activation(c_sb[:, 0, :, :], c_tmp[:, 0, :, :], ACT.Copy)
                    act.activation(c_sb[:, 1, :, :], c_tmp[:, 0, :, :], ACT.Copy, scale=-1.0)
                    act.activation(c_sb[:, 2, :, :], c_tmp[:, 2, :, :], ACT.Copy).then_inc(s_c, 1)

                def mix_block(q, more):
                    it = l * NQ + q
                    angles(q, 1)
                    if more:
                        copy_u(q + 1)
                    for head in range(2):
                        act.wait_ge(s_max, it * 2 + head + 1)
                        for a in range(TT):
                            s = 2 * head + a
                            m = act.activation(probs[:, s, :], ps[:, 2 + head, a * S:(a + 1) * S], ACT.Exp,
                                               bias=stat[:, 8 + s:9 + s], accum_out=stat[:, 12 + s:13 + s])
                        m.then_inc(s_exp, 1)
                    for head in range(2):
                        if head and more:
                            angles(q + 1, 0)
                        act.wait_ge(s_ptr, 1 + it * 2 + head + 1)
                        act.activation(pT, ps[:, 4, :].rearrange("p (s a n) -> p s a n", s=2, a=TT), ACT.Copy)\
                            .then_inc(s_pT, 1)
                    if more:
                        copy_qk(q + 1)
                        copy_c(q + 1)
                    act.drain()
                    act.wait_ge(s_ysum, 1 + it + 1)
                    fenced(ACT.Gelu)
                    act.activation(yT[:, bass.ds(q, 1), :].rearrange("p o n -> p (o n)"), ysum[:, 1, :],
                                   ACT.Gelu).then_inc(s_yT, 1)
                    if more:
                        copy_v(q + 1)

                copy_u(0)
                copy_qk(0)
                angles(0, 0)
                copy_c(0)
                copy_v(0)
                with act.Fori(0, NQ - 1) as q:
                    mix_block(q, True)
                mix_block(NQ - 1, False)

                act.wait_ge(s_attn, 1 + NQ * (l + 1))
                for a in range(TT):
                    squares(attn[:, a, :], AW, 16 + 2 * a, probs_f[:, a * AW:(a + 1) * AW])
                for a in range(TT):
                    act.wait_ge(s_glu, l * TT + a + 1)
                    act.activation(ssm[:, a, :], ps[:, 2 * a + 1, :], ACT.Sigmoid).then_inc(s_sig, 1)
                    table_of(ACT.Sqrt)
                    act.drain()
                    act.wait_ge(s_ssm, l * TT + a + 1)
                    squares(ssm[:, a, :], AW, 17 + 2 * a, probs_f[:, a * AW:(a + 1) * AW])
                    act.drain()
                    act.activation(stat[:, 20 + 2 * a:22 + 2 * a], stat[:, 16 + 2 * a:18 + 2 * a], ACT.Sqrt,
                                   bias=eps_c, scale=1.0 / AW).then_inc(s_rms, 1)

                def high_u(c, s, pair):
                    act.wait_ge(s_u_ld[s], 16 * (l * (PK // 2) + pair + 1))
                    act.wait_ge(s_u_mm, 2 + l * PK + c - 1)
                    act.activation(u_hl[s][:, 0, :, :], u_raw[s][:, :, :], ACT.Copy).then_inc(s_u_hi, 1)

                high_u(0, 0, 0)
                high_u(1, 1, 0)
                table_of(ACT.Sqrt)
                for a in range(TT):
                    act.wait_ge(s_x1, TT * l + a + 1)
                    squares(xs[:, a, :], D, a, probs_f)
                    act.drain()
                    act.activation(stat[:, 2 + a:3 + a], stat[:, a:a + 1], ACT.Sqrt, bias=eps_c,
                                   scale=1.0 / D).then_inc(s_rms, 1)
                    act.wait_ge(s_hT, (2 * l + 1) * 4 + 2 * a + 2)
                    act.activation(h_hl[:, 0, :, a * P:(a + 1) * P], hT[:, :, a * P:(a + 1) * P], ACT.Copy)\
                        .then_inc(s_hhi, 1)

                def high_v(c, s, pair):
                    act.wait_ge(s_v_ld[s], 16 * (l * (PK // 2) + pair + 1))
                    act.wait_ge(s_v_mm, 2 + l * PK + c - 1)
                    act.activation(v_hl[s][:, 0, :], v_raw[s][:, :], ACT.Copy).then_inc(s_v_hi, 1)

                def gelu_early(c, s):
                    act.drain()
                    act.wait_ge(s_u_mm, 2 + l * PK + c + 1)
                    fenced(ACT.Gelu)
                    act.activation(gates[:, bass.ds(c, 1), :].rearrange("p o t -> p (o t)"), ps[:, 4 + s, 0:S],
                                   ACT.Gelu).then_inc(s_gelu, 1)

                def gelu(c, s):
                    n = l * PK + c
                    act.wait_ge(s_u_mm, 2 + n + 1)
                    act.wait_ge(s_wt, n - 1)
                    act.activation(act_w[:, s, :], ps[:, 4 + s, 0:S], ACT.Gelu).then_inc(s_gelu, 1)

                with act.Fori(0, PH // 2) as hp:
                    for s in range(2):
                        ih = l * PH + hp * 2 + s
                        if s == 0:
                            act.wait_ge(s_spill, 16 * (l + 1))
                        act.wait_ge(s_q, ih + 1)
                        act.activation(qh, ps[:, 6, 0:S], ACT.Copy).then_inc(s_qh, 1)
                        for j in range(2):
                            c = hp * 8 + s * 4 + j
                            high_u(c + 2, j, hp * 4 + s * 2 + 1)
                            gelu_early(c, j)
                        act.wait_ge(s_sc, 1 + ih + 1)
                        act.wait_ge(s_sc_used, 1 + ih)
                        act.activation(sc, ps[:, 0:2, 0:S].rearrange("p b (a n) -> p b a n", a=TT), ACT.Copy)\
                            .then_inc(s_sc_sb, 1)
                        for j in range(2):
                            c = hp * 8 + s * 4 + j + 2
                            high_u(c + 2, j, hp * 4 + s * 2 + 2)
                            gelu_early(c, j)
                for j in range(EARLY - WITH_HEADS):
                    c = WITH_HEADS + j
                    high_u(c + 2, j % 2, c // 2 + 1)
                    gelu_early(c, j % 2)
                act.wait_ge(s_topd, l + 1)
                act.activation(sel[:, 2, :, :, :], sel[:, 2, :, :, :], ACT.Exp).then_inc(s_gexp, 1)
                act.wait_ge(s_seltr, l + 1)
                act.activation(sel_T[:, 0:2, :], ps[:, 2, :].rearrange("p (k t) -> p k t", k=2), ACT.Copy)
                act.activation(sel_T[:, 2, :], ps[:, 3, 0:S], ACT.Copy).then_inc(s_selT, 1)
                with act.Fori(0, S // 16) as i:
                    for j in range(4):
                        act.drain()
                        act.wait_ge(s_gmul, (l * (S // 16) + i) * 4 + j + 1)
                        fenced()
                        act.activation(gates[:, EARLY:PK, bass.ds(i * 16 + j * 4, 4)],
                                       ps[:, j, :].rearrange("p (t c) -> p c t", c=PK)[:, EARLY:PK, :],
                                       ACT.Copy).then_inc(s_gates, 1)

                high_v(0, 0, 0)
                high_v(1, 1, 0)
                with act.Fori(0, EARLY // 2 - 1) as i:
                    for s in range(2):
                        high_v(i * 2 + s + 2, s, i + 1)
                high_v(EARLY, 0, EARLY // 2)
                with act.Fori(0, (PK - EARLY) // 2 - 1) as i:
                    for s in range(2):
                        c = i * 2 + s + EARLY
                        gelu(c, s)
                        high_u(c + 2, s, i + EARLY // 2 + 1)
                        high_v(c + 1, 1 - s, i + EARLY // 2 + s)
                gelu(PK - 2, 0)
                high_v(PK - 1, 1, PK // 2 - 1)
                gelu(PK - 1, 1)

            table_of(ACT.Sqrt)
            act.wait_ge(s_layer, 1 + DEPTH)
            for a in range(TT):
                if a:
                    act.drain()
                squares(xs[:, a, :], D, a, turn_f)
            act.drain()
            act.activation(stat[:, 2:4], stat[:, 0:2], ACT.Sqrt, bias=eps_c, scale=1.0 / D).then_inc(s_rms, 1)

        @block.vector
        def _(dve):
            dve.memset(rel_sb, 1.0).then_inc(s_relones, 1)
            dve.memset(fence[:, :], 0.0)
            dve.memset(eps_c, EPS)
            dve.memset(half_pi_c, HALF_PI).then_inc(s_memset, 1)
            dve.sem_inc(s_hot_free, 4)
            dve.sem_inc(s_gates, 4)
            for counter in (s_u_mm, s_v_mm, s_gelu, s_pp, s_drive, s_y):
                dve.sem_inc(counter, 2)
            dve.sem_inc(s_proj, 3)
            dve.sem_inc(s_state, 4)
            dve.sem_inc(s_bu, NT)
            for counter in (s_layer, s_c, s_c_tmp, s_qk_sb, s_v_sb, s_attn, s_pT, s_pv, s_outc, s_ysum, s_yT,
                            s_ptr, s_sc, s_sc_sb, s_sc_used):
                dve.sem_inc(counter, 1)

            def tt(o, a, b, op):
                return dve.tensor_tensor(o, a, b, op)

            with dve.Fori(0, DEPTH) as l:
                def normed(a, count):
                    dve.wait_ge(s_rms, count)
                    dve.reciprocal(stat[:, 4 + a:5 + a], stat[:, 2 + a:3 + a])
                    dve.drain()
                    dve.tensor_scalar(xn[:, a, :], xs[:, a, :], stat[:, 4 + a:5 + a], None, ALU.mult)\
                        .then_inc(s_xn, 1)

                def gained(dst, a, g, transposed, count, done):
                    for j in range(2):
                        dve.wait_ge(transposed, count + 2 * a + j + 1)
                        tt(dst[:, 4 * j:4 * j + 4, a * P:(a + 1) * P],
                           ps[:, 2 * a + j, :].rearrange("p (c t) -> p c t", c=4),
                           g[:, 4 * j:4 * j + 4].unsqueeze(2).broadcast_to([P, 4, P]), ALU.mult).then_inc(done, 1)

                for a in range(TT):
                    normed(a, 6 * l + a + 1)
                dve.wait_ge(s_gain, 16 * (l + 1))
                for a in range(TT):
                    gained(hT, a, g_mix, s_tr, 8 * l, s_hT)

                lr, li, step = par[:, 0, :], par[:, 1, :], sm[:, 0, :]
                theta, sig, mag, turns, whole, phi = (sm[:, i, :] for i in (1, 2, 3, 4, 5, 7))
                dve.wait_ge(s_p1, l + 1)
                tt(theta, li, step, ALU.mult)
                tt(sig, lr, step, ALU.mult)
                dve.drain()
                dve.tensor_scalar(turns, theta, INV_TWO_PI, None, ALU.mult)
                dve.drain()
                dve.tensor_scalar(whole, turns, ROUND, ROUND, ALU.add, ALU.subtract)
                dve.drain()
                dve.scalar_tensor_tensor(theta, whole, -TWO_PI_A, theta, ALU.mult, ALU.add)
                dve.drain()
                dve.scalar_tensor_tensor(theta, whole, -TWO_PI_B, theta, ALU.mult, ALU.add)
                dve.drain()
                dve.tensor_scalar(sm[:, 6, :], theta, INV_TWO_PI, None, ALU.mult)
                dve.drain()
                dve.tensor_scalar(sm[:, 6, :], sm[:, 6, :], 0.5, -0.5, ALU.min, ALU.max)
                dve.drain()
                dve.tensor_copy(phi, sm[:, 6, :]).then_inc(s_p2, 1)
                dve.tensor_scalar(sm[:, 11, :], sm[:, 6, :], GRID14, GRID14, ALU.add, ALU.subtract)
                dve.drain()
                dve.tensor_tensor(sm[:, 12, :], sm[:, 6, :], sm[:, 11, :], ALU.subtract)
                dve.drain()
                n_all = NQ * NT

                def wide(i):
                    return sm[:, i, :].unsqueeze(2).broadcast_to([P, n_all, 32])

                ab = over(steps_ab, n_all)
                tt(angle, wide(11), ab, ALU.mult)
                dve.drain()
                dve.tensor_scalar(angle_t, angle, ROUND, ROUND, ALU.add, ALU.subtract)
                dve.drain()
                tt(angle, angle, angle_t, ALU.subtract)
                dve.drain()
                tt(angle_t, wide(12), ab, ALU.mult)
                dve.drain()
                tt(angle, angle, angle_t, ALU.add)
                def block_turns(q, half, first=False):
                    it = l * NQ + q
                    tiles = slice(half * NT // 2, (half + 1) * NT // 2)
                    some = angle[:, bass.ds(q * NT + half * NT // 2, NT // 2), :]
                    shape = [P, NT // 2, 16, 16]
                    a_part = some[:, :, 0:16].unsqueeze(3).broadcast_to(shape)
                    b_part = some[:, :, 16:32].unsqueeze(2).broadcast_to(shape)
                    dve.drain()
                    dve.wait_ge(s_outc, 1 + it * NT - (0 if half or first else NT // 2))
                    tt(tab[:, 0, tiles, :].rearrange("p n (a b) -> p n a b", a=16), a_part, b_part, ALU.add)
                    dve.drain()
                    dve.tensor_scalar(tab[:, 1, tiles, :], tab[:, 0, tiles, :], ROUND, ROUND, ALU.add, ALU.subtract)
                    dve.drain()
                    tt(tab[:, 0, tiles, :], tab[:, 0, tiles, :], tab[:, 1, tiles, :], ALU.subtract)\
                        .then_inc(s_turns, 1)

                def two(j, n):
                    return over(tab[:, j, n % NT, :], 2)

                def turn_in(q, n):
                    s, it = n % 2, l * NQ + q
                    if n % 4 == 0:
                        dve.wait_ge(s_tab, 2 * it + n // 4 + 1)
                    dve.wait_ge(s_bu, NT + it * NT + n + 1)
                    dve.wait_ge(s_drive, it * NT + n + 1)
                    src = ps[:, 5 + s, :].rearrange("p (r t) -> p r t", r=2)
                    tt(turn[:, s, :, :], src, two(1, n), ALU.mult)
                    tt(turn2[:, s, :, :], src, two(0, n), ALU.mult).then_inc(s_pp, 1)

                def scan(q, n):
                    s, it = n % 2, l * NQ + q
                    dve.wait_ge(s_drive, 2 + it * NT + n + 1)
                    dve.wait_ge(s_y, it * NT + n + 1)
                    r_all = col(mag, q * NT + n).broadcast_to([P, S])
                    for r in range(2):
                        dve.tensor_tensor_scan(state[:, s, r, :], r_all, drive[:, s, r, :], 0.0,
                                               ALU.mult, ALU.add).then_inc(s_state, 1)
                    dve.wait_ge(s_state, 4 + 2 * (it * NT + n + 1))
                    tt(outs[:, s, :, :], state[:, s, :, :], two(0, n), ALU.mult).then_inc(s_outs, 1)

                def row_max(q, head):
                    dve.wait_ge(s_score, (l * NQ + q) * 2 + head + 1)
                    dve.tensor_reduce(stat[:, 8 + 2 * head:10 + 2 * head],
                                      ps[:, 2 + head, :].rearrange("p (a n) -> p a n", a=TT), AX.X, ALU.max,
                                      negate=True).then_inc(s_max, 1)

                def attn_out(q):
                    dve.wait_ge(s_pv, 1 + l * NQ + q + 1)
                    dve.reciprocal(stat[:, 24:28], stat[:, 12:16])
                    dve.drain()
                    for s in range(4):
                        m = dve.tensor_scalar(attn[:, s % 2, bass.ds((q * 2 + s // 2) * HD, HD)],
                                              ps[:, 2, s * HD:(s + 1) * HD], stat[:, 24 + s:25 + s], None,
                                              ALU.mult)
                    m.then_inc(s_attn, 1)

                def mix_block(q, more):
                    it = l * NQ + q
                    for n in range(1, NT + 1 if more else NT):
                        if n + 1 < NT or more:
                            turn_in(q, n + 1)
                        if n == 1:
                            block_turns(q, 1)
                        if n in (2, 3):
                            row_max(q, n - 2)
                        scan(q, n)
                        if n == 4 and more:
                            block_turns(q + 1, 0)
                        if n == 7:
                            attn_out(q)
                    dve.wait_ge(s_y, 2 + (it + 1) * NT)
                    dve.scalar_tensor_tensor(ysum[:, 0, :],
                                             u_all[:, bass.ds(q, 1), 0, :].rearrange("p o t -> p (o t)"),
                                             col(d_skip, q), ps[:, 7, 0:S], ALU.mult, ALU.add)
                    dve.drain()
                    dve.wait_ge(s_yT, 1 + it)
                    tt(ysum[:, 1, :], ysum[:, 0, :], ps[:, 7, S:2 * S][:, ::-1], ALU.add).then_inc(s_ysum, 1)

                dve.wait_ge(s_tr, 8 * l + 4)
                dve.memset(fence[:, 2:3], 0.0)
                block_turns(0, 0, first=True)
                dve.wait_ge(s_p3, l + 1)
                sin, cos = sm[:, 9, :], sm[:, 10, :]
                re, im, den, tmp = (sm[:, i, :] for i in (13, 14, 15, 16))
                f_re, f_im, nf_re, nf_im = (sm[:, i, :] for i in (17, 18, 19, 20))
                tt(re, mag, cos, ALU.mult)
                tt(im, mag, sin, ALU.mult)
                tt(den, lr, lr, ALU.mult)
                tt(tmp, li, li, ALU.mult)
                dve.drain()
                dve.tensor_scalar(re, re, -1.0, None, ALU.add)
                tt(den, den, tmp, ALU.add)
                dve.drain()
                dve.reciprocal(den, den)
                tt(f_re, re, lr, ALU.mult)
                tt(tmp, im, li, ALU.mult)
                dve.drain()
                tt(f_re, f_re, tmp, ALU.add)
                tt(f_im, im, lr, ALU.mult)
                dve.drain()
                tt(tmp, re, li, ALU.mult)
                dve.drain()
                tt(f_im, f_im, tmp, ALU.subtract)
                tt(f_re, f_re, den, ALU.mult)
                dve.drain()
                tt(f_im, f_im, den, ALU.mult)
                dve.tensor_scalar(nf_re, f_re, -1.0, None, ALU.mult)
                dve.drain()
                dve.tensor_scalar(nf_im, f_im, -1.0, None, ALU.mult).then_inc(s_coef, 1)

                turn_in(0, 0)
                turn_in(0, 1)
                scan(0, 0)
                with dve.Fori(0, NQ - 1) as q:
                    mix_block(q, True)
                mix_block(NQ - 1, False)

                def gated_mix(a):
                    dve.wait_ge(s_sig, l * TT + a + 1)
                    tt(ssm[:, a, :], ps[:, 2 * a, :], ssm[:, a, :], ALU.mult).then_inc(s_ssm, 1)
                    dve.wait_ge(s_rms, 6 * l + 2 + a + 1)
                    r = 20 + 2 * a
                    dve.reciprocal(stat[:, r:r + 2], stat[:, r:r + 2])
                    dve.drain()
                    dve.tensor_scalar(mixn[:, a, 0:AW], attn[:, a, :], stat[:, r:r + 1], None, ALU.mult)
                    dve.tensor_scalar(mixn[:, a, AW:D], ssm[:, a, :], stat[:, r + 1:r + 2], None, ALU.mult)\
                        .then_inc(s_mixn, 1)

                def add_x(a, half):
                    dve.wait_ge(s_wo, 4 * l + 2 * a + half + 1)
                    o = xs[:, a, half * 512:(half + 1) * 512]
                    m = tt(o, o, ps[:, 4 + 2 * a + half, :], ALU.add)
                    if half:
                        m.then_inc(s_x1, 1)

                def low_h(a):
                    dve.wait_ge(s_hhi, TT * l + a + 1)
                    cols = slice(a * P, (a + 1) * P)
                    tt(h_hl[:, 1, :, cols], hT[:, :, cols], h_hl[:, 0, :, cols].bitcast(F32), ALU.subtract)\
                        .then_inc(s_hlo, 1)

                gated_mix(0)
                gained(mixT, 0, g_cat, s_mixtr, 4 * l, s_mixT)
                gated_mix(1)
                add_x(0, 0)
                gained(mixT, 1, g_cat, s_mixtr, 4 * l, s_mixT)
                add_x(0, 1)
                normed(0, 6 * l + 5)
                add_x(1, 0)
                gained(hT, 0, g_ffn, s_tr, 8 * l + 4, s_hT)
                low_h(0)
                add_x(1, 1)
                normed(1, 6 * l + 6)
                gained(hT, 1, g_ffn, s_tr, 8 * l + 4, s_hT)
                low_h(1)

                def top16(src, spare, vals, idx):
                    for a, b, v, i in zip(src, spare, vals, idx):
                        dve.max(v[:, 0:8], a)
                    dve.drain()
                    for a, b, v, i in zip(src, spare, vals, idx):
                        dve.match_replace(b, v[:, 0:8], a, LOWEST)
                        dve.max_index(i[:, 0:8], v[:, 0:8], a)
                    dve.drain()
                    for a, b, v, i in zip(src, spare, vals, idx):
                        dve.max(v[:, 8:16], b)
                    dve.drain()
                    for a, b, v, i in zip(src, spare, vals, idx):
                        m = dve.max_index(i[:, 8:16], v[:, 8:16], b)
                    return m

                with dve.Fori(0, PH) as h:
                    ih = l * PH + h
                    dve.wait_ge(s_sc_sb, 1 + ih + 1)
                    dve.memset(fence[:, 2:3], 0.0)
                    pairs = [(b, a) for b in range(2) for a in range(TT)]
                    top16([sc[:, b, a, :] for b, a in pairs], [sc2[:, b, a, :] for b, a in pairs],
                          [t16[:, b, a, :] for b, a in pairs], [i16u[:, b, a, :] for b, a in pairs])\
                        .then_inc(s_sc_used, 1)
                    dve.drain()
                    dve.tensor_copy(i16, i16u)
                    tt(cand, t16[:, 0, :, :].unsqueeze(3).broadcast_to([P, TT, 16, 16]),
                       t16[:, 1, :, :].unsqueeze(2).broadcast_to([P, TT, 16, 16]), ALU.add)
                    dve.drain()
                    cf = [cand[:, a, :, :].rearrange("p i j -> p (i j)") for a in range(TT)]
                    top16(cf, [cand2[:, a, :] for a in range(TT)], [top[:, a, :] for a in range(TT)],
                          [cu[:, a, :] for a in range(TT)])
                    dve.drain()
                    dve.tensor_scalar(rank_u[:, 0, :, :], cu, 4, None, ALU.logical_shift_right)
                    dve.tensor_scalar(rank_u[:, 1, :, :], cu, 15, None, ALU.bitwise_and)
                    tt(sel[:, 2, :, bass.ds(h, 1), :].rearrange("p a o j -> p a (o j)"), top,
                       top[:, :, 0:1].broadcast_to([P, TT, TOPK]), ALU.subtract)
                    dve.drain()
                    dve.tensor_copy(rank, rank_u)
                    dve.drain()
                    for b in range(2):
                        for a in range(TT):
                            tt(pick[:, b, a, :, :], rank[:, b, a, :].unsqueeze(2).broadcast_to([P, 16, 16]),
                               over(iota16, 16), ALU.is_equal)
                    dve.drain()
                    for b in range(2):
                        for a in range(TT):
                            tt(pick[:, b, a, :, :], pick[:, b, a, :, :], over(i16[:, b, a, :], 16), ALU.mult)
                    dve.drain()
                    for b in range(2):
                        dve.tensor_reduce(sel[:, b, :, bass.ds(h, 1), :].rearrange("p a o j -> p a (o j)"),
                                          pick[:, b, :, :, :], AX.X, ALU.add)
                    dve.drain()
                dve.memset(fence[:, 2:3], 0.0).then_inc(s_topd, 1)
                dve.wait_ge(s_gexp, l + 1)
                dve.tensor_reduce(gsum, sel[:, 2, :, :, :], AX.X, ALU.add)
                dve.drain()
                dve.reciprocal(gsum, gsum)
                dve.drain()
                tt(sel[:, 2, :, :, :], sel[:, 2, :, :, :], gsum.unsqueeze(3).broadcast_to([P, TT, PH, TOPK]),
                   ALU.mult).then_inc(s_sel, 1)

                def hot_rows(i, b):
                    n = (l * (S // 16) + i) * BATCHES + b
                    for j, (rows, done) in enumerate(((hot1, s_hot1), (hot2, s_hot2))):
                        dve.wait_ge(s_hot_free, n + 1)
                        tt(rows[b], over(iota, HOT),
                           sel_T[:, j, bass.ds(i * 16 + b * HOT, HOT)].unsqueeze(2).broadcast_to([P, HOT, PK]),
                           ALU.is_equal).then_inc(done, 1)

                def gate_early(i, b):
                    dve.wait_ge(s_hot_free, BATCHES + (l * (S // 16) + i) * BATCHES + b + 1)
                    place = gates[:, 0:EARLY, bass.ds(i * 16 + b * HOT, HOT)]
                    tt(place, place, ps[:, b, :].rearrange("p (t c) -> p c t", c=PK)[:, 0:EARLY, :],
                       ALU.mult).then_inc(s_gmul, 1)

                dve.wait_ge(s_selT, l + 1)
                dve.memset(fence[:, 2:3], 0.0)
                dve.wait_ge(s_u_lo, l * PK + EARLY + 2)
                dve.wait_ge(s_gelu, 2 + l * PK + EARLY)
                hot_rows(0, 0)
                hot_rows(0, 1)
                with dve.Fori(0, S // 16 - 1) as i:
                    for b in range(BATCHES):
                        hot_rows(i + (b + 2) // BATCHES, (b + 2) % BATCHES)
                        gate_early(i, b)
                for b in range(BATCHES):
                    if b < 2:
                        hot_rows(S // 16 - 1, b + 2)
                    gate_early(S // 16 - 1, b)

                def low_v(c, s):
                    dve.wait_ge(s_v_hi, l * PK + c + 1)
                    tt(v_hl[s][:, 1, :], v_raw[s][:, :], v_hl[s][:, 0, :].bitcast(F32), ALU.subtract)\
                        .then_inc(s_v_lo, 1)

                def weights_early(c, s):
                    dve.wait_ge(s_v_mm, 2 + l * PK + c - 1)
                    g = gates[:, bass.ds(c, 1), :].rearrange("p o t -> p (o t)")
                    dve.tensor_scalar(w_hl[s][:, 0, :], g, 1.0, None, ALU.mult)
                    dve.drain()
                    tt(w_hl[s][:, 1, :], g, w_hl[s][:, 0, :].bitcast(F32), ALU.subtract).then_inc(s_wt, 1)

                def weights(c, s):
                    n = l * PK + c
                    dve.wait_ge(s_gelu, 2 + n + 1)
                    dve.wait_ge(s_v_mm, 2 + n - 1)
                    g = gates[:, bass.ds(c, 1), :].rearrange("p o t -> p (o t)")
                    tt(w_hl[s][:, 0, :], act_w[:, s, :], g, ALU.mult)
                    tt(act_w[:, s, :], act_w[:, s, :], g, ALU.mult)
                    dve.drain()
                    tt(w_hl[s][:, 1, :], act_w[:, s, :], w_hl[s][:, 0, :].bitcast(F32), ALU.subtract)\
                        .then_inc(s_wt, 1)

                dve.drain()
                with dve.Fori(0, EARLY // 2) as i:
                    for s in range(2):
                        weights_early(i * 2 + s, s)
                        low_v(i * 2 + s, s)
                low_v(EARLY, 0)
                with dve.Fori(0, (PK - EARLY) // 2 - 1) as i:
                    dve.wait_ge(s_gates, 4 + (l + 1) * (S // 4))
                    for s in range(2):
                        c = i * 2 + s + EARLY
                        weights(c, s)
                        low_v(c + 1, 1 - s)
                weights(PK - 2, 0)
                low_v(PK - 1, 1)
                weights(PK - 1, 1)
                dve.wait_ge(s_v_mm, 2 + (l + 1) * PK)
                dve.wait_ge(s_xback, 16 * (l + 1))
                for a in range(TT):
                    for half in range(2):
                        o = xs[:, a, half * 512:(half + 1) * 512]
                        m = tt(o, o, ps[:, 2 * a + half, :], ALU.add)
                m.then_inc(s_layer, 1)

            dve.wait_ge(s_rms, 6 * DEPTH + 1)
            dve.reciprocal(stat[:, 4:6], stat[:, 2:4])
            dve.wait_ge(s_gfin, 16)
            dve.drain()
            for a in range(TT):
                m = dve.scalar_tensor_tensor(xn[:, a, :], xs[:, a, :], stat[:, 4 + a:5 + a], gfin,
                                             ALU.mult, ALU.mult)
            m.then_inc(s_fin, 1)

        @block.gpsimd
        def _(pool):
            def tt(o, a, b, op):
                return pool.tensor_tensor(o, a, b, op)

            def low_u(l, c, s):
                pool.wait_ge(s_u_hi, l * PK + c + 1)
                tt(u_hl[s][:, 1, :, :], u_raw[s][:, :, :], u_hl[s][:, 0, :, :].bitcast(F32), ALU.subtract)\
                    .then_inc(s_u_lo, 1)

            with pool.Fori(0, DEPTH) as l:
                def c_terms(q):
                    it = l * NQ + q

                    def f(i):
                        return sm[:, i, bass.ds(q * NT, NT)].unsqueeze(2).broadcast_to([P, NT, 32])

                    cre, cim = c_raw[:, :, 0, :], c_raw[:, :, 1, :]
                    pool.drain()
                    pool.wait_ge(s_coef, l + 1)
                    pool.wait_ge(s_c_ld, 16 * (it + 1))
                    pool.wait_ge(s_c, 1 + it)
                    tt(fence[:, 3:4], fence[:, 4:5], fence[:, 4:5], ALU.add)
                    tt(c_tmp[:, 0, :, :], cre, f(17), ALU.mult)
                    tt(c_tmp[:, 1, :, :], cim, f(18), ALU.mult)
                    tt(c_tmp[:, 2, :, :], cre, f(20), ALU.mult)
                    tt(c_tmp[:, 3, :, :], cim, f(19), ALU.mult)
                    pool.drain()
                    tt(c_tmp[:, 0, :, :], c_tmp[:, 0, :, :], c_tmp[:, 1, :, :], ALU.subtract)
                    tt(c_tmp[:, 2, :, :], c_tmp[:, 2, :, :], c_tmp[:, 3, :, :], ALU.add).then_inc(s_c_tmp, 1)

                def drives(q, n):
                    s, it = n % 2, l * NQ + q
                    pool.wait_ge(s_pp, 2 + it * NT + n + 1)
                    pool.wait_ge(s_state, 2 * (it * NT + n) + 2)
                    tt(drive[:, s, 0, :], turn[:, s, 0, :], turn2[:, s, 1, :], ALU.add)
                    tt(drive[:, s, 1, :], turn[:, s, 1, :], turn2[:, s, 0, :], ALU.subtract).then_inc(s_drive, 1)

                def turn_out(q, n):
                    it = l * NQ + q
                    pool.wait_ge(s_state, 4 + 2 * (it * NT + n + 1))
                    pool.wait_ge(s_y, it * NT + n + 1)
                    tt(outc[:, n % 2, :, :], state[:, n % 2, :, :], over(tab[:, 1, n % NT, :], 2), ALU.mult)\
                        .then_inc(s_outc, 1)

                def mix_block(q, more):
                    for n in range(1, NT + 1 if more else NT):
                        if n + 1 < NT or more:
                            drives(q, n + 1)
                        turn_out(q, n)
                        if n == 5 and more:
                            c_terms(q + 1)

                c_terms(0)
                drives(0, 0)
                drives(0, 1)
                turn_out(0, 0)
                with pool.Fori(0, NQ - 1) as q:
                    mix_block(q, True)
                mix_block(NQ - 1, False)

                with pool.Fori(0, EARLY // 2 + 1) as i:
                    for s in range(2):
                        low_u(l, i * 2 + s, s)
                with pool.Fori(0, S // 16) as i:
                    for b in range(BATCHES):
                        pool.drain()
                        pool.wait_ge(s_hot1, (l * (S // 16) + i) * BATCHES + b + 1)
                        tt(fence[:, 3:4], fence[:, 4:5], fence[:, 4:5], ALU.add)
                        tt(hot1[b], hot1[b], sel_T[:, 2, bass.ds(i * 16 + b * HOT, HOT)].unsqueeze(2)
                           .broadcast_to([P, HOT, PK]), ALU.mult).then_inc(s_gated, 1)
                with pool.Fori(0, (PK - EARLY) // 2 - 1) as i:
                    for s in range(2):
                        low_u(l, i * 2 + s + EARLY + 2, s)


def kernel(x, w_in, w_out, rel_bias, g_attn, g_ssm, norm_mix, norm_ffn, lam_re, lam_im, log_step,
           b_re, b_im, c_re, c_im, d_skip, w_glu, w_query, sub_keys, expert_u, expert_v, norm_final):
    import numpy as np
    import concourse.bacc as bacc
    from concourse.bass_utils import run_bass_kernel_spmd

    f32 = np.float32
    L = DEPTH

    def lay(a, shape, perm, to):
        return np.ascontiguousarray(np.asarray(a).reshape(shape).transpose(perm).reshape(to))

    def columns(a, n):
        return np.asarray(a).reshape(L, n, P).transpose(0, 2, 1)

    a_w_in = lay(w_in, (L, DC, P, 4, NQ, P), (0, 4, 2, 3, 1, 5), (L * NQ, P, DC * 512))
    a_w_out = lay(w_out, (L, DC, P, D), (0, 2, 1, 3), (L, P, DC * D))
    a_w_glu = lay(w_glu, (L, 4, P, D), (0, 2, 1, 3), (L, P, 4 * D))
    a_w_query = lay(w_query, (L, DC, P, PH, P), (0, 3, 2, 1, 4), (L * PH, P, DC * P))
    a_keys = lay(sub_keys, (L, 2, PH, PK, 64), (0, 2, 1, 4, 3), (L * PH, P, PK))
    a_u = lay(expert_u, (L, PK, PK, DC, P), (0, 1, 4, 3, 2), (L * PK, P, DC * P))
    a_v = lay(expert_v, (L, PK, PK, D), (0, 1, 2, 3), (L * PK, PK, D))
    a_gain = np.ascontiguousarray(np.concatenate(
        [columns(norm_mix, 8), columns(norm_ffn, 8), columns(g_attn, 4), columns(g_ssm, 4),
         columns(d_skip, 4)], axis=2))
    def per_state(a):
        return np.asarray(a).reshape(L, 2, NQ, 4, 2, 64).transpose(0, 4, 5, 2, 3, 1).reshape(L, P, 32)
    steps = np.broadcast_to(np.asarray(log_step)[..., None], (L, 2, 32, 64))
    a_par = np.ascontiguousarray(np.stack([per_state(lam_re), per_state(lam_im), per_state(steps)], axis=2))
    a_b = np.zeros((L, NQ, 4, 2, 16, 4, 2, 2, 2, 64), f32)
    a_c = np.zeros((L, NQ, 2, 64, 4, 2, 2, 2, 16), f32)
    for r, (b, c) in enumerate(((b_re, c_re), (b_im, c_im))):
        b = np.asarray(b).reshape(L, 2, NQ, 4, 2, 64, 16)
        c = np.asarray(c).reshape(L, 2, NQ, 4, 2, 16, 64)
        for k in range(4):
            for g in range(2):
                a_b[:, :, k, g, :, k, :, r, g, :] = b[:, :, :, k, g].transpose(0, 2, 4, 1, 3)
                a_c[:, :, g, :, k, :, r, g, :] = c[:, :, :, k, g].transpose(0, 2, 4, 1, 3)
    a_b = a_b.reshape(L * NQ, P, NT * 2 * P)
    a_c = a_c.reshape(L * NQ, P, NT * 2 * 32)

    a_const = np.zeros((P, NCONST), f32)
    a_const[:, 0:P] = np.eye(P)
    a_const[:, P:2 * P] = np.eye(P)[::-1]
    a_const[:, 2 * P:3 * P] = np.arange(P)
    a_const[:, 3 * P:3 * P + 16] = 16 * np.arange(16)
    a_const[:, 3 * P + 16:] = np.arange(16)
    delta = np.arange(TOEP) - (S - 1)
    n = np.abs(delta)
    large = 8 + (np.log(np.maximum(n, 1) / 8) / np.log(1024 / 8) * 8).astype(np.int32)
    bucket = np.where(delta > 0, 16, 0) + np.where(n < 8, n, np.minimum(large, 15))
    count = sum(((n % dil == 0) & (n <= win // 2)).astype(np.int64)
                for win, dil in ((128, 1), (512, 4), (2048, 16)))
    a_rows = np.zeros((33, TOEP), f32)
    a_rows[bucket, np.arange(TOEP)] = 1.0
    a_rows[32] = np.where(count > 0, np.log(np.maximum(count, 1)), -1e30)

    ins = {
        "x_in": np.ascontiguousarray(np.asarray(x).reshape(S, D)), "w_in": a_w_in, "w_out": a_w_out,
        "w_glu": a_w_glu, "w_query": a_w_query, "keys": a_keys, "expert_u": a_u, "expert_v": a_v,
        "rel_bias": np.ascontiguousarray(rel_bias), "gains": a_gain,
        "norm_final": np.ascontiguousarray(norm_final), "ssm_par": a_par, "ssm_b": a_b, "ssm_c": a_c,
        "consts": a_const, "bucket_rows": a_rows,
    }
    nc = bacc.Bacc("TRN2", target_bir_lowering=False, num_devices=1)
    args = [nc.dram_tensor(f"in_{k}", a.shape, mybir.dt.from_np(a.dtype), kind="ExternalInput").ap()
            for k, a in ins.items()]
    args.append(nc.dram_tensor("out_x", (S, D), F32, kind="ExternalOutput").ap())
    encoder(nc, *args)
    r = run_bass_kernel_spmd(nc, [{f"in_{k}": a for k, a in ins.items()}], core_ids=[0])
    return r.results[0]["out_x"].reshape(1, S, D)
```
